# Optimizing a Trainium2 kernel written in Bass

```python
import jax, jax.numpy as jnp
from jax import lax
import numpy as np

D_MODEL = 1024
BATCH = 1
SEQ = 128
DEPTH = 2
DEC_BATCH = 1
DEC_SEQ = 512
PAST_LEN = 128

GRID_W = 64
N_EVEN = (DEPTH + 1) // 2
N_ODD = DEPTH // 2
EPS = 1e-6
H_MLA = 8
Q_RANK = 256
KV_RANK = 128
MLA_NOPE = 64
ROPE_DIM = 32
MLA_QK = MLA_NOPE + ROPE_DIM
MLA_V = 64
ROPE_BASE = 10000.0
Q_BLOCK = 128
H_RET = 4
RET_DK = 64
RET_DV = 128
RET_CHUNK = 128
EVEN_IN = Q_RANK + KV_RANK + ROPE_DIM + 2 * H_RET * RET_DK + 2 * H_RET * RET_DV
EVEN_MIX = H_MLA * MLA_V + H_RET * RET_DV
CONV_DIM = 1024
CONV_W = 31
N_GROUPS = 4
EXP_PER_GROUP = 8
N_EXPERTS = N_GROUPS * EXP_PER_GROUP
TOP_K = 2
D_EXPERT = 256
EXPERT_BLOCK = 128

kernel_name = 'hybrid_mla_retention_conformer_hmoe_dit_step'

def rms_norm(x, g):
    xf = x.astype(jnp.float32)
    y = xf * lax.rsqrt(jnp.mean(xf * xf, axis=-1, keepdims=True) + EPS)
    return (y * g.astype(jnp.float32)).astype(x.dtype)

def layer_norm(x, g, b):
    xf = x.astype(jnp.float32)
    mu = jnp.mean(xf, axis=-1, keepdims=True)
    var = jnp.mean(jnp.square(xf - mu), axis=-1, keepdims=True)
    y = (xf - mu) * lax.rsqrt(var + EPS)
    return (y * g.astype(jnp.float32) + b.astype(jnp.float32)).astype(x.dtype)

def modulation(cond, w, b):
    m = jax.nn.silu(cond) @ w + b
    return jnp.split(m[:, None, :], 6, axis=-1)

def modulate(h, shift, scale):
    return h * (1.0 + scale) + shift

def axial_rope(L):
    rows = L // GRID_W
    r = jnp.repeat(jnp.arange(rows, dtype=jnp.float32), GRID_W)
    col = jnp.tile(jnp.arange(GRID_W, dtype=jnp.float32), rows)
    n_f = ROPE_DIM // 4
    freqs = ROPE_BASE ** (-jnp.arange(n_f, dtype=jnp.float32) / n_f)
    ang = jnp.concatenate([r[:, None] * freqs, col[:, None] * freqs], axis=-1)
    return jnp.cos(ang), jnp.sin(ang)

def apply_rope(x, rope):
    cos, sin = rope
    half = ROPE_DIM // 2
    c = cos[None, :, None, :].astype(x.dtype)
    s = sin[None, :, None, :].astype(x.dtype)
    x1, x2 = x[..., :half], x[..., half:]
    return jnp.concatenate([x1 * c - x2 * s, x1 * s + x2 * c], axis=-1)

def split_even(z):
    sizes = (Q_RANK, KV_RANK, ROPE_DIM, H_RET * RET_DK, H_RET * RET_DK, H_RET * RET_DV, H_RET * RET_DV)
    idx, acc = [], 0
    for s in sizes[:-1]:
        acc += s
        idx.append(acc)
    return jnp.split(z, idx, axis=-1)

def mla_queries(cq, q_a_norm, w_q_up, q_norm, rope):
    B, L = cq.shape[:2]
    q = (rms_norm(cq, q_a_norm) @ w_q_up).reshape(B, L, H_MLA, MLA_QK)
    q = rms_norm(q, q_norm)
    if rope is not None:
        q = jnp.concatenate([q[..., :MLA_NOPE], apply_rope(q[..., MLA_NOPE:], rope)], axis=-1)
    return q

def mla_keys(ckv, k_rope, w_kv_up, k_norm, rope):
    B, L = ckv.shape[:2]
    kv = (ckv @ w_kv_up).reshape(B, L, H_MLA, MLA_NOPE + MLA_V)
    k_nope, v = kv[..., :MLA_NOPE], kv[..., MLA_NOPE:]
    k_pe = jnp.broadcast_to(k_rope[:, :, None, :], (B, L, H_MLA, ROPE_DIM)).astype(k_nope.dtype)
    k = rms_norm(jnp.concatenate([k_nope, k_pe], axis=-1), k_norm)
    if rope is not None:
        k = jnp.concatenate([k[..., :MLA_NOPE], apply_rope(k[..., MLA_NOPE:], rope)], axis=-1)
    return k, v

def block_attention(q, k, v):
    B, Lq, H, dq = q.shape
    nb = Lq // Q_BLOCK
    qb = q.reshape(B, nb, Q_BLOCK, H, dq).transpose(1, 0, 2, 3, 4)
    scale = dq ** -0.5

    def one(qblk):
        s = jnp.einsum('bqhd,bkhd->bhqk', qblk, k, preferred_element_type=jnp.float32) * scale
        p = jax.nn.softmax(s, axis=-1).astype(v.dtype)
        return jnp.einsum('bhqk,bkhd->bqhd', p, v)

    o = lax.map(one, qb)
    return o.transpose(1, 0, 2, 3, 4).reshape(B, Lq, H, v.shape[-1])

def retention_chunkwise(q, k, v, log_g, s0):
    B, L, H, DK = q.shape
    DV = v.shape[-1]
    C = RET_CHUNK
    nc = L // C
    qc = q.reshape(B, nc, C, H, DK)
    kc = k.reshape(B, nc, C, H, DK)
    vc = v.reshape(B, nc, C, H, DV)
    pos = jnp.arange(C, dtype=jnp.float32)
    diff = pos[:, None] - pos[None, :]
    causal = diff >= 0
    dmask = jnp.where(causal[..., None], jnp.exp(jnp.where(causal, diff, 0.0)[..., None] * log_g), 0.0)
    scores = jnp.einsum('bnqhd,bnkhd->bnhqk', qc, kc) * dmask.transpose(2, 0, 1)
    inner = jnp.einsum('bnhqk,bnkhe->bnqhe', scores, vc)
    w_k = jnp.exp((C - 1 - pos)[:, None] * log_g)
    u = jnp.einsum('bnkhd,kh,bnkhe->bnhde', kc, w_k, vc)
    chunk_decay = jnp.exp(C * log_g)[None, :, None, None]

    def step(s, u_j):
        return chunk_decay * s + u_j, s

    s_final, s_prev = lax.scan(step, s0.astype(jnp.float32), jnp.moveaxis(u, 1, 0))
    xi = jnp.exp((pos + 1.0)[:, None] * log_g)
    cross = jnp.einsum('bnqhd,qh,nbhde->bnqhe', qc, xi, s_prev)
    return (inner + cross).reshape(B, L, H, DV), s_final

def retention_bidir(rq, rk, rv, decay_logit, s0):
    B, L = rq.shape[:2]
    q = rq.reshape(B, L, H_RET, RET_DK).astype(jnp.float32)
    k = rk.reshape(B, L, H_RET, RET_DK).astype(jnp.float32) * (RET_DK ** -0.5)
    v = rv.reshape(B, L, H_RET, RET_DV).astype(jnp.float32)
    log_g = jax.nn.log_sigmoid(decay_logit.astype(jnp.float32))
    o_f, s_f = retention_chunkwise(q, k, v, log_g[0], s0[:, 0])
    o_b, s_b = retention_chunkwise(q[:, ::-1], k[:, ::-1], v[:, ::-1], log_g[1], s0[:, 1])
    return o_f + o_b[:, ::-1], jnp.stack([s_f, s_b], axis=1)

def retention_out(o, gn_gain, gate):
    B, L = o.shape[:2]
    mu = jnp.mean(o, axis=-1, keepdims=True)
    var = jnp.mean(jnp.square(o - mu), axis=-1, keepdims=True)
    o = ((o - mu) * lax.rsqrt(var + EPS)).reshape(B, L, H_RET * RET_DV) * gn_gain.astype(jnp.float32)
    return jax.nn.silu(gate) * o.astype(gate.dtype)

def even_outputs(q, k, v, rq, rk, rv, rg, decay_logit, s0, gn_gain, w_out):
    B, L = q.shape[:2]
    o_mla = block_attention(q, k, v).reshape(B, L, H_MLA * MLA_V)
    o_ret, s_fin = retention_bidir(rq, rk, rv, decay_logit, s0)
    o_ret = retention_out(o_ret, gn_gain, rg)
    y = jnp.concatenate([o_mla, o_ret.astype(o_mla.dtype)], axis=-1) @ w_out
    return y, s_fin

def even_mixer_context(h, w_in, q_a_norm, w_q_up, kv_a_norm, w_kv_up, q_norm, k_norm, decay_logit, gn_gain, w_out):
    cq, ckv, kr, rq, rk, rv, rg = split_even(h @ w_in)
    ckv = rms_norm(ckv, kv_a_norm)
    q = mla_queries(cq, q_a_norm, w_q_up, q_norm, None)
    k, v = mla_keys(ckv, kr, w_kv_up, k_norm, None)
    s0 = jnp.zeros((h.shape[0], 2, H_RET, RET_DK, RET_DV), jnp.float32)
    y, s_fin = even_outputs(q, k, v, rq, rk, rv, rg, decay_logit, s0, gn_gain, w_out)
    return y, ckv, kr, s_fin

def even_mixer_latent(h, cache_ckv, cache_kr, state, w_in, q_a_norm, w_q_up, kv_a_norm, w_kv_up, q_norm, k_norm, decay_logit, gn_gain, w_out):
    L = h.shape[1]
    rope = axial_rope(L)
    cq, ckv, kr, rq, rk, rv, rg = split_even(h @ w_in)
    ckv = rms_norm(ckv, kv_a_norm)
    q = mla_queries(cq, q_a_norm, w_q_up, q_norm, rope)
    k_lat, v_lat = mla_keys(ckv, kr, w_kv_up, k_norm, rope)
    k_ctx, v_ctx = mla_keys(cache_ckv, cache_kr, w_kv_up, k_norm, None)
    k = jnp.concatenate([k_ctx.astype(k_lat.dtype), k_lat], axis=1)
    v = jnp.concatenate([v_ctx.astype(v_lat.dtype), v_lat], axis=1)
    y, _ = even_outputs(q, k, v, rq, rk, rv, rg, decay_logit, state, gn_gain, w_out)
    return y

def depthwise_conv(u, w, b):
    out = lax.conv_general_dilated(u, w[:, None, :].astype(u.dtype), window_strides=(1,),
                                   padding=[(CONV_W // 2, CONV_W // 2)],
                                   dimension_numbers=('NWC', 'WIO', 'NWC'),
                                   feature_group_count=u.shape[-1])
    return out + b

def conformer_conv(h, w_in, dw, dw_b, ln_g, ln_b, w_out):
    a, g = jnp.split(h @ w_in, 2, axis=-1)
    u = a * jax.nn.sigmoid(g)
    u = depthwise_conv(u, dw, dw_b)
    u = layer_norm(u, ln_g, ln_b)
    return jax.nn.silu(u) @ w_out

def grouped_expert_mlp(xf, eid, top_w, w_up, w_down):
    N, D = xf.shape
    M = N * TOP_K
    e_flat = eid.reshape(M)
    tok = (jnp.arange(M, dtype=jnp.int32) // TOP_K).astype(jnp.int32)
    order = jnp.argsort(e_flat)
    e_sorted = e_flat[order]
    counts = jnp.bincount(e_flat, length=N_EXPERTS).astype(jnp.int32)
    padded = (counts + EXPERT_BLOCK - 1) // EXPERT_BLOCK * EXPERT_BLOCK
    pad_end = jnp.cumsum(padded)
    pad_start = pad_end - padded
    start = jnp.cumsum(counts) - counts
    dest_sorted = (pad_start[e_sorted] + (jnp.arange(M, dtype=jnp.int32) - start[e_sorted])).astype(jnp.int32)
    n_blocks = -(-M // EXPERT_BLOCK) + N_EXPERTS
    P = n_blocks * EXPERT_BLOCK
    buf_tok = jnp.full((P,), N, jnp.int32).at[dest_sorted].set(tok[order])
    x_pad = jnp.concatenate([xf, jnp.zeros((1, D), xf.dtype)], axis=0)
    x_buf = x_pad[buf_tok].reshape(n_blocks, EXPERT_BLOCK, D)
    blk_start = jnp.arange(n_blocks, dtype=jnp.int32) * EXPERT_BLOCK
    blk_exp = jnp.minimum(jnp.searchsorted(pad_end, blk_start, side='right'), N_EXPERTS - 1)

    def run(args):
        xb, e = args
        a, b = jnp.split(xb @ w_up[e], 2, axis=-1)
        return (jax.nn.silu(a) * b) @ w_down[e]

    out_buf = lax.map(run, (x_buf, blk_exp)).reshape(P, D)
    dest = jnp.zeros((M,), jnp.int32).at[order].set(dest_sorted)
    y = out_buf[dest].reshape(N, TOP_K, D) * top_w[..., None].astype(xf.dtype)
    return jnp.sum(y, axis=1)

def hier_moe(h, w_group, b_group, w_expert, b_expert, w_up, w_down):
    B, L, D = h.shape
    N = B * L
    xf = h.reshape(N, D)
    rows = jnp.arange(N)
    p_group = jax.nn.softmax((xf @ w_group).astype(jnp.float32) + b_group.astype(jnp.float32), axis=-1)
    g_idx = jnp.argmax(p_group, axis=-1)
    g_w = p_group[rows, g_idx]
    e_logits = ((xf @ w_expert).astype(jnp.float32) + b_expert.astype(jnp.float32)).reshape(N, N_GROUPS, EXP_PER_GROUP)[rows, g_idx]
    p_exp = jax.nn.softmax(e_logits, axis=-1)
    top_w, top_i = lax.top_k(p_exp, TOP_K)
    top_w = top_w / jnp.sum(top_w, axis=-1, keepdims=True) * g_w[:, None]
    eid = (g_idx[:, None] * EXP_PER_GROUP + top_i).astype(jnp.int32)
    return grouped_expert_mlp(xf, eid, top_w, w_up, w_down).reshape(B, L, D)

def setup_inputs(seed: int = 0) -> dict:
    key = jax.random.key(seed)
    ks = iter(jax.random.split(key, 48))

    def nrm(shape, scale=1.0):
        return jax.random.normal(next(ks), shape, jnp.float32) * scale

    def gain(shape):
        return 1.0 + nrm(shape, 0.02)

    a = 5.0 + jnp.arange(H_RET, dtype=jnp.float32)
    decay = jnp.log(2.0 ** a - 1.0)[None, None, :] + nrm((N_EVEN, 2, H_RET), 0.01)
    return {
        'x_prompt': nrm((BATCH, SEQ, D_MODEL)),
        'x_sample': nrm((DEC_BATCH, DEC_SEQ, D_MODEL)),
        'cache_mla_ckv': nrm((DEC_BATCH, N_EVEN, PAST_LEN, KV_RANK)),
        'cache_mla_krope': nrm((DEC_BATCH, N_EVEN, PAST_LEN, ROPE_DIM), 0.5),
        'state_retention': nrm((DEC_BATCH, N_EVEN, 2, H_RET, RET_DK, RET_DV), 0.5),
        'c': nrm((DEC_BATCH, D_MODEL)),
        'c_ctx': nrm((D_MODEL,)),
        'ada_w': nrm((DEPTH, D_MODEL, 6 * D_MODEL), 0.5 * D_MODEL ** -0.5),
        'ada_b': nrm((DEPTH, 6 * D_MODEL), 0.02),
        'norm_mix': gain((DEPTH, D_MODEL)),
        'norm_ffn': gain((DEPTH, D_MODEL)),
        'ev_w_in': nrm((N_EVEN, D_MODEL, EVEN_IN), D_MODEL ** -0.5),
        'ev_q_a_norm': gain((N_EVEN, Q_RANK)),
        'ev_w_q_up': nrm((N_EVEN, Q_RANK, H_MLA * MLA_QK), Q_RANK ** -0.5),
        'ev_kv_a_norm': gain((N_EVEN, KV_RANK)),
        'ev_w_kv_up': nrm((N_EVEN, KV_RANK, H_MLA * (MLA_NOPE + MLA_V)), KV_RANK ** -0.5),
        'ev_q_norm': gain((N_EVEN, MLA_QK)),
        'ev_k_norm': gain((N_EVEN, MLA_QK)),
        'ev_ret_decay': decay,
        'ev_ret_gn': gain((N_EVEN, H_RET * RET_DV)),
        'ev_w_out': nrm((N_EVEN, EVEN_MIX, D_MODEL), EVEN_MIX ** -0.5),
        'od_w_in': nrm((N_ODD, D_MODEL, 2 * CONV_DIM), D_MODEL ** -0.5),
        'od_dw': nrm((N_ODD, CONV_W, CONV_DIM), CONV_W ** -0.5),
        'od_dw_b': nrm((N_ODD, CONV_DIM), 0.02),
        'od_ln_g': gain((N_ODD, CONV_DIM)),
        'od_ln_b': nrm((N_ODD, CONV_DIM), 0.02),
        'od_w_out': nrm((N_ODD, CONV_DIM, D_MODEL), CONV_DIM ** -0.5),
        'moe_w_group': nrm((DEPTH, D_MODEL, N_GROUPS), D_MODEL ** -0.5),
        'moe_b_group': nrm((DEPTH, N_GROUPS), 0.01),
        'moe_w_expert': nrm((DEPTH, D_MODEL, N_EXPERTS), D_MODEL ** -0.5),
        'moe_b_expert': nrm((DEPTH, N_EXPERTS), 0.01),
        'moe_w_up': nrm((DEPTH, N_EXPERTS, D_MODEL, 2 * D_EXPERT), D_MODEL ** -0.5),
        'moe_w_down': nrm((DEPTH, N_EXPERTS, D_EXPERT, D_MODEL), D_EXPERT ** -0.5),
    }

def reference(x_prompt, x_sample, cache_mla_ckv, cache_mla_krope, state_retention, c, c_ctx,
              ada_w, ada_b, norm_mix, norm_ffn,
              ev_w_in, ev_q_a_norm, ev_w_q_up, ev_kv_a_norm, ev_w_kv_up, ev_q_norm, ev_k_norm,
              ev_ret_decay, ev_ret_gn, ev_w_out,
              od_w_in, od_dw, od_dw_b, od_ln_g, od_ln_b, od_w_out,
              moe_w_group, moe_b_group, moe_w_expert, moe_b_expert, moe_w_up, moe_w_down):
    xp, xs = x_prompt, x_sample
    new_ckv, new_krope, new_state = [], [], []
    for l in range(DEPTH):
        mp = modulation(c_ctx[None, :], ada_w[l], ada_b[l])
        ms = modulation(c, ada_w[l], ada_b[l])
        hp = modulate(rms_norm(xp, norm_mix[l]), mp[0], mp[1])
        hs = modulate(rms_norm(xs, norm_mix[l]), ms[0], ms[1])
        j = l // 2
        if l % 2 == 0:
            even = (ev_w_in[j], ev_q_a_norm[j], ev_w_q_up[j], ev_kv_a_norm[j], ev_w_kv_up[j],
                    ev_q_norm[j], ev_k_norm[j], ev_ret_decay[j], ev_ret_gn[j], ev_w_out[j])
            yp, ckv, kr, st = even_mixer_context(hp, *even)
            ys = even_mixer_latent(hs, cache_mla_ckv[:, j], cache_mla_krope[:, j], state_retention[:, j], *even)
            new_ckv.append(ckv)
            new_krope.append(kr)
            new_state.append(st)
        else:
            odd = (od_w_in[j], od_dw[j], od_dw_b[j], od_ln_g[j], od_ln_b[j], od_w_out[j])
            yp = conformer_conv(hp, *odd)
            ys = conformer_conv(hs, *odd)
        xp = xp + mp[2] * yp
        xs = xs + ms[2] * ys
        moe = (moe_w_group[l], moe_b_group[l], moe_w_expert[l], moe_b_expert[l], moe_w_up[l], moe_w_down[l])
        hp = modulate(rms_norm(xp, norm_ffn[l]), mp[3], mp[4])
        hs = modulate(rms_norm(xs, norm_ffn[l]), ms[3], ms[4])
        xp = xp + mp[5] * hier_moe(hp, *moe)
        xs = xs + ms[5] * hier_moe(hs, *moe)
    new_mla_ckv = jnp.stack(new_ckv, axis=1)
    new_mla_krope = jnp.stack(new_krope, axis=1)
    new_retention_state = jnp.stack(new_state, axis=1)
    return (xp, xs, new_mla_ckv, new_mla_krope, new_retention_state)


_drawn_inputs = setup_inputs


def setup_inputs(seed=0):
    import zlib

    import numpy as np

    out = dict(_drawn_inputs(seed))
    spreads = {}
    factors = {'cache_mla_ckv': 5.674,
     'cache_mla_krope': 8.0,
     'norm_ffn': 3.751,
     'ev_q_a_norm': 8.0,
     'ev_kv_a_norm': 2.809,
     'ev_q_norm': 8.0,
     'ev_k_norm': 8.0,
     'ev_ret_gn': 8.0,
     'od_dw_b': 8.0,
     'od_ln_g': 8.0,
     'od_ln_b': 8.0,
     'moe_b_group': 7.605,
     'moe_b_expert': 6.439}
    for name, (base, spread) in spreads.items():
        noise = np.random.default_rng([zlib.crc32(name.encode()), seed]).standard_normal(out[name].shape)
        drawn = base * np.exp(spread * noise) if base else spread * noise
        out[name] = __import__('jax').numpy.asarray(drawn.astype(out[name].dtype))
    for name, factor in factors.items():
        out[name] = (out[name] * factor).astype(out[name].dtype)
    return out
```

```python
from contextlib import ExitStack

import concourse.bass as bass
from concourse import mybir

F32 = mybir.dt.float32
I32 = mybir.dt.int32
U32 = mybir.dt.uint32
ALU = mybir.AluOpType
ACT = mybir.ActivationFunctionType
AX = mybir.AxisListType

P = 128
D = 1024
KD = D // P
SAMPLE, CONTEXT = 512, 128
T = SAMPLE + CONTEXT
NT = T // P
ST = SAMPLE // P
PAST = 128
GRID_W = 64
EPS = 1e-6
HEADS, NOPE, ROPE, VD = 8, 64, 32, 64
QK = NOPE + ROPE
QRANK, KVRANK = 256, 128
RH, RK, RV = 4, 64, 128
EVEN_IN = QRANK + KVRANK + ROPE + 2 * RH * RK + 2 * RH * RV
Z_KR = QRANK + KVRANK
Z_RQ = Z_KR + ROPE
Z_RK = Z_RQ + RH * RK
Z_RV = Z_RK + RH * RK
Z_RG = Z_RV + RH * RV
CONV = 1024
TAPS = 31
HALO = TAPS // 2
PADW = HALO + SAMPLE + HALO + CONTEXT + HALO
SPAN = SAMPLE + HALO + CONTEXT
CTX0 = SAMPLE + HALO
GROUPS, PER, EXPERTS, TOPK, FF = 4, 8, 32, 2, 256
ROUTE = GROUPS + EXPERTS
ROWS = T * TOPK
RT = ROWS // P
BLK = 64
XW = ROWS + BLK
MAXBLK = (T + BLK - 1) // BLK
ALLBLK = ROWS // BLK + EXPERTS

SLOT = 2048
SLOTS = 9
PER_EXPERT = 3
RING_EXPERTS = SLOTS // PER_EXPERT

C_ID, C_ONE, C_TRI = 0, P, 2 * P
D_A1, D_U, D_A2, D_L = 0, P, 2 * P, 3 * P
C_COS = 3 * P
C_SIN = C_COS + ST * 16
C_POS = C_SIN + ST * 16
C_PRI4 = C_POS + 4
C_PRI8 = C_PRI4 + 4
C_THR = C_PRI8 + 8
C_EPS = C_THR + MAXBLK - 1
C_W = C_EPS + 1

V_ADAB, V_COND, V_NMIX = 0, 96, 112
V_NFFN, V_DWB, V_LNG, V_LNB, V_GN, V_QA = 0, 16, 24, 32, 40, 44
V_ROWS = (128, 46, 128, TAPS * 8 - 128)

A_H = 0
A_QT = 0
A_Z = 5120
A_KT = A_Z + NT * EVEN_IN
A_V = A_KT + 6144
ARENA = A_V + 3072
A_XS = 0
A_HTOK = 5120
A_YG = KD * XW
A_BLK = A_YG + 2 * NT * D
A_U = 5120
A_CV = A_U + KD * PADW
A_DG = A_CV + KD * SPAN
PE_TAPS = 16
assert A_BLK + 1408 <= ARENA and A_DG + 2 * PE_TAPS * P <= ARENA


def weight_plan():
    plan = [("ada0", j) for j in range(8)]
    for c in range(8):
        plan += [("ev_in", c), ("ada0", 8 + 2 * c), ("ada0", 9 + 2 * c)]
    plan += [("ada1", j) for j in range(20)]
    plan += [("q_up", 0), ("kv_up", 0)]
    plan += [("ada1", j) for j in range(20, 24)]
    plan += [("ev_out", j) for j in range(4)]
    plan += [("expert0", i) for i in range(PER_EXPERT * EXPERTS)]
    plan += [("od_in", j) for j in range(8)]
    plan += [("od_out", j) for j in range(4)]
    plan += [("expert1", i) for i in range(PER_EXPERT * EXPERTS)]
    return plan


def build(nc, io):
    f = io
    ctx = ExitStack()
    with ctx:
        def sb(name, shape, dt=F32):
            return ctx.enter_context(nc.sbuf_tensor(name, shape, dt))

        def sem(name):
            return ctx.enter_context(nc.semaphore(name))

        xT = sb("xT", [P, KD, T])
        arena = sb("arena", [P, ARENA])
        ring = sb("ring", [P, SLOTS, SLOT])
        cst = sb("cst", [P, C_W])
        vrow = arena[:, A_V:A_V + 4 * P].rearrange("p (g n) -> p g n", g=4)
        vecT = sb("vecT", [P, 4, P])
        scT = sb("scT", [P, KD, 2])
        modT = sb("modT", [P, 2, 48, 2])
        modA = sb("modA", [P, 4, KD, 2])
        wr = sb("wr", [P, KD, ROUTE])
        rb = sb("rb", [P, 2, ROUTE])
        kvg = sb("kvg", [P, KVRANK])
        qkg = sb("qkg", [P, 2, QK])
        dec = sb("dec", [P, 2 * RH])
        decw = sb("decw", [P, 3, 2 * RH])
        edge = sb("edge", [P, 6, RH])
        cache_cT = sb("cache_cT", [P, P])
        ss = sb("ss", [P, 2, 16])
        stat = sb("stat", [P, RH, 6])
        mv = sb("mv", [P, RH, 2])
        rmv = sb("rmv", [P, RH])
        nmx = sb("nmx", [P, 2])
        den = sb("den", [P, 2])
        rden = sb("rden", [P, 2])
        r1 = sb("r1", [P, 12, NT])
        cnt = sb("cnt", [P, 6, EXPERTS])
        posf = sb("posf", [P, 2, NT])
        posu = sb("posu", [P, 2 * NT], U32)
        wtok = sb("wtok", [P, 2, NT])
        tab = sb("tab", [1, 3 * EXPERTS + 1], I32)
        blocks0 = sb("blocks0", [P, 1])
        tick = sb("tick", [P, 4])
        PS = ctx.enter_context(nc.psum_tensor("PS", [P, 8, 512], F32))

        rows_in = nc.dram_tensor("rows_in", (ROWS, D), F32).ap()
        rows_out = nc.dram_tensor("rows_out", (XW, D), F32).ap()

        ident = cst[:, C_ID:C_ID + P]
        ones = cst[:, C_ONE:C_ONE + P]
        tri = cst[:, C_TRI:C_TRI + P]
        eps = cst[:, C_EPS:C_EPS + 1]

        hT = arena[:, A_H:A_H + KD * T].rearrange("p (k t) -> p k t", k=KD)
        z = arena[:, A_Z:A_Z + NT * EVEN_IN].rearrange("p (t n) -> p t n", t=NT)
        xtok = arena[:, A_Z:A_Z + NT * D].rearrange("p (t n) -> p t n", t=NT)
        A_K = A_KT
        states = arena[:, A_K:A_K + ST * 512].rearrange("p (t h n) -> p t h n", t=ST, h=RH)
        upd = arena[:, A_K + 2048:A_K + 2048 + NT * 512].rearrange("p (t h n) -> p t h n", t=NT, h=RH)
        rqT = arena[0:RK, A_K + 4608:A_K + 5120].rearrange("p (h n) -> p h n", h=RH)
        rkT = arena[0:RK, A_K + 5120:A_K + 5632].rearrange("p (h n) -> p h n", h=RH)
        qfbT = arena[:, A_K + 5632:A_K + 6144].rearrange("p (h n) -> p h n", h=RH)
        kfb = arena[:, A_V:A_V + 512].rearrange("p (h n) -> p h n", h=RH)
        qfb = arena[:, A_V + 512:A_V + 1024].rearrange("p (h n) -> p h n", h=RH)
        rsc = arena[:, A_V + 1024:A_V + 1536].rearrange("p (h n) -> p h n", h=RH)
        onrm = arena[:, A_V + 1536:A_V + 2048].rearrange("p (h n) -> p h n", h=RH)
        mtmp = arena[:, A_V + 1024:A_V + 2048].rearrange("p (a n) -> p a n", a=8)
        dist = arena[:, A_V + 2048:A_V + 2560]
        mask = arena[:, A_V + 2560:A_V + 3072].rearrange("p (h n) -> p h n", h=RH)
        qT = arena[0:QK, A_QT:A_QT + HEADS * T].rearrange("p (h t) -> p h t", h=HEADS)
        kT = arena[0:QK, A_KT:A_KT + HEADS * 768].rearrange("p (h t) -> p h t", h=HEADS)
        vS = arena[:, A_V:A_V + 3072].rearrange("p (j h n) -> p j h n", j=6, h=HEADS)

        def part(off, n):
            return z[:, :, Z_RV + off:Z_RV + off + n]
        cT = z[:, :, Z_RV:Z_RV + 3 * P].rearrange("p t (j n) -> p t j n", j=3)
        prob = [part(0, P), part(P, P)]
        probT = [part(2 * P, P), part(3 * P, P)]
        omla = z[:, :, Z_RQ:Z_RQ + 512]
        oret = z[:, :, Z_RG:Z_RG + 512]
        oT = arena[:, A_KT:A_KT + KD * T].rearrange("p (k t) -> p k t", k=KD)
        htok = arena[:, A_HTOK:A_HTOK + NT * D].rearrange("p (t n) -> p t n", t=NT)
        xsT = arena[:, A_XS:A_XS + KD * XW].rearrange("p (k r) -> p k r", k=KD)
        xback = arena[:, A_YG:A_YG + RT * D].rearrange("p (j n) -> p j n", j=RT)
        ygat = xback
        xblk = arena[:, A_BLK:A_BLK + 512].rearrange("p (k n) -> p k n", k=KD)
        gsil = arena[:, A_BLK + 512:A_BLK + 640]
        gact = arena[:, A_BLK + 640:A_BLK + 768]
        hblk = arena[:, A_BLK + 768:A_BLK + 896].rearrange("p (i n) -> p i n", i=2)
        yblk = arena[:, A_BLK + 896:A_BLK + 1408]
        upad = arena[:, A_U:A_U + KD * PADW].rearrange("p (k t) -> p k t", k=KD)
        cv = arena[:, A_CV:A_CV + KD * SPAN].rearrange("p (k t) -> p k t", k=KD)
        cv2 = arena[:, 0:KD * SPAN].rearrange("p (k t) -> p k t", k=KD)
        tapd = arena[:, A_DG:A_DG + 2 * PE_TAPS * P].rearrange("p (b w n) -> p b w n", b=2, w=PE_TAPS)
        cache_in = sb("cache_in", [P, KVRANK + ROPE])
        scratch = sb("scratch", [P, 3 * HEADS * QK])
        qkraw = scratch[:, 0:2 * HEADS * QK].rearrange("p (b n) -> p b n", b=2)
        qksq = scratch[:, 2 * HEADS * QK:].unsqueeze(1)
        ropet = z[:, 0:4, Z_RV + 3 * P:Z_RV + 4 * P]
        cell = [0]

        def cells(*shape):
            n = 1
            for x in shape:
                n *= x
            cell[0] += n
            assert cell[0] <= 3 * HEADS * QK
            names = " ".join("abc"[:len(shape)])
            return scratch[:, cell[0] - n:cell[0]].rearrange(
                f"p ({names}) -> p {names}", **dict(zip("abc", shape))) if len(shape) > 1 \
                else scratch[:, cell[0] - n:cell[0]]
        lgt = cells(NT, ROUTE)
        rt = cells(9, NT, PER)
        one32 = cells(2, NT, EXPERTS)
        both = cells(NT, EXPERTS)
        slotpos = cells(NT, EXPERTS)
        cmpt = cells(EXPERTS, MAXBLK - 1)
        rs = cells(T)

        plan = weight_plan()
        at = {}
        for n, key in enumerate(plan):
            at[key] = n
        ring_full = [sem(f"ring_full{s}") for s in range(SLOTS)]
        S = {}

        def ev(name):
            if name not in S:
                S[name] = sem(name)
            return S[name]

        def released(key):
            kind, j = key
            if kind == "ada0":
                return ev("mod_mm"), j + 1
            if kind == "ada1":
                return ev("mod_mm"), 24 + j + 1
            if kind == "ev_in":
                return ev("z_mm"), NT * (j + 1)
            if kind in ("q_up", "kv_up"):
                return ev("qk_mm"), NT + NT + 1
            if kind == "ev_out":
                return ev("wo_mm"), 2 * (j + 1)
            if kind == "od_in":
                return ev("gate_mm"), j + 1
            if kind == "od_out":
                return ev("wo_mm"), KD + 2 * (j + 1)
            return ev("expert_done"), EXPERTS * int(kind[6]) + j // PER_EXPERT + 1

        NPARAM = 14
        sum_sem = ("tap_sum0", "tap_sum1")
        full_count, filled = [], [0] * SLOTS
        for n, key in enumerate(plan):
            filled[n % SLOTS] += 32 if key[0] == "od_in" else 16
            full_count.append(filled[n % SLOTS])
        NATT = ST * HEADS + HEADS
        ATT = [(t, h) for t in range(ST) for h in range(HEADS)] + [(ST, h) for h in range(HEADS)]
        UNITS = [(kind, t) for t in range(NT) for kind in "qk"] + [("k", NT)]
        KCOL = [0, P, 2 * P, 3 * P, 5 * P, 4 * P]
        VROW = [0, 1, 2, 3, 5, 4]
        PSf = PS[:, :, :].rearrange("p b n -> p (b n)")

        def w_view(key):
            return ring[:, at[key] % SLOTS, :]

        def quad(b):
            return PS[:, b, :].rearrange("p (j n) -> p j n", j=4)

        def bc(ap, shape):
            return ap.to_broadcast(shape)

        block = ctx.enter_context(nc.Block())

        @block.sync
        def _(sp):
            def source(key):
                kind, j = key
                v8 = w_view(key).rearrange("p (k n) -> p k n", k=KD)
                if kind in ("ada0", "ada1"):
                    return f["ada_w"][int(kind[3]), :, 256 * j:256 * j + 256].rearrange("(k p) n -> p k n", p=P), v8
                if kind == "ev_in":
                    n = min(256, EVEN_IN - 256 * j)
                    return f["ev_w_in"][0, :, 256 * j:256 * j + n].rearrange("(k p) n -> p k n", p=P), v8[:, :, 0:n]
                if kind == "q_up":
                    return (f["ev_w_q_up"][0].rearrange("(k p) n -> p k n", p=P),
                            w_view(key)[:, 0:1536].rearrange("p (k n) -> p k n", k=2))
                if kind == "kv_up":
                    return f["ev_w_kv_up"][0], w_view(key)[:, 0:1024]
                if kind in ("ev_out", "od_out"):
                    w = f["ev_w_out" if kind == "ev_out" else "od_w_out"]
                    return w[0, :, 256 * j:256 * j + 256].rearrange("(k p) n -> p k n", p=P), v8

            def load(n):
                key = plan[n]
                if n >= SLOTS:
                    sp.wait_ge(*released(plan[n - SLOTS]))
                full = ring_full[n % SLOTS]
                if key[0] == "od_in":
                    v = f["od_w_in"][0].rearrange("(k p) (a n) -> p k a n", p=P, a=2)
                    d = w_view(key).rearrange("p (k a n) -> p k a n", k=KD, a=2)
                    for a in range(2):
                        sp.dma_start(d[:, :, a, :], v[:, :, a, P * key[1]:P * key[1] + P]).then_inc(full, 16)
                elif key[0].startswith("expert"):
                    load_part(int(key[0][6]), key[1] // PER_EXPERT, key[1] % PER_EXPERT, n % SLOTS)
                else:
                    src, dst = source(key)
                    sp.dma_start(dst, src).then_inc(full, 16)

            def load_part(l, e, j, s):
                if j < 2:
                    src = f["moe_w_up"][l, bass.ds(e, 1), 512 * j:512 * j + 512, :] \
                        .rearrange("e (k p) n -> p (e k) n", p=P)
                    sp.dma_start(ring[:, s, :].rearrange("p (k n) -> p k n", k=4), src).then_inc(ring_full[s], 16)
                else:
                    src = f["moe_w_down"][l, bass.ds(e, 1), :, :].rearrange("e (k p) n -> p (e k) n", p=P)
                    sp.dma_start(ring[:, s, :].rearrange("p (k n) -> p k n", k=2), src).then_inc(ring_full[s], 16)

            def load_experts(l):
                n0 = at[(f"expert{l}", 0)]
                rounds = EXPERTS // RING_EXPERTS
                for i in range(SLOTS):
                    load(n0 + i)
                with sp.Fori(1, rounds) as g:
                    for p in range(RING_EXPERTS):
                        sp.wait_ge(ev("expert_done"), g * RING_EXPERTS + (EXPERTS * l + p + 1 - RING_EXPERTS))
                        for j in range(PER_EXPERT):
                            load_part(l, g * RING_EXPERTS + p, j, (n0 + PER_EXPERT * p + j) % SLOTS)
                for n in range(n0 + SLOTS * rounds, n0 + PER_EXPERT * EXPERTS):
                    load(n)

            n = 0
            while n < len(plan):
                if plan[n][0].startswith("expert"):
                    load_experts(int(plan[n][0][6]))
                    n += PER_EXPERT * EXPERTS
                else:
                    load(n)
                    n += 1
            for t in range(NT):
                sp.wait_ge(ev("fin_v"), t + 1)
                sp.wait_ge(ev("fin_a"), t + 1)
                dst = f["y_sample"][0, t * P:t * P + P, :] if t < ST else f["y_prompt"][0, :, :]
                sp.dma_start(dst, xtok[:, t, :]).then_inc(ev("y_out"), 16)
            sp.wait_ge(ev("y_out"), 16 * NT)

        @block.tensor
        def _(pe):
            def arrived(key):
                n = at[key]
                pe.wait_ge(ring_full[n % SLOTS], full_count[n])

            def modulation(l, j, b, first):
                arrived((f"ada{l}", j))
                w = w_view((f"ada{l}", j)).rearrange("p (k n) -> p k n", k=KD)
                for m in range(2):
                    c = 2 * (2 * (j - first) + m)
                    for k in range(KD):
                        last = pe.matmul(PS[:, b, c:c + 2], w[:, k, m * P:m * P + P], scT[:, k, :],
                                         start=(k == 0), stop=(k == KD - 1))
                last.then_inc(ev("mod_mm"), 1)

            def norm_sums(q):
                for k in range(KD):
                    pe.wait_ge(ev("squared"), KD * q + k + 1)
                    pe.matmul(PS[:, 4, :], ones, hT[:, k, 0:SAMPLE], start=(k == 0), stop=(k == KD - 1))
                    last = pe.matmul(PS[:, 6, 0:CONTEXT], ones, hT[:, k, SAMPLE:T],
                                     start=(k == 0), stop=(k == KD - 1))
                last.then_inc(ev("sumsq"), 1)

            def project_out(l, kind, src_s, src_c):
                for m in range(KD):
                    if m % 2 == 0:
                        arrived((kind, m // 2))
                        w = w_view((kind, m // 2)).rearrange("p (k n) -> p k n", k=KD)
                    if m >= 2:
                        pe.wait_ge(ev("wo_ev"), KD * l + m - 1)
                    b = 4 + 2 * (m % 2)
                    c = (m % 2) * P
                    for k in range(KD):
                        if l == 1 and m == 0:
                            pe.wait_ge(ev("act1"), k + 1)
                        pe.matmul(PS[:, b, :], w[:, k, c:c + P], src_s(k), start=(k == 0), stop=(k == KD - 1))
                        last = pe.matmul(PS[:, b + 1, 0:CONTEXT], w[:, k, c:c + P], src_c(k),
                                         start=(k == 0), stop=(k == KD - 1))
                    last.then_inc(ev("wo_mm"), 1)

            pe.wait_ge(ev("params_in"), 16 * NPARAM)
            for g, r in enumerate(V_ROWS):
                last = pe.transpose(PS[:, 5, g * P:g * P + r], vrow[0:r, g, :], cst[0:r, C_ID:C_ID + r])
            last.then_inc(ev("vec_t"), 1)
            for i in range(2 * NT):
                t, half = i // 2, i % 2
                if half == 0:
                    pe.wait_ge(ev("x_in0" if t < ST else "x_in1"), 16)
                if i >= 4:
                    pe.wait_ge(ev(("xt_v", "xt_a")[i % 2]), (i - 4) // 2 + 1)
                for j in range(4):
                    last = pe.transpose(quad(i % 4)[:, j, :],
                                        xtok[:, t, (4 * half + j) * P:(4 * half + j + 1) * P], ident)
                last.then_inc(ev("x_t"), 1)
            norm_sums(0)
            pe.wait_ge(ev("sc_ready"), 1)
            for j in range(8):
                modulation(0, j, 7, 0)
            pe.wait_ge(ev("xt_v"), NT)
            pe.wait_ge(ev("xt_a"), NT)
            pe.wait_ge(ev("vec_c"), 4)
            for c in range(8):
                n = min(256, EVEN_IN - 256 * c)
                arrived(("ev_in", c))
                w = w_view(("ev_in", c)).rearrange("p (k n) -> p k n", k=KD)
                for t in range(NT):
                    i = NT * c + t
                    if i >= 4:
                        pe.wait_ge(ev(("z_v", "z_a")[i % 2]), (i - 4) // 2 + 1)
                    for k in range(KD):
                        if i < NT:
                            pe.wait_ge(ev("h_s" if t < ST else "h_c"), k + 1)
                        last = pe.matmul(PS[:, i % 4, 0:n], hT[:, k, t * P:t * P + P], w[:, k, 0:n],
                                         start=(k == 0), stop=(k == KD - 1))
                    last.then_inc(ev("z_mm"), 1)
                for j in (8 + 2 * c, 9 + 2 * c):
                    modulation(0, j, 5, 8)
            pe.wait_ge(ev("z_v"), 20)
            pe.wait_ge(ev("z_a"), 20)
            pe.wait_ge(ev("mod_c"), 1)
            for t in range(NT):
                pe.wait_ge(ev("kfb"), t + 1)
                if t >= 2:
                    pe.wait_ge(ev("upd_c"), t - 1)
                for h in range(RH):
                    last = pe.matmul(quad(t % 2)[:, h, :], kfb[:, h, :], z[:, t, Z_RV + h * RV:Z_RV + (h + 1) * RV],
                                     start=True, stop=True)
                last.then_inc(ev("upd_mm"), 1)
                modulation(1, 2 * t, 7, 0)
                modulation(1, 2 * t + 1, 7, 0)
            pe.wait_ge(ev("upd_c"), NT)
            pe.wait_ge(ev("mod_c"), 2)
            for t in range(NT):
                if t >= 1:
                    pe.wait_ge(ev("rq_c"), t)
                for h in range(RH):
                    last = pe.transpose(quad(0)[0:RK, h, :], z[:, t, Z_RQ + h * RK:Z_RQ + (h + 1) * RK], ident)
                last.then_inc(ev("rq_t"), 1)
                if t >= 1:
                    pe.wait_ge(ev("rk_c"), t)
                for h in range(RH):
                    last = pe.transpose(quad(1)[0:RK, h, :], z[:, t, Z_RK + h * RK:Z_RK + (h + 1) * RK], ident)
                last.then_inc(ev("rk_t"), 1)
                if t < ST:
                    pe.wait_ge(ev("qfb"), t + 1)
                    if t >= 1:
                        pe.wait_ge(ev("qfb_c"), t)
                    for h in range(RH):
                        last = pe.transpose(quad(2)[:, h, :], qfb[:, h, :], ident)
                    last.then_inc(ev("qfb_t"), 1)
                modulation(1, 10 + 2 * t, 7, 0)
                pe.wait_ge(ev("rq_c"), t + 1)
                pe.wait_ge(ev("rk_c"), t + 1)
                if t >= 1:
                    pe.wait_ge(ev("rsc"), t)
                for h in range(RH):
                    last = pe.matmul(quad(3)[:, h, :], rkT[:, h, :], rqT[:, h, :], start=True, stop=True)
                last.then_inc(ev("rs_mm"), 1)
                modulation(1, 11 + 2 * t, 7, 0)
                pe.wait_ge(ev("rsc"), t + 1)
                if t < ST:
                    pe.wait_ge(ev("qfb_c"), t + 1)
                    pe.wait_ge(ev("state_f"), ST - 1)
                    pe.wait_ge(ev("state_b"), ST - 1)
                if t >= 1:
                    pe.wait_ge(ev("onrm"), t)
                for h in range(RH):
                    last = pe.matmul(quad(4)[:, h, :], rsc[:, h, :], z[:, t, Z_RV + h * RV:Z_RV + (h + 1) * RV],
                                     start=True, stop=(t == ST))
                    if t < ST:
                        last = pe.matmul(quad(4)[:, h, :], qfbT[:, h, :], states[:, t, h, :],
                                         start=False, stop=True)
                last.then_inc(ev("ro_mm"), 1)
            for t in range(NT + 1):
                if t < NT:
                    pe.wait_ge(ev("lat_n"), t + 1)
                if t >= 2:
                    pe.wait_ge(ev("lat_c"), t - 1)
                b = 5 + t % 2
                if t < NT:
                    for j in range(3):
                        last = pe.transpose(quad(b)[:, j, :], z[:, t, j * P:(j + 1) * P], ident)
                else:
                    last = pe.transpose(quad(b)[:, 0, :], cache_in[:, 0:KVRANK], ident)
                last.then_inc(ev("lat_t"), 1)
            arrived(("q_up", 0))
            arrived(("kv_up", 0))
            wq = w_view(("q_up", 0))[:, 0:1536].rearrange("p (k n) -> p k n", k=2)
            wkv = w_view(("kv_up", 0))
            pe.wait_ge(ev("lat_c"), NT + 1)
            pe.wait_ge(ev("onrm"), NT)
            for u in range(len(UNITS) + 1):
                if u < len(UNITS):
                    kind, t = UNITS[u]
                    b = 2 * (u % 2)
                    if u >= 2:
                        pe.wait_ge(ev("raw_a"), u - 1)
                        if UNITS[u - 2][0] == "k":
                            pe.wait_ge(ev("v_c"), (u - 2) // 2 + 1 if u - 2 < 10 else 6)
                    if u == 10:
                        pe.wait_ge(ev("v_c"), 4)
                    for half in range(2):
                        if kind == "q":
                            for k in range(2):
                                last = pe.matmul(PS[:, b + half, 0:384], cT[:, t, k, :],
                                                 wq[:, k, half * 384:half * 384 + 384],
                                                 start=(k == 0), stop=(k == 1))
                        else:
                            lat = cT[:, t, 2, :] if t < NT else cache_cT[:, :]
                            last = pe.matmul(PS[:, b + half, :], lat, wkv[:, half * 512:half * 512 + 512],
                                             start=True, stop=True)
                    last.then_inc(ev("qk_mm"), 1)
                    if u % 2 == 1 and u // 2 < 4:
                        modulation(1, 20 + u // 2, 7, 0)
                if u >= 1:
                    pe.wait_ge(ev("qk_n"), u)
                    if u >= 2:
                        pe.wait_ge(ev("hd_a"), u - 1)
                        pe.wait_ge(ev("hd_v"), u - 1)
                    raw = qkraw[:, (u - 1) % 2, :].rearrange("p (h n) -> p h n", h=HEADS)
                    for h in range(HEADS):
                        last = pe.transpose(quad(4 + h // 4)[0:QK, h % 4, :], raw[:, h, :], ident)
                    last.then_inc(ev("hd_t"), 1)
            pe.wait_ge(ev("hd_a"), len(UNITS))
            pe.wait_ge(ev("hd_v"), len(UNITS))
            pe.wait_ge(ev("v_c"), NT + 1)
            pe.wait_ge(ev("mod_c"), 3)
            for i in range(NATT + 2):
                if i < NATT:
                    t, h = ATT[i]
                    b = 2 * (i % 2)
                    if i >= 2:
                        pe.wait_ge(ev("prob"), i - 1)
                    if t < ST:
                        pe.matmul(PS[:, b, :], qT[:, h, t * P:t * P + P], kT[:, h, 0:512], start=True, stop=True)
                        last = pe.matmul(PS[:, b + 1, 0:P], qT[:, h, t * P:t * P + P], kT[:, h, 512:640],
                                         start=True, stop=True)
                    else:
                        last = pe.matmul(PS[:, b, 0:P], qT[:, h, t * P:t * P + P], kT[:, h, 640:768],
                                         start=True, stop=True)
                    last.then_inc(ev("s_mm"), 1)
                if 1 <= i <= NATT:
                    t, h = ATT[i - 1]
                    n = ST + 1 if t < ST else 1
                    pe.wait_ge(ev("prob"), i)
                    if i >= 2:
                        pe.wait_ge(ev("pt_a"), i - 1)
                        pe.wait_ge(ev("pt_v"), min(i - 1, ST * HEADS))
                    for j in range(n):
                        last = pe.transpose(quad(4 + j // 4)[:, j % 4, :], prob[(i - 1) % 2][:, j, :], ident)
                    last.then_inc(ev("p_t"), 1)
                if i >= 2:
                    t, h = ATT[i - 2]
                    n = ST + 1 if t < ST else 1
                    pe.wait_ge(ev("pt_a"), i - 1)
                    pe.wait_ge(ev("pt_v"), min(i - 1, ST * HEADS))
                    if i >= 4:
                        pe.wait_ge(ev("o_c"), i - 3)
                    for j in range(n):
                        last = pe.matmul(PS[:, 6 + i % 2, 0:VD], probT[i % 2][:, j, :],
                                         vS[:, j if t < ST else 5, h, :], start=(j == 0), stop=(j == n - 1))
                    last.then_inc(ev("pv_mm"), 1)
            pe.wait_ge(ev("o_c"), NATT)
            pe.wait_ge(ev("gated"), NT)
            for i in range(2 * NT):
                t, half = i // 2, i % 2
                if i >= 4:
                    pe.wait_ge(ev("ot_v" if half else "ot_a"), (i - 4) // 2 + 1)
                src = oret if half else omla
                for j in range(4):
                    last = pe.transpose(quad(i % 4)[:, j, :], src[:, t, j * P:(j + 1) * P], ident)
                last.then_inc(ev("o_t"), 1)
            pe.wait_ge(ev("ot_a"), NT)
            pe.wait_ge(ev("ot_v"), NT)
            project_out(0, "ev_out", lambda k: oT[:, k, 0:SAMPLE], lambda k: oT[:, k, SAMPLE:T])

            def moe(l):
                q = 2 * l + 1
                pe.wait_ge(ev("wo_ev"), KD * l + KD)
                norm_sums(q)
                pe.wait_ge(ev("wr_in"), 32 * (l + 1))
                for t in range(NT):
                    for k in range(KD):
                        if t in (0, ST):
                            pe.wait_ge(ev("h_s" if t < ST else "h_c"), KD * q + k + 1)
                        last = pe.matmul(PS[:, 0, t * ROUTE:(t + 1) * ROUTE], hT[:, k, t * P:t * P + P],
                                         wr[:, k, :], start=(k == 0), stop=(k == KD - 1))
                last.then_inc(ev("route_mm"), 1)
                for i in range(2 * NT):
                    t, half = i // 2, i % 2
                    if i >= 4:
                        pe.wait_ge(ev("htok_a"), 2 * NT * l + i - 3)
                    for j in range(4):
                        last = pe.transpose(quad((1, 2, 3, 7)[i % 4])[:, j, :],
                                            hT[:, 4 * half + j, t * P:t * P + P], ident)
                    last.then_inc(ev("htok_t"), 1)
                pe.wait_ge(ev("chosen"), l + 1)
                for t in range(NT):
                    for j in range(t + 1):
                        pe.matmul(PS[:, 5, t * EXPERTS:(t + 1) * EXPERTS], ones if j < t else tri, both[:, j, :],
                                  start=(j == 0), stop=(j == t))
                for j in range(NT):
                    last = pe.matmul(PS[:, 6, 0:EXPERTS], ones, both[:, j, :], start=(j == 0), stop=(j == NT - 1))
                last.then_inc(ev("rank_mm"), 1)
                pe.wait_ge(ev("htok_a"), 2 * NT * l + 2 * NT)
                for i in range(2 * RT):
                    j, half = i // 2, i % 2
                    if half == 0 and j % 2 == 0:
                        pe.wait_ge(ev(f"rows_back{j // 2}"), 16 * (l + 1))
                    if i >= 4:
                        pe.wait_ge(ev(("xs_v", "xs_a")[i % 2]), RT * l + (i - 4) // 2 + 1)
                    for m in range(4):
                        last = pe.transpose(quad(i % 4)[:, m, :], xback[:, j, (4 * half + m) * P:(4 * half + m + 1) * P],
                                            ident)
                    last.then_inc(ev("xs_t"), 1)
                pe.wait_ge(ev("xs_v"), RT * l + RT)
                pe.wait_ge(ev("xs_a"), RT * l + RT)
                pe.wait_ge(ev("pad"), l + 1)
                pe.wait_ge(ev("tab"), 4 * l + 4)
                n0 = at[(f"expert{l}", 0)]

                def expert(e, p, laps):
                    blocks = pe.value_load(tab[0:1, bass.ds(e + EXPERTS, 1)], min_val=1, max_val=MAXBLK)
                    before = pe.value_load(tab[0:1, bass.ds(e + 2 * EXPERTS, 1)], min_val=0, max_val=2 * ALLBLK)
                    s = [(n0 + PER_EXPERT * p + j) % SLOTS for j in range(PER_EXPERT)]
                    up = [ring[:, s[j], :].rearrange("p (k a n) -> p k a n", k=4, a=2) for j in range(2)]
                    down = ring[:, s[2], :].rearrange("p (k n) -> p k n", k=2)
                    with pe.Fori(0, blocks) as b:
                        pe.wait_ge(ev("xblk_c"), before + b + 1)
                        pe.wait_ge(ev("act"), before + b + 1)
                        for k in range(KD):
                            if k % 4 == 0:
                                pe.wait_ge(ring_full[s[k // 4]], laps(PER_EXPERT * p + k // 4))
                            for i in range(2):
                                last = pe.matmul(
                                    PS[i * BLK:(i + 1) * BLK, 0, 0:2 * P].rearrange("p (a n) -> p a n", a=2),
                                    xblk[:, k, :], up[k // 4][:, k % 4, :, i * P:(i + 1) * P],
                                    start=(k == 0), stop=(k == KD - 1))
                        last.then_inc(ev("up_mm"), 1)
                        pe.wait_ge(ev("act"), before + b + 2)
                        pe.transpose(PS[:, 1, 0:P], gact[:, :], ident).then_inc(ev("h_t"), 1)
                        pe.wait_ge(ring_full[s[2]], laps(PER_EXPERT * p + 2))
                        pe.wait_ge(ev("hblk_c"), before + b + 1)
                        pe.wait_ge(ev("yblk_c"), before + b + 1)
                        for i in range(2):
                            for c in range(2):
                                last = pe.matmul(PS[c * BLK:(c + 1) * BLK, 2, :], hblk[:, i, :],
                                                 down[:, i, c * 512:(c + 1) * 512], start=(i == 0), stop=(i == 1))
                        last.then_inc(ev("down_mm"), 1)

                rounds = EXPERTS // RING_EXPERTS
                with pe.Fori(0, rounds) as g:
                    for p in range(RING_EXPERTS):
                        expert(g * RING_EXPERTS + p, p, lambda c: g * 16 + full_count[n0 + c])
                for e in range(rounds * RING_EXPERTS, EXPERTS):
                    expert(e, e % RING_EXPERTS, lambda c: 16 * rounds + full_count[n0 + c])
                for i in range(2 * NT):
                    t, half = i // 2, i % 2
                    if half == 0:
                        pe.wait_ge(ev("comb_v"), NT * l + t + 1)
                    if i >= 4:
                        pe.wait_ge(ev("comb"), 2 * NT * l + i - 3)
                    for m in range(4):
                        c = (4 * half + m) * P
                        last = pe.transpose(quad(4 + i % 4)[:, m, :], ygat[:, t, c:c + P], ident)
                    last.then_inc(ev("comb_mm"), 1)

            moe(0)
            pe.wait_ge(ev("comb"), 2 * NT)
            norm_sums(2)

            def gated_in(j):
                arrived(("od_in", j))
                w = w_view(("od_in", j)).rearrange("p (k a n) -> p k a n", k=KD, a=2)
                if j >= 1:
                    pe.wait_ge(ev("sig"), 2 * j)
                    pe.wait_ge(ev("u_w"), 2 * j)
                for a in (1, 0):
                    for k in range(KD):
                        if j == 0 and a == 1:
                            pe.wait_ge(ev("h_s"), 2 * KD + k + 1)
                            pe.wait_ge(ev("h_c"), 2 * KD + k + 1)
                        pe.matmul(PS[:, a, :], w[:, k, a, :], hT[:, k, 0:SAMPLE],
                                  start=(k == 0), stop=(k == KD - 1))
                        last = pe.matmul(PS[:, 2, a * CONTEXT:(a + 1) * CONTEXT], w[:, k, a, :], hT[:, k, SAMPLE:T],
                                         start=(k == 0), stop=(k == KD - 1))
                last.then_inc(ev("gate_mm"), 1)

            def taps(j):
                pe.wait_ge(ev("tap_d"), PE_TAPS * (j + 1))
                pe.wait_ge(ev("u_w"), 2 * (j + 1))
                if j == 0:
                    pe.wait_ge(ev("u_zero"), 1)
                else:
                    pe.wait_ge(ev("conv_a"), 2 * j)
                for w in range(PE_TAPS):
                    pe.matmul(PS[:, 4, :], tapd[:, j % 2, w, :], upad[:, j, w:w + 512],
                              start=(w == 0), stop=(w == PE_TAPS - 1))
                    last = pe.matmul(PS[:, 6, 0:SPAN - 512], tapd[:, j % 2, w, :], upad[:, j, w + 512:w + SPAN],
                                     start=(w == 0), stop=(w == PE_TAPS - 1))
                last.then_inc(ev("tap_mm"), 1)

            gated_in(0)
            for j in range(KD):
                if j + 1 < KD:
                    gated_in(j + 1)
                taps(j)
            pe.wait_ge(ev("sig"), 2 * KD)
            pe.wait_ge(ev("u_w"), 2 * KD)
            for src, name, b, done in ((cv, "conv_v", 0, "ln_sum"), (cv2, "ln_sq", 2, "ln_var")):
                for k in range(KD):
                    pe.wait_ge(ev(name), (2 if src is cv else 1) * (k + 1))
                    pe.matmul(PS[:, b, :], ones, src[:, k, 0:512], start=(k == 0), stop=(k == KD - 1))
                    last = pe.matmul(PS[:, b + 1, 0:SPAN - 512], ones, src[:, k, 512:SPAN],
                                     start=(k == 0), stop=(k == KD - 1))
                last.then_inc(ev(done), 1)
            project_out(1, "od_out", lambda k: cv[:, k, 0:SAMPLE], lambda k: cv[:, k, CTX0:SPAN])
            moe(1)
            pe.wait_ge(ev("comb"), 4 * NT)
            for i in range(2 * NT):
                t, half = i // 2, i % 2
                if i >= 4:
                    pe.wait_ge(ev(("fin_v", "fin_a")[i % 2]), (i - 4) // 2 + 1)
                for j in range(4):
                    last = pe.transpose(quad(4 + i % 4)[:, j, :], xT[:, 4 * half + j, t * P:t * P + P], ident)
                last.then_inc(ev("fin_t"), 1)

        @block.scalar
        def _(act):
            step = [0]

            def link(ins):
                step[0] += 1
                ins.then_inc(ev("act_step"), 1)
                act.wait_ge(ev("act_step"), step[0])

            n_param = [0]

            def param(dst, src):
                n_param[0] += 1
                act.dma_start(dst, src).then_inc(ev("params_in"), 16)

            param(cst[:, :], f["consts"])
            v = vrow
            for l in range(2):
                param(v[48 * l:48 * l + 48, 0, :], f["ada_b"][l].rearrange("(r n) -> r n", n=P))
            param(v[96:104, 0, :], f["c"][0].rearrange("(r n) -> r n", n=P))
            param(v[104:112, 0, :], f["c_ctx"].rearrange("(r n) -> r n", n=P))
            param(v[112:128, 0, :], f["norm_mix"].rearrange("l (r n) -> (l r) n", n=P))
            param(v[0:16, 1, :], f["norm_ffn"].rearrange("l (r n) -> (l r) n", n=P))
            param(v[16:24, 1, :], f["od_dw_b"][0].rearrange("(r n) -> r n", n=P))
            param(v[24:32, 1, :], f["od_ln_g"][0].rearrange("(r n) -> r n", n=P))
            param(v[32:40, 1, :], f["od_ln_b"][0].rearrange("(r n) -> r n", n=P))
            param(v[40:44, 1, :], f["ev_ret_gn"][0].rearrange("(r n) -> r n", n=P))
            param(v[44:46, 1, :], f["ev_q_a_norm"][0].rearrange("(r n) -> r n", n=P))
            dw = f["od_dw"][0].rearrange("w (r n) -> (w r) n", n=P)
            param(v[:, 2, :], dw[0:P, :])
            param(v[0:V_ROWS[3], 3, :], dw[P:, :])
            act.dma_start(xtok[:, 0:ST, :], f["x_sample"][0].rearrange("(t p) n -> p t n", p=P)).then_inc(ev("x_in0"), 16)
            act.dma_start(xtok[:, ST, :], f["x_prompt"][0]).then_inc(ev("x_in1"), 16)

            def late(dst, src):
                act.dma_start(dst, src).then_inc(ev("late_in"), 16)
            late(dist, f["distances"])
            late(dec[:, :], f["ev_ret_decay"][0].rearrange("d h -> (d h)").partition_broadcast(P))
            late(kvg[:, :], f["ev_kv_a_norm"][0].partition_broadcast(P))
            late(qkg[:, 0, :], f["ev_q_norm"][0].partition_broadcast(P))
            late(qkg[:, 1, :], f["ev_k_norm"][0].partition_broadcast(P))
            late(cache_in[:, 0:KVRANK], f["cache_mla_ckv"][0, 0])
            late(cache_in[:, KVRANK:], f["cache_mla_krope"][0, 0])
            for l in range(2):
                late(rb[:, l, 0:GROUPS], f["moe_b_group"][l].partition_broadcast(P))
                late(rb[:, l, GROUPS:], f["moe_b_expert"][l].partition_broadcast(P))

            def router_weights(l):
                act.dma_start(wr[:, :, 0:GROUPS], f["moe_w_group"][l].rearrange("(k p) n -> p k n", p=P)) \
                    .then_inc(ev("wr_in"), 16)
                act.dma_start(wr[:, :, GROUPS:], f["moe_w_expert"][l].rearrange("(k p) n -> p k n", p=P)) \
                    .then_inc(ev("wr_in"), 16)
            router_weights(0)

            act.wait_ge(ev("vec_c"), 4)
            act.activation(scT[:, :, :].rearrange("p k a -> p a k"),
                           vecT[:, 0, V_COND:V_COND + 16].rearrange("p (a k) -> p a k", a=2),
                           ACT.Silu).then_inc(ev("sc_ready"), 1)
            act.dma_start(rows_out[ROWS:XW, 0:C_ID + P], cst[0:BLK, C_ID:C_ID + P]).then_inc(ev("y_sent"), 16)
            for i in range(1, 2 * NT, 2):
                act.wait_ge(ev("x_t"), i + 1)
                act.activation(xT[:, 4:8, (i // 2) * P:(i // 2 + 1) * P], quad(i % 4), ACT.Copy).then_inc(ev("xt_a"), 1)

            def norm(q, ready):
                l = q // 2
                for k in range(KD):
                    ready(k)
                    act.activation(hT[:, k, :], xT[:, k, :], ACT.Square).then_inc(ev("squared"), 1)
                act.wait_ge(ev("sumsq"), q + 1)
                act.activation(rs[:, 0:SAMPLE], PS[:, 4, :], ACT.Sqrt, bias=eps, scale=1.0 / D).then_inc(ev("root"), 1)
                act.activation(rs[:, SAMPLE:T], PS[:, 6, 0:CONTEXT], ACT.Sqrt, bias=eps, scale=1.0 / D) \
                    .then_inc(ev("root"), 1)
                act.wait_ge(ev("coef"), q + 1)
                for k in range(KD):
                    act.wait_ge(ev("hn"), 2 * KD * q + 2 * k + 1)
                    act.activation(hT[:, k, 0:SAMPLE], hT[:, k, 0:SAMPLE], ACT.Identity,
                                   bias=modT[:, l, 24 * (q % 2) + k, 0:1], scale=modA[:, q, k, 0:1]) \
                        .then_inc(ev("h_s"), 1)

            def x_ready(k):
                if k == 0:
                    act.wait_ge(ev("xt_v"), NT)
                    act.wait_ge(ev("xt_a"), NT)
            norm(0, x_ready)
            for i in range(1, 8 * NT, 2):
                c, t = i // NT, i % NT
                n = min(256, EVEN_IN - 256 * c)
                act.wait_ge(ev("z_mm"), i + 1)
                act.activation(z[:, t, 256 * c:256 * c + n], PS[:, i % 4, 0:n], ACT.Copy).then_inc(ev("z_a"), 1)
            act.dma_start(states[0:RK, 0, :, :], f["state_retention"][0, 0, 0].rearrange("h k v -> k h v")) \
                .then_inc(ev("state_in"), 16)
            act.dma_start(states[RK:P, ST - 1, :, :], f["state_retention"][0, 0, 1].rearrange("h k v -> k h v")) \
                .then_inc(ev("state_in"), 16)
            act.wait_ge(ev("late_in"), 16 * 11)
            link(act.activation(decw[:, 0, :], dec[:, :], ACT.Abs))
            link(act.activation(decw[:, 1, :], decw[:, 0, :], ACT.Exp, scale=-1.0))
            act.activation(decw[:, 2, :], decw[:, 1, :], ACT.Ln, bias=1.0).then_inc(ev("ln_dec"), 1)
            act.wait_ge(ev("edge_arg"), 6)
            act.activation(edge[:, :, :], edge[:, :, :], ACT.Exp).then_inc(ev("edge_e"), 1)
            for h in range(RH):
                for d in range(2):
                    a = D_A1 if d == 0 else D_A2
                    act.activation(mtmp[:, 2 * h + d, :], dist[:, a:a + P], ACT.Exp,
                                   scale=dec[:, d * RH + h:d * RH + h + 1]).then_inc(ev("mask_e"), 1)
            act.wait_ge(ev("z_v"), 4 * NT)
            act.wait_ge(ev("z_a"), 4 * NT)
            act.wait_ge(ev("mask_v"), RH)
            for t in range(NT):
                act.activation(oret[:, t, :], oret[:, t, :], ACT.Silu).then_inc(ev("silu_g"), 1)
            for t in range(NT):
                link(act.activation(qksq[:, 0, 0:QRANK], z[:, t, 0:QRANK], ACT.Square, accum_out=ss[:, 0, t:t + 1]))
                link(act.activation(qksq[:, 0, 0:KVRANK], z[:, t, QRANK:Z_KR], ACT.Square,
                                    accum_out=ss[:, 0, 8 + t:9 + t]))
            act.activation(ss[:, 1, 0:NT], ss[:, 0, 0:NT], ACT.Sqrt, bias=eps, scale=1.0 / QRANK) \
                .then_inc(ev("lat_root"), 1)
            act.activation(ss[:, 1, 8:8 + NT], ss[:, 0, 8:8 + NT], ACT.Sqrt, bias=eps, scale=1.0 / KVRANK) \
                .then_inc(ev("lat_root"), 1)
            for t in range(NT):
                act.wait_ge(ev("rq_t"), t + 1)
                if t >= 1:
                    act.wait_ge(ev("rs_mm"), t)
                act.activation(rqT, quad(0)[0:RK], ACT.Copy).then_inc(ev("rq_c"), 1)
                if t < ST:
                    act.wait_ge(ev("qfb_t"), t + 1)
                    if t >= 1:
                        act.wait_ge(ev("ro_mm"), t)
                    act.activation(qfbT, quad(2), ACT.Copy).then_inc(ev("qfb_c"), 1)
                act.wait_ge(ev("gn_v"), t + 1)
                act.activation(rmv[:, :], mv[:, :, 1], ACT.Sqrt, bias=eps).then_inc(ev("gn_root"), 1)
            for u, (kind, t) in enumerate(UNITS):
                raw = qkraw[:, u % 2, :].rearrange("p (h n) -> p h n", h=HEADS)
                act.wait_ge(ev("qk_mm"), u + 1)
                if u >= 2:
                    act.wait_ge(ev("hd_t"), u - 1)
                b = 2 * (u % 2)
                for half in range(2):
                    if kind == "q":
                        ins = act.activation(raw[:, 4 * half:4 * half + 4, :],
                                             PS[:, b + half, 0:384].rearrange("p (h n) -> p h n", h=4), ACT.Copy)
                    else:
                        ins = act.activation(raw[:, 4 * half:4 * half + 4, 0:NOPE],
                                             quad(b + half)[:, :, 0:NOPE], ACT.Copy)
                    if half == 0:
                        link(ins)
                ins.then_inc(ev("raw_a"), 1)
                act.wait_ge(ev("raw_a"), u + 1)
                if kind == "k":
                    act.wait_ge(ev("kr_p"), t + 1)
                if u >= 1:
                    act.wait_ge(ev("hsum"), u)
                act.activation(qksq[:, 0, :], qkraw[:, u % 2, :], ACT.Square).then_inc(ev("qk_sq"), 1)
                act.wait_ge(ev("hsum"), u + 1)
                act.activation(ss[:, 1, 0:HEADS], ss[:, 0, 0:HEADS], ACT.Sqrt, bias=eps, scale=1.0 / QK) \
                    .then_inc(ev("hroot"), 1)
                if u >= 1:
                    k2, t2 = UNITS[u - 1]
                    col = t2 * P if k2 == "q" else KCOL[t2]
                    dst = qT if k2 == "q" else kT
                    act.wait_ge(ev("hd_t"), u)
                    if u == 2:
                        act.wait_ge(ev("side_out"), 48)
                    act.activation(dst[:, 0:4, col:col + P], quad(4)[0:QK], ACT.Copy).then_inc(ev("hd_a"), 1)
            act.wait_ge(ev("hd_t"), len(UNITS))
            act.activation(kT[:, 0:4, KCOL[NT]:KCOL[NT] + P], quad(4)[0:QK], ACT.Copy).then_inc(ev("hd_a"), 1)
            for i in range(NATT + 1):
                if i < NATT:
                    t, h = ATT[i]
                    n = ST + 1 if t < ST else 1
                    act.wait_ge(ev("nmax"), i + 1)
                    if i >= 2:
                        act.wait_ge(ev("p_t"), i - 1)
                        act.wait_ge(ev("o_c"), i - 1)
                    act.activation(prob[i % 2][:, 0:n, :],
                                   PSf[:, 1024 * (i % 2):1024 * (i % 2) + n * P].rearrange("p (j n) -> p j n", n=P),
                                   ACT.Exp, bias=nmx[:, i % 2:i % 2 + 1], accum_out=den[:, i % 2:i % 2 + 1]) \
                        .then_inc(ev("prob"), 1)
                if i >= 1:
                    t, h = ATT[i - 1]
                    n = 4 if t < ST else 1
                    act.wait_ge(ev("p_t"), i)
                    if i >= 3:
                        act.wait_ge(ev("pv_mm"), i - 2)
                    act.activation(probT[(i - 1) % 2][:, 0:n, :], quad(4)[:, 0:n, :], ACT.Copy).then_inc(ev("pt_a"), 1)
            for t in range(NT):
                act.wait_ge(ev("o_t"), 2 * t + 1)
                act.activation(oT[:, 0:4, t * P:t * P + P], quad((2 * t) % 4), ACT.Copy).then_inc(ev("ot_a"), 1)

            def moe(l):
                q = 2 * l + 1
                norm(q, lambda k: act.wait_ge(ev("wo_ev"), KD * l + k + 1))
                act.wait_ge(ev("gdiff"), l + 1)
                act.activation(rt[:, 0, :, 0:GROUPS], rt[:, 0, :, 0:GROUPS], ACT.Exp).then_inc(ev("gexp"), 1)
                for i in range(2 * NT):
                    t, half = i // 2, i % 2
                    act.wait_ge(ev("htok_t"), 2 * NT * l + i + 1)
                    act.activation(htok[:, t, 512 * half:512 * half + 512], PS[:, (1, 2, 3, 7)[i % 4], :], ACT.Copy) \
                        .then_inc(ev("htok_a"), 1)
                    if i == 3:
                        act.wait_ge(ev("ediff"), l + 1)
                        act.activation(r1[:, 4, :], r1[:, 4, :], ACT.Exp).then_inc(ev("eexp"), 1)
                act.wait_ge(ev("rows_sent"), 16 * 2 * NT * (l + 1))
                for j in range(RT // 2):
                    act.dma_start(xback[:, 2 * j:2 * j + 2, :],
                                  rows_in[2 * j * P:(2 * j + 2) * P, :].rearrange("(j p) n -> p j n", p=P)) \
                        .then_inc(ev(f"rows_back{j}"), 16)
                for i in range(1, 2 * RT, 2):
                    j = i // 2
                    act.wait_ge(ev("xs_t"), 2 * RT * l + i + 1)
                    act.activation(xsT[:, 4:8, j * P:(j + 1) * P], quad(i % 4), ACT.Copy).then_inc(ev("xs_a"), 1)
                act.wait_ge(ev("tab"), 4 * l + 4)

                with act.Fori(0, EXPERTS) as e:
                    off = act.value_load(tab[0:1, bass.ds(e, 1)], min_val=0, max_val=ROWS)
                    blocks = act.value_load(tab[0:1, bass.ds(e + EXPERTS, 1)], min_val=1, max_val=MAXBLK)
                    before = act.value_load(tab[0:1, bass.ds(e + 2 * EXPERTS, 1)], min_val=0, max_val=2 * ALLBLK)
                    with act.Fori(0, blocks) as b:
                        act.wait_ge(ev("up_mm"), before + b + 2)
                        act.wait_ge(ev("act"), before + b + 1)
                        act.activation(gsil[:, :], PS[:, 0, 0:P], ACT.Silu).then_inc(ev("silu"), 1)
                        act.wait_ge(ev("down_mm"), before + b + 2)
                        act.wait_ge(ev("y_sent"), (before + b) * 32 + 16)
                        act.activation(yblk[:, :], PS[:, 2, :], ACT.Copy).then_inc(ev("yblk_c"), 1)
                        row = act.snap(nc.s_assert_within(
                            off + b * BLK, 0, ROWS,
                            skip_runtime_bounds_check_because="a further block starts inside the expert's rows"))
                        act.wait_ge(ev("yblk_c"), before + b + 2)
                        for c in range(2):
                            act.dma_start(rows_out[bass.ds(row, BLK), c * 512:(c + 1) * 512],
                                          yblk[c * BLK:(c + 1) * BLK, :]).then_inc(ev("y_sent"), 16)
                    act.activation(tick[:, 0:1], eps, ACT.Copy).then_inc(ev("expert_done"), 1)
                total = act.value_load(tab[0:1, 3 * EXPERTS:3 * EXPERTS + 1], min_val=EXPERTS, max_val=2 * ALLBLK)
                act.wait_ge(ev("y_sent"), total * 32 + 16)
                act.activation(tick[:, 2:3], eps, ACT.Copy).then_inc(ev("results_sent"), 1)
                for t in range(NT):
                    act.wait_ge(ev(f"picked{t}"), 32 * (l + 1))
                    act.activation(ygat[:, t, :], ygat[:, t, :], ACT.Copy, scale=wtok[:, 0, t:t + 1]) \
                        .then_inc(ev("y0_w"), 1)
                if l == 0:
                    act.wait_ge(ev("route_mm"), 1)
                    router_weights(1)

            moe(0)
            norm(2, lambda k: act.wait_ge(ev("comb"), 2 * NT))
            for j in range(KD):
                act.wait_ge(ev("gate_mm"), j + 1)
                if j >= 1:
                    act.wait_ge(ev("u_w"), 2 * j)
                act.activation(rs[:, 0:SAMPLE], PS[:, 1, :], ACT.Sigmoid).then_inc(ev("sig"), 1)
                act.activation(rs[:, SAMPLE:T], PS[:, 2, CONTEXT:2 * CONTEXT], ACT.Sigmoid).then_inc(ev("sig"), 1)
                act.wait_ge(ev("tap_mm"), j + 1)
                dwb = vecT[:, 1, V_DWB + j:V_DWB + j + 1]
                act.activation(cv[:, j, 0:512], PS[:, 4, :], ACT.Identity, bias=dwb).then_inc(ev("conv_a"), 1)
                act.activation(cv[:, j, 512:SPAN], PS[:, 6, 0:SPAN - 512], ACT.Identity, bias=dwb) \
                    .then_inc(ev("conv_a"), 1)
            for k in range(KD):
                act.wait_ge(ev("ln_d"), 2 * (k + 1))
                act.activation(cv2[:, k, :], cv[:, k, :], ACT.Square).then_inc(ev("ln_sq"), 1)
            act.wait_ge(ev("ln_var"), 1)
            act.activation(rs[:, 0:512], PS[:, 2, :], ACT.Sqrt, bias=eps, scale=1.0 / CONV).then_inc(ev("ln_root"), 1)
            act.activation(cache_cT[:, :], PS[:, 3, CTX0 - 512:SPAN - 512], ACT.Sqrt, bias=eps, scale=1.0 / CONV) \
                .then_inc(ev("ln_root"), 1)
            for k in range(KD):
                act.wait_ge(ev("ln_n"), 2 * (k + 1))
                for c0, c1 in ((0, SAMPLE), (CTX0, SPAN)):
                    ins = act.activation(cv[:, k, c0:c1], cv[:, k, c0:c1], ACT.Silu,
                                         bias=vecT[:, 1, V_LNB + k:V_LNB + k + 1],
                                         scale=vecT[:, 1, V_LNG + k:V_LNG + k + 1])
                ins.then_inc(ev("act1"), 1)
            moe(1)
            for i in range(1, 2 * NT, 2):
                t = i // 2
                act.wait_ge(ev("fin_t"), i + 1)
                act.activation(xtok[:, t, 512:D], PS[:, 4 + i % 4, :], ACT.Copy).then_inc(ev("fin_a"), 1)

        @block.vector
        def _(dve):
            step = [0]

            def link(ins):
                step[0] += 1
                ins.then_inc(ev("dve_step"), 1)
                dve.wait_ge(ev("dve_step"), step[0])

            def tt(out, a, b, op):
                return dve.tensor_tensor(out, a, b, op)

            dve.wait_ge(ev("vec_t"), 1)
            for g, r in enumerate(V_ROWS):
                dve.tensor_copy(vecT[:, g, 0:r], PS[:, 5, g * P:g * P + r]).then_inc(ev("vec_c"), 1)
            for i in range(0, 2 * NT, 2):
                dve.wait_ge(ev("x_t"), i + 1)
                dve.tensor_copy(xT[:, 0:4, (i // 2) * P:(i // 2 + 1) * P], quad(i % 4)).then_inc(ev("xt_v"), 1)

            def evac_mod(l, m0, m1, b, count):
                dve.wait_ge(ev("mod_mm"), count)
                dve.wait_ge(ev("vec_c"), 4)
                n = m1 - m0
                bias = vecT[:, 0, 48 * l + m0:48 * l + m1].unsqueeze(2)
                tt(modT[:, l, m0:m1, :], PS[:, b, 0:2 * n].rearrange("p (m a) -> p m a", a=2),
                   bc(bias, [P, n, 2]), ALU.add).then_inc(ev("mod_c"), 1)

            def coef(q):
                l = q // 2
                base = (V_NMIX if q % 2 == 0 else V_NFFN) + 8 * l
                g = vecT[:, q % 2, base:base + KD].unsqueeze(2)
                s = 24 * (q % 2) + 8
                dve.scalar_tensor_tensor(out=modA[:, q, :, :], in0=modT[:, l, s:s + KD, :], scalar=1.0,
                                         in1=bc(g, [P, KD, 2]), op0=ALU.add, op1=ALU.mult).then_inc(ev("coef"), 1)

            def normed(q):
                dve.wait_ge(ev("root"), 2 * q + 2)
                link(dve.reciprocal(PS[:, 4, :], rs[:, 0:SAMPLE]))
                link(dve.reciprocal(PS[:, 6, 0:CONTEXT], rs[:, SAMPLE:T]))
                for k in range(KD):
                    tt(hT[:, k, 0:SAMPLE], xT[:, k, 0:SAMPLE], PS[:, 4, :], ALU.mult).then_inc(ev("hn"), 1)
                    tt(hT[:, k, SAMPLE:T], xT[:, k, SAMPLE:T], PS[:, 6, 0:CONTEXT], ALU.mult).then_inc(ev("hn"), 1)

            dve.wait_ge(ev("xt_a"), NT)
            dve.wait_ge(ev("xt_v"), NT)
            normed(0)
            evac_mod(0, 0, 16, 7, 8)
            dve.wait_ge(ev("mod_c"), 1)
            coef(0)
            for i in range(0, 8 * NT, 2):
                c, t = i // NT, i % NT
                n = min(256, EVEN_IN - 256 * c)
                dve.wait_ge(ev("z_mm"), i + 1)
                dve.tensor_copy(z[:, t, 256 * c:256 * c + n], PS[:, i % 4, 0:n]).then_inc(ev("z_v"), 1)
            evac_mod(0, 16, 48, 5, 24)
            dve.wait_ge(ev("mod_c"), 2)
            coef(1)
            dve.wait_ge(ev("ln_dec"), 1)
            link(dve.scalar_tensor_tensor(out=dec[:, :], in0=dec[:, :], scalar=0.0, in1=decw[:, 2, :],
                                          op0=ALU.min, op1=ALU.subtract))
            for n, d in enumerate((0, 0, 1, 1)):
                dve.tensor_scalar(edge[:, n, :], dec[:, d * RH:(d + 1) * RH], cst[:, C_POS + n:C_POS + n + 1], None,
                                  ALU.mult).then_inc(ev("edge_arg"), 1)
            for d in range(2):
                dve.tensor_scalar(edge[:, 4 + d, :], dec[:, d * RH:(d + 1) * RH], float(P), None, ALU.mult) \
                    .then_inc(ev("edge_arg"), 1)
            dve.wait_ge(ev("edge_e"), 1)
            link(dve.tensor_scalar(edge[:, 0, :], edge[:, 0, :], RK ** -0.5, None, ALU.mult))
            link(dve.tensor_scalar(edge[:, 2, :], edge[:, 2, :], RK ** -0.5, None, ALU.mult))
            for h in range(RH):
                dve.wait_ge(ev("mask_e"), 2 * h + 2)
                link(tt(mtmp[:, 2 * h, :], mtmp[:, 2 * h, :], dist[:, D_U:D_U + P], ALU.mult))
                link(tt(mtmp[:, 2 * h + 1, :], mtmp[:, 2 * h + 1, :], dist[:, D_L:D_L + P], ALU.mult))
                link(tt(mtmp[:, 2 * h, :], mtmp[:, 2 * h, :], mtmp[:, 2 * h + 1, :], ALU.add))
                dve.tensor_scalar(mask[:, h, :], mtmp[:, 2 * h, :], RK ** -0.5, None, ALU.mult).then_inc(ev("mask_v"), 1)
            dve.wait_ge(ev("z_a"), 4 * NT)
            dve.wait_ge(ev("z_v"), 4 * NT)

            def by_edge(out, t, off, n):
                src = z[:, t, off:off + RH * RK].rearrange("p (h n) -> p h n", h=RH)
                return tt(out, src, bc(edge[:, n, :].unsqueeze(2), [P, RH, RK]), ALU.mult)

            def state_row(t):
                if t == 0:
                    dve.wait_ge(ev("state_in"), 32)
            for t in range(NT):
                if t >= 1:
                    dve.wait_ge(ev("upd_mm"), t)
                link(by_edge(kfb[:, :, 0:RK], t, Z_RK, 0))
                by_edge(kfb[:, :, RK:P], t, Z_RK, 2).then_inc(ev("kfb"), 1)
                dve.wait_ge(ev("upd_mm"), t + 1)
                dve.tensor_copy(upd[:, t, :, :], quad(t % 2)).then_inc(ev("upd_c"), 1)
            dve.wait_ge(ev("state_in"), 32)
            dve.wait_ge(ev("upd_c"), NT)
            for j in range(ST - 1):
                for h in range(RH):
                    ins = dve.scalar_tensor_tensor(
                        out=states[0:RK, j + 1, h, :], in0=states[0:RK, j, h, :], scalar=edge[0:RK, 4, h:h + 1],
                        in1=upd[0:RK, j, h, :], op0=ALU.mult, op1=ALU.add)
                ins.then_inc(ev("state_f"), 1)
                r = ST - 1 - j
                for h in range(RH):
                    ins = dve.scalar_tensor_tensor(
                        out=states[RK:P, r - 1, h, :], in0=states[RK:P, r, h, :], scalar=edge[RK:P, 5, h:h + 1],
                        in1=upd[RK:P, r, h, :], op0=ALU.mult, op1=ALU.add)
                ins.then_inc(ev("state_b"), 1)
                dve.wait_ge(ev("state_f"), j + 1)
                dve.wait_ge(ev("state_b"), j + 1)
            dve.wait_ge(ev("mask_v"), RH)
            for t in range(NT):
                if t < ST:
                    if t >= 1:
                        dve.wait_ge(ev("qfb_t"), t)
                    link(by_edge(qfb[:, :, 0:RK], t, Z_RQ, 1))
                    by_edge(qfb[:, :, RK:P], t, Z_RQ, 3).then_inc(ev("qfb"), 1)
                dve.wait_ge(ev("rk_t"), t + 1)
                if t >= 1:
                    dve.wait_ge(ev("rs_mm"), t)
                dve.tensor_copy(rkT, quad(1)[0:RK]).then_inc(ev("rk_c"), 1)
                dve.wait_ge(ev("rs_mm"), t + 1)
                if t >= 1:
                    dve.wait_ge(ev("ro_mm"), t)
                tt(rsc, quad(3), mask[:, :, :], ALU.mult).then_inc(ev("rsc"), 1)
                dve.wait_ge(ev("ro_mm"), t + 1)
                for h in range(RH):
                    link(dve.bn_stats(stat[:, h, :], quad(4)[:, h, :]))
                for h in range(RH):
                    ins = dve.bn_aggr(mv[:, h, :], stat[:, h, :])
                ins.then_inc(ev("gn_v"), 1)
                dve.wait_ge(ev("gn_root"), t + 1)
                link(dve.reciprocal(mv[:, :, 1], rmv[:, :]))
                for h in range(RH):
                    ins = dve.tensor_scalar(onrm[:, h, :], quad(4)[:, h, :], mv[:, h, 0:1], mv[:, h, 1:2],
                                            ALU.subtract, ALU.mult)
                ins.then_inc(ev("onrm"), 1)
                dve.wait_ge(ev("onrm"), t + 1)
                dve.wait_ge(ev("silu_g"), t + 1)
                tt(oret[:, t, :], oret[:, t, :], arena[:, A_V + 1536:A_V + 2048], ALU.mult).then_inc(ev("gated"), 1)
                dve.wait_ge(ev("gated"), t + 1)
            dve.wait_ge(ev("lat_root"), 2)
            link(dve.reciprocal(ss[:, 1, 0:NT], ss[:, 1, 0:NT]))
            link(dve.reciprocal(ss[:, 1, 8:8 + NT], ss[:, 1, 8:8 + NT]))
            for t in range(NT):
                dve.tensor_scalar(z[:, t, 0:QRANK], z[:, t, 0:QRANK], ss[:, 1, t:t + 1], None, ALU.mult)
                dve.scalar_tensor_tensor(out=z[:, t, QRANK:Z_KR], in0=z[:, t, QRANK:Z_KR],
                                         scalar=ss[:, 1, 8 + t:9 + t], in1=kvg[:, :],
                                         op0=ALU.mult, op1=ALU.mult).then_inc(ev("lat_n"), 1)
            link(dve.tensor_scalar(qkg[:, 0, :], qkg[:, 0, :], QK ** -0.5, None, ALU.mult))
            tt(tick[:, 0:1], cst[:, 0:1], cst[:, 0:1], ALU.mult).then_inc(ev("qkg_s"), 1)
            for t in range(NT + 1):
                dve.wait_ge(ev("lat_t"), t + 1)
                b = 5 + t % 2
                if t < NT:
                    for j in range(2):
                        dve.tensor_scalar(cT[:, t, j, :], quad(b)[:, j, :], vecT[:, 1, V_QA + j:V_QA + j + 1], None,
                                          ALU.mult)
                    dve.tensor_copy(cT[:, t, 2, :], quad(b)[:, 2, :]).then_inc(ev("lat_c"), 1)
                else:
                    dve.tensor_copy(cache_cT[:, :], quad(b)[:, 0, :]).then_inc(ev("lat_c"), 1)
            for u, (kind, t) in enumerate(UNITS):
                raw = qkraw[:, u % 2, :].rearrange("p (h n) -> p h n", h=HEADS)
                b = 2 * (u % 2)
                if kind == "k":
                    dve.wait_ge(ev("raw_a"), u + 1)
                    for half in range(2):
                        ins = dve.tensor_copy(vS[:, VROW[t], 4 * half:4 * half + 4, :],
                                              quad(b + half)[:, :, NOPE:NOPE + VD])
                    ins.then_inc(ev("v_c"), 1)
                dve.wait_ge(ev("qk_sq"), u + 1)
                dve.tensor_reduce(ss[:, 0, 0:HEADS], qksq[:, 0, :].rearrange("p (h n) -> p h n", h=HEADS), AX.X,
                                  ALU.add).then_inc(ev("hsum"), 1)
                dve.wait_ge(ev("hroot"), u + 1)
                link(dve.reciprocal(ss[:, 0, 8:16], ss[:, 1, 0:HEADS]))
                tt(raw, raw, bc(ss[:, 0, 8:16].unsqueeze(2), [P, HEADS, QK]), ALU.mult).then_inc(ev("qk_r"), 1)
                if u >= 1:
                    k2, t2 = UNITS[u - 1]
                    col = t2 * P if k2 == "q" else KCOL[t2]
                    dst = qT if k2 == "q" else kT
                    dve.wait_ge(ev("hd_t"), u)
                    if u == 2:
                        dve.wait_ge(ev("side_out"), 48)
                    dve.tensor_copy(dst[:, 4:8, col:col + P], quad(5)[0:QK]).then_inc(ev("hd_v"), 1)
            dve.wait_ge(ev("hd_t"), len(UNITS))
            dve.tensor_copy(kT[:, 4:8, KCOL[NT]:KCOL[NT] + P], quad(5)[0:QK]).then_inc(ev("hd_v"), 1)
            evac_mod(1, 0, 48, 7, 48)
            dve.wait_ge(ev("mod_c"), 3)
            coef(2)
            coef(3)
            for i in range(NATT + 2):
                if i < NATT:
                    t, h = ATT[i]
                    n = ST + 1 if t < ST else 1
                    dve.wait_ge(ev("s_mm"), i + 1)
                    if i >= 2:
                        dve.wait_ge(ev("prob"), i - 1)
                    dve.tensor_reduce(nmx[:, i % 2:i % 2 + 1], PSf[:, 1024 * (i % 2):1024 * (i % 2) + n * P], AX.X,
                                      ALU.max, negate=True).then_inc(ev("nmax"), 1)
                if 1 <= i <= NATT and ATT[i - 1][0] < ST:
                    dve.wait_ge(ev("p_t"), i)
                    if i >= 3:
                        dve.wait_ge(ev("pv_mm"), i - 2)
                    dve.tensor_copy(probT[(i - 1) % 2][:, 4, :], quad(5)[:, 0, :]).then_inc(ev("pt_v"), 1)
                if i >= 2:
                    t, h = ATT[i - 2]
                    link(dve.reciprocal(rden[:, i % 2:i % 2 + 1], den[:, i % 2:i % 2 + 1]))
                    dve.wait_ge(ev("pv_mm"), i - 1)
                    dve.tensor_scalar(omla[:, t, h * VD:(h + 1) * VD], PS[:, 6 + i % 2, 0:VD],
                                      rden[:, i % 2:i % 2 + 1], None, ALU.mult).then_inc(ev("o_c"), 1)
            for t in range(NT):
                dve.wait_ge(ev("o_t"), 2 * t + 2)
                for j in range(4):
                    ins = dve.tensor_scalar(oT[:, 4 + j, t * P:t * P + P], quad((2 * t + 1) % 4)[:, j, :],
                                            vecT[:, 1, V_GN + j:V_GN + j + 1], None, ALU.mult)
                ins.then_inc(ev("ot_v"), 1)

            def add_out(l):
                for m in range(KD):
                    dve.wait_ge(ev("wo_mm"), KD * l + m + 1)
                    b = 4 + 2 * (m % 2)
                    dve.scalar_tensor_tensor(out=xT[:, m, 0:SAMPLE], in0=PS[:, b, :], scalar=modT[:, l, 16 + m, 0:1],
                                             in1=xT[:, m, 0:SAMPLE], op0=ALU.mult, op1=ALU.add)
                    dve.scalar_tensor_tensor(out=xT[:, m, SAMPLE:T], in0=PS[:, b + 1, 0:CONTEXT],
                                             scalar=modT[:, l, 16 + m, 1:2], in1=xT[:, m, SAMPLE:T],
                                             op0=ALU.mult, op1=ALU.add).then_inc(ev("wo_ev"), 1)
            add_out(0)

            def moe(l):
                q = 2 * l + 1
                dve.wait_ge(ev("wo_ev"), KD * l + KD)
                normed(q)
                dve.wait_ge(ev("route_mm"), l + 1)
                link(tt(lgt[:, :, :], PS[:, 0, 0:NT * ROUTE].rearrange("p (t n) -> p t n", t=NT),
                        bc(rb[:, l, :].unsqueeze(1), [P, NT, ROUTE]), ALU.add))
                lg = lgt[:, :, 0:GROUPS]
                le = lgt[:, :, GROUPS:ROUTE]
                g4 = [P, NT, GROUPS]
                g8 = [P, NT, PER]
                g48 = [P, NT, GROUPS, PER]

                def w4(i):
                    return rt[:, i, :, 0:GROUPS]

                def w8(i):
                    return rt[:, i, :, :]

                def col(i, n):
                    return bc(r1[:, i, :].unsqueeze(2), [P, NT, n])

                link(dve.tensor_reduce(r1[:, 0, :], lg, AX.X, ALU.max))
                tt(w4(0), lg, col(0, GROUPS), ALU.subtract).then_inc(ev("gdiff"), 1)
                link(tt(w4(1), lg, col(0, GROUPS), ALU.is_equal))
                link(tt(w4(1), w4(1), bc(cst[:, C_PRI4:C_PRI4 + GROUPS].unsqueeze(1), g4), ALU.mult))
                link(dve.tensor_reduce(r1[:, 1, :], w4(1), AX.X, ALU.max))
                link(tt(w4(2), w4(1), col(1, GROUPS), ALU.is_equal))
                b48 = both[:, :, :].rearrange("p t (g e) -> p t g e", g=GROUPS)
                for t in range(NT):
                    ins = tt(b48[:, t], le[:, t].rearrange("p (g e) -> p g e", g=GROUPS),
                             bc(w4(2)[:, t].unsqueeze(2), [P, GROUPS, PER]), ALU.mult)
                link(ins)
                link(dve.tensor_reduce(w8(3), b48.rearrange("p t g e -> p t e g"), AX.X, ALU.add))
                for src, mx, eq, hot in ((3, 2, 4, 5), (6, 3, 7, 8)):
                    link(dve.tensor_reduce(r1[:, mx, :], w8(src), AX.X, ALU.max))
                    link(tt(w8(eq), w8(src), col(mx, PER), ALU.is_equal))
                    link(tt(w8(eq), w8(eq), bc(cst[:, C_PRI8:C_PRI8 + PER].unsqueeze(1), g8), ALU.mult))
                    link(dve.tensor_reduce(r1[:, 5, :], w8(eq), AX.X, ALU.max))
                    link(tt(w8(hot), w8(eq), col(5, PER), ALU.is_equal))
                    if src == 3:
                        link(dve.scalar_tensor_tensor(out=w8(6), in0=w8(5), scalar=-3.0e38, in1=w8(3),
                                                      op0=ALU.mult, op1=ALU.add))
                tt(r1[:, 4, :], r1[:, 3, :], r1[:, 2, :], ALU.subtract).then_inc(ev("ediff"), 1)
                for c in range(2):
                    o48 = one32[:, c, :, :].rearrange("p t (g e) -> p t g e", g=GROUPS)
                    for t in range(NT):
                        ins = tt(o48[:, t], bc(w4(2)[:, t].unsqueeze(2), [P, GROUPS, PER]),
                                 bc(w8(5 + 3 * c)[:, t].unsqueeze(1), [P, GROUPS, PER]), ALU.mult)
                    link(ins)
                tt(both[:, :, :], one32[:, 0, :, :], one32[:, 1, :, :], ALU.add).then_inc(ev("chosen"), 1)
                dve.wait_ge(ev("gexp"), l + 1)
                link(dve.tensor_reduce(r1[:, 6, :], w4(0), AX.X, ALU.add))
                link(dve.reciprocal(r1[:, 7, :], r1[:, 6, :]))
                dve.wait_ge(ev("eexp"), l + 1)
                link(dve.tensor_scalar(r1[:, 8, :], r1[:, 4, :], 1.0, None, ALU.add))
                link(dve.reciprocal(r1[:, 9, :], r1[:, 8, :]))
                link(tt(wtok[:, 0, :], r1[:, 9, :], r1[:, 7, :], ALU.mult))
                tt(wtok[:, 1, :], wtok[:, 0, :], r1[:, 4, :], ALU.mult).then_inc(ev("wtok"), 1)
                dve.wait_ge(ev("rank_mm"), l + 1)
                one = cst[:, C_ONE:C_ONE + EXPERTS]
                link(dve.tensor_copy(cnt[:, 0, :], PS[:, 6, 0:EXPERTS]))
                link(dve.tensor_tensor_scan(cnt[:, 1, :], one, cnt[:, 0, :], 0.0, ALU.mult, ALU.add))
                link(tt(cnt[:, 1, :], cnt[:, 1, :], cnt[:, 0, :], ALU.subtract))
                link(tt(slotpos[:, :, :], PS[:, 5, 0:NT * EXPERTS].rearrange("p (t n) -> p t n", t=NT),
                        bc(cnt[:, 1, :].unsqueeze(1), [P, NT, EXPERTS]), ALU.add))
                for c in range(2):
                    link(tt(one32[:, c, :, :], one32[:, c, :, :], slotpos[:, :, :], ALU.mult))
                    link(dve.tensor_reduce(posf[:, c, :], one32[:, c, :, :], AX.X, ALU.add))
                dve.tensor_copy(posu[:, :], posf[:, :, :].rearrange("p c t -> p (c t)")).then_inc(ev("pos"), 1)
                link(tt(cmpt[:, :, :], bc(cnt[:, 0, :].unsqueeze(2), [P, EXPERTS, MAXBLK - 1]),
                        bc(cst[:, C_THR:C_THR + MAXBLK - 1].unsqueeze(1), [P, EXPERTS, MAXBLK - 1]), ALU.is_gt))
                link(dve.tensor_reduce(cnt[:, 2, :], cmpt[:, :, :], AX.X, ALU.add))
                link(dve.tensor_scalar(cnt[:, 2, :], cnt[:, 2, :], 1.0, None, ALU.add))
                link(dve.tensor_tensor_scan(cnt[:, 3, :], one, cnt[:, 2, :], 0.0, ALU.mult, ALU.add))
                link(tt(cnt[:, 3, :], cnt[:, 3, :], cnt[:, 2, :], ALU.subtract))
                if l == 0:
                    link(tt(blocks0[:, :], cnt[:, 3, EXPERTS - 1:EXPERTS], cnt[:, 2, EXPERTS - 1:EXPERTS], ALU.add))
                else:
                    link(dve.tensor_scalar(cnt[:, 3, :], cnt[:, 3, :], blocks0[:, 0:1], None, ALU.add))
                tt(tab[0:1, 3 * EXPERTS:], cnt[0:1, 3, EXPERTS - 1:EXPERTS], cnt[0:1, 2, EXPERTS - 1:EXPERTS],
                   ALU.add).then_inc(ev("tab"), 1)
                for n in range(3):
                    dve.tensor_copy(tab[0:1, n * EXPERTS:(n + 1) * EXPERTS], cnt[0:1, n + 1, :]).then_inc(ev("tab"), 1)
                for i in range(0, 2 * RT, 2):
                    j = i // 2
                    dve.wait_ge(ev("xs_t"), 2 * RT * l + i + 1)
                    dve.tensor_copy(xsT[:, 0:4, j * P:(j + 1) * P], quad(i % 4)).then_inc(ev("xs_v"), 1)
                dve.wait_ge(ev("tab"), 4 * l + 4)
                if l == 0:
                    for name in ("act", "up_mm", "h_t", "down_mm", "yblk_c"):
                        dve.memset(tick[:, 1:2], 0.0).then_inc(ev(name), 1)
                        dve.wait_ge(ev(name), 1)
                with dve.Fori(0, EXPERTS) as e:
                    blocks = dve.value_load(tab[0:1, bass.ds(e + EXPERTS, 1)], min_val=1, max_val=MAXBLK)
                    before = dve.value_load(tab[0:1, bass.ds(e + 2 * EXPERTS, 1)], min_val=0, max_val=2 * ALLBLK)
                    with dve.Fori(0, blocks) as b:
                        dve.wait_ge(ev("silu"), before + b + 1)
                        dve.wait_ge(ev("h_t"), before + b + 1)
                        tt(gact[:, :], gsil[:, :], PS[:, 0, P:2 * P], ALU.mult).then_inc(ev("act"), 1)
                        dve.wait_ge(ev("h_t"), before + b + 2)
                        dve.wait_ge(ev("down_mm"), before + b + 1)
                        dve.tensor_copy(hblk[:, :, :], PS[:, 1, 0:P].rearrange("p (i n) -> p i n", i=2)) \
                            .then_inc(ev("hblk_c"), 1)
                for t in range(NT):
                    dve.wait_ge(ev("y0_w"), NT * l + t + 1)
                    dve.scalar_tensor_tensor(out=ygat[:, t, :], in0=ygat[:, NT + t, :], scalar=wtok[:, 1, t:t + 1],
                                             in1=ygat[:, t, :], op0=ALU.mult, op1=ALU.add).then_inc(ev("comb_v"), 1)
                for i in range(2 * NT):
                    t, half = i // 2, i % 2
                    dve.wait_ge(ev("comb_mm"), 2 * NT * l + i + 1)
                    for m in range(4):
                        k = 4 * half + m
                        c = 0 if t < ST else 1
                        ins = dve.scalar_tensor_tensor(
                            out=xT[:, k, t * P:t * P + P], in0=quad(4 + i % 4)[:, m, :], scalar=modT[:, l, 40 + k, c:c + 1],
                            in1=xT[:, k, t * P:t * P + P], op0=ALU.mult, op1=ALU.add)
                    ins.then_inc(ev("comb"), 1)

            moe(0)
            dve.wait_ge(ev("comb"), 2 * NT)
            normed(2)

            def gated_u(j):
                for n in range(2):
                    dve.wait_ge(ev("sig"), 2 * j + n + 1)
                    if n == 0:
                        ins = tt(upad[:, j, HALO:HALO + SAMPLE], rs[:, 0:SAMPLE], PS[:, 0, :], ALU.mult)
                    else:
                        ins = tt(upad[:, j, HALO + CTX0:HALO + CTX0 + CONTEXT], rs[:, SAMPLE:T], PS[:, 2, 0:CONTEXT],
                                 ALU.mult)
                    ins.then_inc(ev("u_w"), 1)

            for j in range(KD):
                gated_u(j)
                if j == 0:
                    dve.wait_ge(ev("u_zero"), 1)
                dve.wait_ge(ev("u_w"), 2 * (j + 1))
                for w in range(PE_TAPS, TAPS):
                    r = w * KD + j
                    wc = vecT[:, 2 + r // P, r % P:r % P + 1]
                    for n, (b, c0, c1) in enumerate(((5, 0, 512), (7, 512, SPAN))):
                        acc = PS[:, b, 0:c1 - c0]
                        s = sum_sem[n]
                        if w == PE_TAPS:
                            dve.tensor_scalar(acc, upad[:, j, w + c0:w + c1], wc, None, ALU.mult).then_inc(ev(s), 1)
                        else:
                            dve.wait_ge(ev(s), (TAPS - PE_TAPS) * j + w - PE_TAPS)
                            dve.scalar_tensor_tensor(out=acc, in0=upad[:, j, w + c0:w + c1], scalar=wc, in1=acc,
                                                     op0=ALU.mult, op1=ALU.add).then_inc(ev(s), 1)
                dve.wait_ge(ev("conv_a"), 2 * (j + 1))
                for n, (b, c0, c1) in enumerate(((5, 0, 512), (7, 512, SPAN))):
                    dve.wait_ge(ev(sum_sem[n]), (TAPS - PE_TAPS) * (j + 1))
                    tt(cv[:, j, c0:c1], cv[:, j, c0:c1], PS[:, b, 0:c1 - c0], ALU.add).then_inc(ev("conv_v"), 1)
                dve.wait_ge(ev("conv_v"), 2 * (j + 1))
            dve.wait_ge(ev("ln_sum"), 1)
            for k in range(KD):
                for b, c0, c1 in ((0, 0, 512), (1, 512, SPAN)):
                    dve.scalar_tensor_tensor(out=cv[:, k, c0:c1], in0=PS[:, b, 0:c1 - c0], scalar=-1.0 / CONV,
                                             in1=cv[:, k, c0:c1], op0=ALU.mult, op1=ALU.add).then_inc(ev("ln_d"), 1)
            dve.wait_ge(ev("ln_root"), 2)
            dve.wait_ge(ev("ln_d"), 2 * KD)
            link(dve.reciprocal(PS[:, 2, :], rs[:, 0:512]))
            link(dve.reciprocal(PS[:, 3, 0:CONTEXT], cache_cT[:, :]))
            for k in range(KD):
                tt(cv[:, k, 0:SAMPLE], cv[:, k, 0:SAMPLE], PS[:, 2, :], ALU.mult).then_inc(ev("ln_n"), 1)
                tt(cv[:, k, CTX0:SPAN], cv[:, k, CTX0:SPAN], PS[:, 3, 0:CONTEXT], ALU.mult).then_inc(ev("ln_n"), 1)
            add_out(1)
            moe(1)
            for i in range(0, 2 * NT, 2):
                t = i // 2
                dve.wait_ge(ev("fin_t"), i + 1)
                dve.tensor_copy(xtok[:, t, 0:512], PS[:, 4 + i % 4, :]).then_inc(ev("fin_v"), 1)

        @block.gpsimd
        def _(pool):
            step = [0]

            def link(ins):
                step[0] += 1
                ins.then_inc(ev("pool_step"), 1)
                pool.wait_ge(ev("pool_step"), step[0])

            def ctx_mod(q):
                l = q // 2
                pool.wait_ge(ev("coef"), q + 1)
                for k in range(KD):
                    pool.wait_ge(ev("hn"), 2 * KD * q + 2 * k + 2)
                    pool.tensor_scalar(hT[:, k, SAMPLE:T], hT[:, k, SAMPLE:T], modA[:, q, k, 1:2],
                                       modT[:, l, 24 * (q % 2) + k, 1:2], ALU.mult, ALU.add).then_inc(ev("h_c"), 1)

            ctx_mod(0)
            n_out = 0
            pool.wait_ge(ev("z_v"), 4 * NT)
            pool.wait_ge(ev("z_a"), 4 * NT)
            pool.dma_start(f["new_krope"][0, 0], z[:, ST, Z_KR:Z_RQ]).then_inc(ev("side_out"), 16)
            pool.wait_ge(ev("upd_c"), NT)
            for d in range(2):
                pool.dma_start(f["new_state"][0, 0, d].rearrange("h k v -> k h v"),
                               upd[d * RK:(d + 1) * RK, ST, :, :]).then_inc(ev("side_out"), 16)
            pool.wait_ge(ev("lat_n"), NT)
            pool.dma_start(f["new_ckv"][0, 0], z[:, ST, QRANK:Z_KR]).then_inc(ev("ckv_out"), 16)
            pool.wait_ge(ev("qkg_s"), 1)
            for u, (kind, t) in enumerate(UNITS):
                raw = qkraw[:, u % 2, :].rearrange("p (h n) -> p h n", h=HEADS)
                if kind == "k":
                    kr = z[:, t, Z_KR:Z_RQ] if t < NT else cache_in[:, KVRANK:]
                    if u >= 2:
                        pool.wait_ge(ev("hd_t"), u - 1)
                    pool.tensor_copy(raw[:, :, NOPE:QK], bc(kr.unsqueeze(1), [P, HEADS, ROPE])).then_inc(ev("kr_p"), 1)
                pool.wait_ge(ev("qk_r"), u + 1)
                gain = bc(qkg[:, 0 if kind == "q" else 1, :].unsqueeze(1), [P, HEADS, QK])
                ins = pool.tensor_tensor(raw, raw, gain, ALU.mult)
                if t < ST:
                    link(ins)
                    x1, x2 = raw[:, :, NOPE:NOPE + 16], raw[:, :, NOPE + 16:QK]
                    cs = bc(cst[:, C_COS + 16 * t:C_COS + 16 * t + 16].unsqueeze(1), [P, HEADS, 16])
                    sn = bc(cst[:, C_SIN + 16 * t:C_SIN + 16 * t + 16].unsqueeze(1), [P, HEADS, 16])
                    r = [ropet[:, n, :].rearrange("p (h n) -> p h n", h=HEADS) for n in range(4)]
                    pool.tensor_tensor(r[0], x1, cs, ALU.mult)
                    pool.tensor_tensor(r[1], x2, sn, ALU.mult)
                    pool.tensor_tensor(r[2], x1, sn, ALU.mult)
                    link(pool.tensor_tensor(r[3], x2, cs, ALU.mult))
                    link(pool.tensor_tensor(x1, r[0], r[1], ALU.subtract))
                    ins = pool.tensor_tensor(x2, r[2], r[3], ALU.add)
                ins.then_inc(ev("qk_n"), 1)
                pool.wait_ge(ev("qk_n"), u + 1)

            def moe(l):
                q = 2 * l + 1
                ctx_mod(q)
                if l == 0:
                    pool.wait_ge(ev("side_out"), 48)
                    pool.wait_ge(ev("ckv_out"), 16)
                pool.wait_ge(ev("pos"), l + 1)
                for t in range(NT):
                    pool.wait_ge(ev("htok_a"), 2 * NT * l + 2 * (t + 1))
                    for c in range(2):
                        pool.indirect_dma_start(
                            rows_in[:, :], bass.IndirectOffsetOnAxis(ap=posu[:, c * NT + t:c * NT + t + 1], axis=0),
                            htok[:, t, :], None).then_inc(ev("rows_sent"), 16)
                pool.wait_ge(ev("rows_sent"), 16 * 2 * NT * (l + 1))
                pool.memset(xsT[:, :, ROWS:XW], 0.0).then_inc(ev("pad"), 1)
                pool.wait_ge(ev("xs_v"), RT * l + RT)
                pool.wait_ge(ev("xs_a"), RT * l + RT)
                pool.wait_ge(ev("pad"), l + 1)
                pool.wait_ge(ev("tab"), 4 * l + 4)
                if l == 0:
                    pool.wait_ge(ev("up_mm"), 1)
                with pool.Fori(0, EXPERTS) as e:
                    off = pool.value_load(tab[0:1, bass.ds(e, 1)], min_val=0, max_val=ROWS)
                    blocks = pool.value_load(tab[0:1, bass.ds(e + EXPERTS, 1)], min_val=1, max_val=MAXBLK)
                    before = pool.value_load(tab[0:1, bass.ds(e + 2 * EXPERTS, 1)], min_val=0, max_val=2 * ALLBLK)
                    with pool.Fori(0, blocks) as b:
                        pool.wait_ge(ev("up_mm"), before + b + 1)
                        row = pool.snap(nc.s_assert_within(
                            off + b * BLK, 0, ROWS,
                            skip_runtime_bounds_check_because="a further block starts inside the expert's rows"))
                        pool.tensor_copy(xblk[:, :, :], xsT[:, :, bass.ds(row, BLK)]).then_inc(ev("xblk_c"), 1)
                pool.wait_ge(ev("results_sent"), l + 1)
                for t in range(NT):
                    for c in range(2):
                        pool.indirect_dma_start(
                            ygat[:, c * NT + t, :], None, rows_out[0:ROWS, :],
                            bass.IndirectOffsetOnAxis(ap=posu[:, c * NT + t:c * NT + t + 1], axis=0)) \
                            .then_inc(ev(f"picked{t}"), 16)

            moe(0)
            pool.wait_ge(ev("comb"), 2 * NT)
            for t in range(NT):
                pool.wait_ge(ev(f"picked{t}"), 32)
            ctx_mod(2)
            pool.memset(upad[:, :, 0:HALO], 0.0)
            pool.memset(upad[:, :, HALO + SAMPLE:HALO + CTX0], 0.0)
            pool.memset(upad[:, :, PADW - HALO:PADW], 0.0).then_inc(ev("u_zero"), 1)
            for j in range(KD):
                if j >= 2:
                    pool.wait_ge(ev("tap_mm"), j - 1)
                for w in range(PE_TAPS):
                    r = w * KD + j
                    pool.tensor_scalar(tapd[:, j % 2, w, :], ident, vecT[:, 2 + r // P, r % P:r % P + 1], None,
                                       ALU.mult).then_inc(ev("tap_d"), 1)
            moe(1)


_INS = ['x_prompt', 'x_sample', 'cache_mla_ckv', 'cache_mla_krope', 'state_retention', 'c', 'c_ctx', 'ada_w', 'ada_b',
        'norm_mix', 'norm_ffn', 'ev_w_in', 'ev_q_a_norm', 'ev_w_q_up', 'ev_kv_a_norm', 'ev_w_kv_up', 'ev_q_norm',
        'ev_k_norm', 'ev_ret_decay', 'ev_ret_gn', 'ev_w_out', 'od_w_in', 'od_dw', 'od_dw_b', 'od_ln_g', 'od_ln_b',
        'od_w_out', 'moe_w_group', 'moe_b_group', 'moe_w_expert', 'moe_b_expert', 'moe_w_up', 'moe_w_down']
_OUTS = [("y_prompt", (1, CONTEXT, D)), ("y_sample", (1, SAMPLE, D)), ("new_ckv", (1, 1, CONTEXT, KVRANK)),
         ("new_krope", (1, 1, CONTEXT, ROPE)), ("new_state", (1, 1, 2, RH, RK, RV))]


def shape_constants():
    import numpy as np
    c = np.zeros((P, C_W), np.float32)
    i = np.arange(P)
    c[:, C_ID:C_ID + P] = np.eye(P)
    c[:, C_ONE:C_ONE + P] = 1.0
    c[:, C_TRI:C_TRI + P] = i[:, None] < i[None, :]
    d = i[None, :] - i[:, None]
    dist = np.concatenate([np.maximum(d, 0), d >= 0, np.maximum(-d, 0), d <= 0], axis=1).astype(np.float32)
    freqs = np.float32(10000.0) ** (-np.arange(8, dtype=np.float32) / np.float32(8))
    tok = np.arange(SAMPLE)
    ang = np.concatenate([(tok // GRID_W)[:, None] * freqs, (tok % GRID_W)[:, None] * freqs], axis=1)
    for off, v in ((C_COS, np.cos(ang)), (C_SIN, np.sin(ang))):
        c[:, off:off + ST * 16] = v.reshape(ST, P, 16).transpose(1, 0, 2).reshape(P, ST * 16)
    c[:, C_POS:C_POS + 4] = np.stack([P - 1 - i, i + 1, i, P - i], axis=1)
    c[:, C_PRI4:C_PRI4 + 4] = np.arange(4, 0, -1)
    c[:, C_PRI8:C_PRI8 + 8] = np.arange(8, 0, -1)
    c[:, C_THR:C_THR + MAXBLK - 1] = BLK * np.arange(1, MAXBLK)
    c[:, C_EPS] = EPS
    return c, dist


def kernel(**inputs):
    import numpy as _np
    import concourse.bacc as _bacc
    from concourse import mybir as _mybir
    from concourse.bass_utils import run_bass_kernel_spmd as _run

    nc = _bacc.Bacc("TRN2", target_bir_lowering=False, num_devices=1)
    arrays, io = {}, {}
    named = {name: _np.ascontiguousarray(inputs[name]) for name in _INS}
    named["consts"], named["distances"] = shape_constants()
    for name, a in named.items():
        arrays[f"in_{name}"] = a
        io[name] = nc.dram_tensor(f"in_{name}", a.shape, _mybir.dt.from_np(a.dtype), kind="ExternalInput").ap()
    for name, shape in _OUTS:
        io[name] = nc.dram_tensor(f"out_{name}", shape, F32, kind="ExternalOutput").ap()
    build(nc, io)
    r = _run(nc, [arrays], core_ids=[0])
    return tuple(r.results[0][f"out_{name}"] for name, _ in _OUTS)
```

```python
from contextlib import ExitStack

import concourse.bass as bass
from concourse import mybir

F32 = mybir.dt.float32
I32 = mybir.dt.int32
U32 = mybir.dt.uint32
ALU = mybir.AluOpType
ACT = mybir.ActivationFunctionType
AX = mybir.AxisListType

P = 128
D = 1024
KD = D // P
SAMPLE, CONTEXT = 512, 128
T = SAMPLE + CONTEXT
NT = T // P
ST = SAMPLE // P
PAST = 128
GRID_W = 64
EPS = 1e-6
HEADS, NOPE, ROPE, VD = 8, 64, 32, 64
QK = NOPE + ROPE
QRANK, KVRANK = 256, 128
RH, RK, RV = 4, 64, 128
EVEN_IN = QRANK + KVRANK + ROPE + 2 * RH * RK + 2 * RH * RV
Z_KR = QRANK + KVRANK
Z_RQ = Z_KR + ROPE
Z_RK = Z_RQ + RH * RK
Z_RV = Z_RK + RH * RK
Z_RG = Z_RV + RH * RV
CONV = 1024
TAPS = 31
HALO = TAPS // 2
PADW = HALO + SAMPLE + HALO + CONTEXT + HALO
SPAN = SAMPLE + HALO + CONTEXT
CTX0 = SAMPLE + HALO
GROUPS, PER, EXPERTS, TOPK, FF = 4, 8, 32, 2, 256
ROUTE = GROUPS + EXPERTS
ROWS = T * TOPK
RT = ROWS // P
BLK = 64
XW = ROWS + BLK
MAXBLK = (T + BLK - 1) // BLK
ALLBLK = ROWS // BLK + EXPERTS

SLOT = 2048
SLOTS = 9
PER_EXPERT = 3
RING_EXPERTS = SLOTS // PER_EXPERT

C_ID, C_ONE, C_TRI = 0, P, 2 * P
D_A1, D_U, D_A2, D_L = 0, P, 2 * P, 3 * P
C_COS = 3 * P
C_SIN = C_COS + ST * 16
C_POS = C_SIN + ST * 16
C_PRI4 = C_POS + 4
C_PRI8 = C_PRI4 + 4
C_THR = C_PRI8 + 8
C_EPS = C_THR + MAXBLK - 1
C_W = C_EPS + 1

V_ADAB, V_COND, V_NMIX = 0, 96, 112
V_NFFN, V_DWB, V_LNG, V_LNB, V_GN, V_QA = 0, 16, 24, 32, 40, 44
V_ROWS = (128, 46, 128, TAPS * 8 - 128)

A_H = 0
A_QT = 0
A_Z = 5120
A_KT = A_Z + NT * EVEN_IN
A_V = A_KT + 6144
ARENA = A_V + 3072
A_XS = 0
A_HTOK = 5120
A_YG = KD * XW
A_BLK = A_YG + 2 * NT * D
A_U = 5120
A_CV = A_U + KD * PADW
A_DG = A_CV + KD * SPAN
PE_TAPS = 5
A_CB = A_DG + 2 * PE_TAPS * P
SEG = T // 2
HALF = (SPAN + 1) // 2
LATE_TAPS = 5
assert A_BLK + 1408 <= ARENA and A_CB + SPAN <= ARENA


def weight_plan():
    plan = [("ada0", j) for j in range(8)]
    for c in range(8):
        plan += [("ev_in", c), ("ada0", 8 + 2 * c), ("ada0", 9 + 2 * c)]
    plan += [("ada1", j) for j in range(20)]
    plan += [("q_up", 0), ("kv_up", 0)]
    plan += [("ada1", j) for j in range(20, 24)]
    plan += [("ev_out", j) for j in range(4)]
    plan += [("expert0", i) for i in range(PER_EXPERT * EXPERTS)]
    plan += [("od_in", j) for j in range(8)]
    plan += [("od_out", j) for j in range(4)]
    plan += [("expert1", i) for i in range(PER_EXPERT * EXPERTS)]
    return plan


def build(nc, io):
    f = io
    ctx = ExitStack()
    with ctx:
        def sb(name, shape, dt=F32):
            return ctx.enter_context(nc.sbuf_tensor(name, shape, dt))

        def sem(name):
            return ctx.enter_context(nc.semaphore(name))

        xT = sb("xT", [P, KD, T])
        arena = sb("arena", [P, ARENA])
        ring = sb("ring", [P, SLOTS, SLOT])
        cst = sb("cst", [P, C_W])
        vrow = arena[:, A_V:A_V + 4 * P].rearrange("p (g n) -> p g n", g=4)
        vecT = sb("vecT", [P, 4, P])
        scT = sb("scT", [P, KD, 32])
        modT = sb("modT", [P, 2, 48, 2])
        modA = sb("modA", [P, 4, KD, 2])
        wr = sb("wr", [P, KD, ROUTE])
        rb = sb("rb", [P, 2, ROUTE])
        kvg = sb("kvg", [P, KVRANK])
        qkg = sb("qkg", [P, 2, QK])
        dec = sb("dec", [P, 2 * RH])
        decw = sb("decw", [P, 3, 2 * RH])
        edge = sb("edge", [P, 6, RH])
        cache_cT = sb("cache_cT", [P, P])
        ss = sb("ss", [P, 2, 16])
        stat = sb("stat", [P, RH, 6])
        mv = sb("mv", [P, RH, 2])
        rmv = sb("rmv", [P, RH])
        nmx = sb("nmx", [P, 2])
        cmx = sb("cmx", [P, 2, 4])
        den = sb("den", [P, 2])
        rden = sb("rden", [P, 2])
        r1 = sb("r1", [P, 12, NT])
        cnt = sb("cnt", [P, 6, EXPERTS])
        posf = sb("posf", [P, 2, NT])
        posu = sb("posu", [P, 2 * NT], U32)
        wtok = sb("wtok", [P, 2, NT])
        tab = sb("tab", [1, 3 * EXPERTS + 1], I32)
        blocks0 = sb("blocks0", [P, 1])
        tick = sb("tick", [P, 4])
        PS = ctx.enter_context(nc.psum_tensor("PS", [P, 8, 512], F32))

        rows_in = nc.dram_tensor("rows_in", (ROWS, D), F32).ap()
        rows_out = nc.dram_tensor("rows_out", (XW, D), F32).ap()

        ident = cst[:, C_ID:C_ID + P]
        ones = cst[:, C_ONE:C_ONE + P]
        tri = cst[:, C_TRI:C_TRI + P]
        eps = cst[:, C_EPS:C_EPS + 1]

        hT = arena[:, A_H:A_H + KD * T].rearrange("p (k t) -> p k t", k=KD)
        z = arena[:, A_Z:A_Z + NT * EVEN_IN].rearrange("p (t n) -> p t n", t=NT)
        xtok = arena[:, A_Z:A_Z + NT * D].rearrange("p (t n) -> p t n", t=NT)
        A_K = A_KT
        states = arena[:, A_K:A_K + ST * 512].rearrange("p (t h n) -> p t h n", t=ST, h=RH)
        upd = arena[:, A_K + 2048:A_K + 2048 + NT * 512].rearrange("p (t h n) -> p t h n", t=NT, h=RH)
        rqT = arena[0:RK, A_K + 4608:A_K + 5120].rearrange("p (h n) -> p h n", h=RH)
        rkT = arena[0:RK, A_K + 5120:A_K + 5632].rearrange("p (h n) -> p h n", h=RH)
        qfbT = arena[:, A_K + 5632:A_K + 6144].rearrange("p (h n) -> p h n", h=RH)
        kfb = arena[:, A_V:A_V + 512].rearrange("p (h n) -> p h n", h=RH)
        qfb = arena[:, A_V + 512:A_V + 1024].rearrange("p (h n) -> p h n", h=RH)
        rsc = arena[:, A_V + 1024:A_V + 1536].rearrange("p (h n) -> p h n", h=RH)
        onrm = arena[:, A_V + 1536:A_V + 2048].rearrange("p (h n) -> p h n", h=RH)
        mtmp = arena[:, A_V + 1024:A_V + 2048].rearrange("p (a n) -> p a n", a=8)
        dist = arena[:, A_V + 2048:A_V + 2560]
        mask = arena[:, A_V + 2560:A_V + 3072].rearrange("p (h n) -> p h n", h=RH)
        qT = arena[0:QK, A_QT:A_QT + HEADS * T].rearrange("p (h t) -> p h t", h=HEADS)
        kT = arena[0:QK, A_KT:A_KT + HEADS * 768].rearrange("p (h t) -> p h t", h=HEADS)
        vS = arena[:, A_V:A_V + 3072].rearrange("p (j h n) -> p j h n", j=6, h=HEADS)

        cT = z[:, :, Z_RV:Z_RV + 3 * P].rearrange("p t (j n) -> p t j n", j=3)
        prob = [z[:, :, 0:P], z[:, :, P:2 * P]]
        probT = [z[:, :, Z_RQ:Z_RQ + 512], z[:, :, Z_RQ + 512:Z_RQ + 1024]]
        oret = z[:, :, Z_RG:Z_RG + 512]
        oT = arena[:, A_QT:A_QT + KD * T].rearrange("p (k t) -> p k t", k=KD)
        htok = arena[:, A_HTOK:A_HTOK + NT * D].rearrange("p (t n) -> p t n", t=NT)
        xsT = arena[:, A_XS:A_XS + KD * XW].rearrange("p (k r) -> p k r", k=KD)
        xback = arena[:, A_YG:A_YG + RT * D].rearrange("p (j n) -> p j n", j=RT)
        ygat = xback
        xblk = arena[:, A_BLK:A_BLK + 512].rearrange("p (k n) -> p k n", k=KD)
        gsil = arena[:, A_BLK + 512:A_BLK + 640]
        gact = arena[:, A_BLK + 640:A_BLK + 768]
        hblk = arena[:, A_BLK + 768:A_BLK + 896].rearrange("p (i n) -> p i n", i=2)
        yblk = arena[:, A_BLK + 896:A_BLK + 1408]
        upad = arena[:, A_U:A_U + KD * PADW].rearrange("p (k t) -> p k t", k=KD)
        cv = arena[:, A_CV:A_CV + KD * SPAN].rearrange("p (k t) -> p k t", k=KD)
        cv2 = arena[:, 0:KD * SPAN].rearrange("p (k t) -> p k t", k=KD)
        tapd = arena[:, A_DG:A_DG + 2 * PE_TAPS * P].rearrange("p (b w n) -> p b w n", b=2, w=PE_TAPS)
        cache_in = sb("cache_in", [P, KVRANK + ROPE])
        sq1 = arena[:, A_Z:A_Z + KD * T].rearrange("p (k t) -> p k t", k=KD)
        cvn = arena[:, KD * SPAN:KD * (SPAN + T)].rearrange("p (k t) -> p k t", k=KD)
        cvb = arena[:, A_CB:A_CB + SPAN]
        scratch = sb("scratch", [P, 3 * HEADS * QK])
        qkraw = scratch[:, 0:2 * HEADS * QK].rearrange("p (b n) -> p b n", b=2)
        qksq = scratch[:, 2 * HEADS * QK:].unsqueeze(1)
        ropet = z[:, 0:4, Z_RV + 3 * P:Z_RV + 4 * P]
        octx = scratch[:, 0:4 * P].rearrange("p (k t) -> p k t", k=4)
        mrow = scratch[:, 0:512]
        cell = [0]

        def cells(*shape):
            n = 1
            for x in shape:
                n *= x
            cell[0] += n
            assert cell[0] <= 3 * HEADS * QK
            names = " ".join("abc"[:len(shape)])
            return scratch[:, cell[0] - n:cell[0]].rearrange(
                f"p ({names}) -> p {names}", **dict(zip("abc", shape))) if len(shape) > 1 \
                else scratch[:, cell[0] - n:cell[0]]
        lgt = cells(NT, ROUTE)
        rt = cells(9, NT, PER)
        one32 = cells(2, NT, EXPERTS)
        both = cells(NT, EXPERTS)
        slotpos = cells(NT, EXPERTS)
        cmpt = cells(EXPERTS, MAXBLK - 1)
        rs = cells(T)

        plan = weight_plan()
        at = {}
        for n, key in enumerate(plan):
            at[key] = n
        ring_full = [sem(f"ring_full{s}") for s in range(SLOTS)]
        S = {}

        def ev(name):
            if name not in S:
                S[name] = sem(name)
            return S[name]

        def released(key):
            kind, j = key
            if kind == "ada0":
                return ev("mod_mm"), j + 1
            if kind == "ada1":
                return ev("mod_mm"), 24 + j + 1
            if kind == "ev_in":
                return ev("z_mm"), NT * (j + 1)
            if kind in ("q_up", "kv_up"):
                return ev("qk_mm"), NT + NT + 1
            if kind == "ev_out":
                return ev("wo_mm"), 2 * (j + 1)
            if kind == "od_in":
                return ev("gate_mm"), 2 * (j + 1)
            if kind == "od_out":
                return ev("wo_mm"), KD + 2 * (j + 1)
            return ev("expert_done"), EXPERTS * int(kind[6]) + j // PER_EXPERT + 1

        NPARAM = 14
        DTAPS = TAPS - PE_TAPS
        CONV_OPS = DTAPS + 3
        full_count, filled = [], [0] * SLOTS
        for n, key in enumerate(plan):
            filled[n % SLOTS] += 32 if key[0] == "od_in" else 16
            full_count.append(filled[n % SLOTS])
        ATT = [("ctx", g, 0) for g in range(2)] + [("lat", h, t) for h in range(HEADS) for t in range(ST)]
        NATT = len(ATT)
        GROUP_END = {0: 0, 1: 1}
        for hp in range(4):
            GROUP_END[2 + (hp + 1) * 2 * ST - 1] = 2 + hp

        def groups_before(i):
            return i if i < 2 else 2 + (i - 2) // (2 * ST)
        UNITS = [(kind, t) for t in range(NT) for kind in "qk"] + [("k", NT)]
        KCOL = [0, P, 2 * P, 3 * P, 5 * P, 4 * P]
        VROW = [0, 1, 2, 3, 5, 4]
        PSf = PS[:, :, :].rearrange("p b n -> p (b n)")

        def w_view(key):
            return ring[:, at[key] % SLOTS, :]

        def quad(b):
            return PS[:, b, :].rearrange("p (j n) -> p j n", j=4)

        def squares(q):
            return sq1 if q == 1 else hT

        def bc(ap, shape):
            return ap.to_broadcast(shape)

        block = ctx.enter_context(nc.Block())

        @block.sync
        def _(sp):
            def source(key):
                kind, j = key
                v8 = w_view(key).rearrange("p (k n) -> p k n", k=KD)
                if kind in ("ada0", "ada1"):
                    r, k = j // KD, j % KD
                    return f["ada_w"][int(kind[3]), k * P:(k + 1) * P, SLOT * r:SLOT * (r + 1)], w_view(key)
                if kind == "ev_in":
                    n = min(256, EVEN_IN - 256 * j)
                    return f["ev_w_in"][0, :, 256 * j:256 * j + n].rearrange("(k p) n -> p k n", p=P), v8[:, :, 0:n]
                if kind == "q_up":
                    return (f["ev_w_q_up"][0].rearrange("(k p) n -> p k n", p=P),
                            w_view(key)[:, 0:1536].rearrange("p (k n) -> p k n", k=2))
                if kind == "kv_up":
                    return f["ev_w_kv_up"][0], w_view(key)[:, 0:1024]
                if kind in ("ev_out", "od_out"):
                    w = f["ev_w_out" if kind == "ev_out" else "od_w_out"]
                    return w[0, :, 256 * j:256 * j + 256].rearrange("(k p) n -> p k n", p=P), v8

            def load(n):
                key = plan[n]
                if n >= SLOTS:
                    sp.wait_ge(*released(plan[n - SLOTS]))
                full = ring_full[n % SLOTS]
                if key[0] == "od_in":
                    v = f["od_w_in"][0].rearrange("(k p) (a n) -> p k a n", p=P, a=2)
                    d = w_view(key).rearrange("p (k a n) -> p k a n", k=KD, a=2)
                    for a in range(2):
                        sp.dma_start(d[:, :, a, :], v[:, :, a, P * key[1]:P * key[1] + P]).then_inc(full, 16)
                elif key[0].startswith("expert"):
                    load_part(int(key[0][6]), key[1] // PER_EXPERT, key[1] % PER_EXPERT, n % SLOTS)
                else:
                    src, dst = source(key)
                    sp.dma_start(dst, src).then_inc(full, 16)

            def load_part(l, e, j, s):
                if j < 2:
                    src = f["moe_w_up"][l, bass.ds(e, 1), 512 * j:512 * j + 512, :] \
                        .rearrange("e (k p) n -> p (e k) n", p=P)
                    sp.dma_start(ring[:, s, :].rearrange("p (k n) -> p k n", k=4), src).then_inc(ring_full[s], 16)
                else:
                    src = f["moe_w_down"][l, bass.ds(e, 1), :, :].rearrange("e (k p) n -> p (e k) n", p=P)
                    sp.dma_start(ring[:, s, :].rearrange("p (k n) -> p k n", k=2), src).then_inc(ring_full[s], 16)

            def load_experts(l):
                n0 = at[(f"expert{l}", 0)]
                rounds = EXPERTS // RING_EXPERTS
                for i in range(SLOTS):
                    load(n0 + i)
                with sp.Fori(1, rounds) as g:
                    for p in range(RING_EXPERTS):
                        sp.wait_ge(ev("expert_done"), g * RING_EXPERTS + (EXPERTS * l + p + 1 - RING_EXPERTS))
                        for j in range(PER_EXPERT):
                            load_part(l, g * RING_EXPERTS + p, j, (n0 + PER_EXPERT * p + j) % SLOTS)
                for n in range(n0 + SLOTS * rounds, n0 + PER_EXPERT * EXPERTS):
                    load(n)

            n = 0
            while n < len(plan):
                if plan[n][0].startswith("expert"):
                    load_experts(int(plan[n][0][6]))
                    n += PER_EXPERT * EXPERTS
                else:
                    load(n)
                    n += 1
            for t in range(NT):
                sp.wait_ge(ev("xt_v"), NT + t + 1)
                sp.wait_ge(ev("xt_a"), NT + t + 1)
                dst = f["y_sample"][0, t * P:t * P + P, :] if t < ST else f["y_prompt"][0, :, :]
                sp.dma_start(dst, xtok[:, t, :]).then_inc(ev("y_out"), 16)
            sp.wait_ge(ev("y_out"), 16 * NT)

        @block.tensor
        def _(pe):
            def arrived(key):
                n = at[key]
                pe.wait_ge(ring_full[n % SLOTS], full_count[n])

            def mod_columns(g):
                pe.wait_ge(ev("mrow_c"), g + 1)
                for q in range(4):
                    last = pe.transpose(quad(5 if g == 0 else 6)[:, q, :], mrow[:, q * P:(q + 1) * P], ident)
                last.then_inc(ev("mod_t"), 1)

            def modulation(l, j):
                n = 24 * l + j
                if n % KD == 0 and n > KD:
                    mod_columns(n // KD - 1)
                arrived((f"ada{l}", j))
                w = w_view((f"ada{l}", j))
                for c in range(4):
                    last = pe.matmul(PS[32 * c:32 * c + 32, 7, :], scT[:, j % KD, :], w[:, 512 * c:512 * c + 512],
                                     start=(j % KD == 0), stop=(j % KD == KD - 1))
                last.then_inc(ev("mod_mm"), 1)

            def norm_sums(q):
                for k in range(KD):
                    pe.wait_ge(ev("squared"), KD * q + k + 1)
                    pe.matmul(PS[:, 4, :], ones, squares(q)[:, k, 0:SAMPLE], start=(k == 0), stop=(k == KD - 1))
                    last = pe.matmul(PS[:, 6, 0:CONTEXT], ones, squares(q)[:, k, SAMPLE:T],
                                     start=(k == 0), stop=(k == KD - 1))
                last.then_inc(ev("sumsq"), 1)

            def project_out(l, kind, src, tile):
                for m in range(KD):
                    if m % 2 == 0:
                        arrived((kind, m // 2))
                        w = w_view((kind, m // 2)).rearrange("p (k n) -> p k n", k=KD)
                    if m >= 2:
                        pe.wait_ge(ev("wo_ev"), KD * l + m - 1)
                    b = 4 + 2 * (m % 2)
                    c = (m % 2) * P
                    for k in range(KD):
                        if l == 1 and m == 0:
                            pe.wait_ge(ev("act1"), k + 1)
                        for n in range(2):
                            last = pe.matmul(PS[:, b + n, 0:SEG], w[:, k, c:c + P], src[:, tile(k), n * SEG:(n + 1) * SEG],
                                             start=(k == 0), stop=(k == KD - 1))
                    last.then_inc(ev("wo_mm"), 1)

            pe.wait_ge(ev("params_in"), 16 * NPARAM)
            for g, r in enumerate(V_ROWS):
                last = pe.transpose(PS[:, 5, g * P:g * P + r], vrow[0:r, g, :], cst[0:r, C_ID:C_ID + r])
            last.then_inc(ev("vec_t"), 1)
            for i in range(2 * NT):
                t, half = i // 2, i % 2
                if half == 0:
                    pe.wait_ge(ev("x_in"), 32)
                if i >= 4:
                    pe.wait_ge(ev(("xt_v", "xt_a")[i % 2]), (i - 4) // 2 + 1)
                for j in range(4):
                    last = pe.transpose(quad(i % 4)[:, j, :],
                                        xtok[:, t, (4 * half + j) * P:(4 * half + j + 1) * P], ident)
                last.then_inc(ev("x_t"), 1)
            norm_sums(0)
            pe.wait_ge(ev("sc_ready"), 1)
            for j in range(8):
                modulation(0, j)
            mod_columns(0)
            pe.wait_ge(ev("xt_v"), NT)
            pe.wait_ge(ev("xt_a"), NT)
            pe.wait_ge(ev("vec_c"), 4)
            for c in range(8):
                n = min(256, EVEN_IN - 256 * c)
                arrived(("ev_in", c))
                w = w_view(("ev_in", c)).rearrange("p (k n) -> p k n", k=KD)
                for t in range(NT):
                    i = NT * c + t
                    if i >= 4:
                        pe.wait_ge(ev(("z_v", "z_a")[i % 2]), (i - 4) // 2 + 1)
                    for k in range(KD):
                        if i < NT:
                            pe.wait_ge(ev("h_s" if t < ST else "h_c"), k + 1)
                        last = pe.matmul(PS[:, i % 4, 0:n], hT[:, k, t * P:t * P + P], w[:, k, 0:n],
                                         start=(k == 0), stop=(k == KD - 1))
                    last.then_inc(ev("z_mm"), 1)
                for j in (8 + 2 * c, 9 + 2 * c):
                    modulation(0, j)
            pe.wait_ge(ev("z_v"), 20)
            pe.wait_ge(ev("z_a"), 20)
            for t in range(NT):
                pe.wait_ge(ev("kfb"), t + 1)
                if t >= 2:
                    pe.wait_ge(ev("upd_c"), t - 1)
                for h in range(RH):
                    last = pe.matmul(quad(t % 2)[:, h, :], kfb[:, h, :], z[:, t, Z_RV + h * RV:Z_RV + (h + 1) * RV],
                                     start=True, stop=True)
                last.then_inc(ev("upd_mm"), 1)
                modulation(1, 2 * t)
                modulation(1, 2 * t + 1)
            pe.wait_ge(ev("upd_c"), NT)
            for t in range(NT):
                if t >= 1:
                    pe.wait_ge(ev("rq_c"), t)
                for h in range(RH):
                    last = pe.transpose(quad(0)[0:RK, h, :], z[:, t, Z_RQ + h * RK:Z_RQ + (h + 1) * RK], ident)
                last.then_inc(ev("rq_t"), 1)
                if t >= 1:
                    pe.wait_ge(ev("rk_c"), t)
                for h in range(RH):
                    last = pe.transpose(quad(1)[0:RK, h, :], z[:, t, Z_RK + h * RK:Z_RK + (h + 1) * RK], ident)
                last.then_inc(ev("rk_t"), 1)
                if t < ST:
                    pe.wait_ge(ev("qfb"), t + 1)
                    if t >= 1:
                        pe.wait_ge(ev("qfb_c"), t)
                    for h in range(RH):
                        last = pe.transpose(quad(2)[:, h, :], qfb[:, h, :], ident)
                    last.then_inc(ev("qfb_t"), 1)
                modulation(1, 10 + 2 * t)
                pe.wait_ge(ev("rq_c"), t + 1)
                pe.wait_ge(ev("rk_c"), t + 1)
                if t >= 1:
                    pe.wait_ge(ev("rsc"), t)
                for h in range(RH):
                    last = pe.matmul(quad(3)[:, h, :], rkT[:, h, :], rqT[:, h, :], start=True, stop=True)
                last.then_inc(ev("rs_mm"), 1)
                modulation(1, 11 + 2 * t)
                pe.wait_ge(ev("rsc"), t + 1)
                if t < ST:
                    pe.wait_ge(ev("qfb_c"), t + 1)
                    pe.wait_ge(ev("states"), ST - 1)
                if t >= 1:
                    pe.wait_ge(ev("onrm"), t)
                for h in range(RH):
                    last = pe.matmul(quad(4)[:, h, :], rsc[:, h, :], z[:, t, Z_RV + h * RV:Z_RV + (h + 1) * RV],
                                     start=True, stop=(t == ST))
                    if t < ST:
                        last = pe.matmul(quad(4)[:, h, :], qfbT[:, h, :], states[:, t, h, :],
                                         start=False, stop=True)
                last.then_inc(ev("ro_mm"), 1)
            pe.wait_ge(ev("mod_c"), 5)
            for t in range(NT + 1):
                if t < NT:
                    pe.wait_ge(ev("lat_n"), t + 1)
                if t >= 2:
                    pe.wait_ge(ev("lat_c"), t - 1)
                b = 5 + t % 2
                if t < NT:
                    for j in range(3):
                        last = pe.transpose(quad(b)[:, j, :], z[:, t, j * P:(j + 1) * P], ident)
                else:
                    last = pe.transpose(quad(b)[:, 0, :], cache_in[:, 0:KVRANK], ident)
                last.then_inc(ev("lat_t"), 1)
            arrived(("q_up", 0))
            arrived(("kv_up", 0))
            wq = w_view(("q_up", 0))[:, 0:1536].rearrange("p (k n) -> p k n", k=2)
            wkv = w_view(("kv_up", 0))
            pe.wait_ge(ev("lat_c"), NT + 1)
            pe.wait_ge(ev("onrm"), NT)
            for u in range(len(UNITS) + 1):
                if u < len(UNITS):
                    kind, t = UNITS[u]
                    b = 2 * (u % 2)
                    if u >= 2:
                        pe.wait_ge(ev("raw_a"), u - 1)
                        if UNITS[u - 2][0] == "k":
                            pe.wait_ge(ev("v_c"), (u - 2) // 2 + 1 if u - 2 < 10 else 6)
                    if u == 10:
                        pe.wait_ge(ev("v_c"), 4)
                    for half in range(2):
                        if kind == "q":
                            for k in range(2):
                                last = pe.matmul(PS[:, b + half, 0:384], cT[:, t, k, :],
                                                 wq[:, k, half * 384:half * 384 + 384],
                                                 start=(k == 0), stop=(k == 1))
                        else:
                            lat = cT[:, t, 2, :] if t < NT else cache_cT[:, :]
                            last = pe.matmul(PS[:, b + half, :], lat, wkv[:, half * 512:half * 512 + 512],
                                             start=True, stop=True)
                    last.then_inc(ev("qk_mm"), 1)
                    if u % 2 == 1 and u // 2 < 4:
                        modulation(1, 20 + u // 2)
                if u >= 1:
                    pe.wait_ge(ev("qk_n"), u)
                    if u >= 2:
                        pe.wait_ge(ev("hd_a"), u - 1)
                        pe.wait_ge(ev("hd_v"), u - 1)
                    raw = qkraw[:, (u - 1) % 2, :].rearrange("p (h n) -> p h n", h=HEADS)
                    for h in range(HEADS):
                        last = pe.transpose(quad(4 + h // 4)[0:QK, h % 4, :], raw[:, h, :], ident)
                    last.then_inc(ev("hd_t"), 1)
            pe.wait_ge(ev("hd_a"), len(UNITS))
            pe.wait_ge(ev("hd_v"), len(UNITS))
            pe.wait_ge(ev("v_c"), NT + 1)
            mod_columns(5)
            pe.wait_ge(ev("mod_c"), 6)
            for i in range(NATT + 3):
                if i < NATT:
                    kind, h, t = ATT[i]
                    b = 2 * (i % 2)
                    if i >= 2:
                        pe.wait_ge(ev("prob"), i - 1)
                    if kind == "lat":
                        for n in range(2):
                            last = pe.matmul(PS[:, b + n, 0:SEG], qT[:, h, t * P:t * P + P],
                                             kT[:, h, n * SEG:(n + 1) * SEG], start=True, stop=True)
                    else:
                        for n in range(4):
                            last = pe.matmul(quad(b)[:, n, :], qT[:, 4 * h + n, SAMPLE:T],
                                             kT[:, 4 * h + n, 640:768], start=True, stop=True)
                    last.then_inc(ev("s_mm"), 1)
                if 2 <= i <= NATT + 1:
                    kind = ATT[i - 2][0]
                    pe.wait_ge(ev("prob_n"), i - 1)
                    if i >= 3:
                        pe.wait_ge(ev("pt_a"), i - 2)
                    if i >= 5:
                        pe.wait_ge(ev("pt_v"), i - 4)
                    for j in range(ST + 1 if kind == "lat" else 4):
                        last = pe.transpose(quad(4 + j // 4)[:, j % 4, :], prob[i % 2][:, j, :], ident)
                    last.then_inc(ev("p_t"), 1)
                if i - 3 in GROUP_END:
                    g = GROUP_END[i - 3]
                    pe.wait_ge(ev("pt_a"), i - 2)
                    if g >= 2:
                        pe.wait_ge(ev("pt_v"), i - 4)
                        pe.wait_ge(ev("o_c"), g - 1)
                    for pair in (range(2) if g < 2 else (0,)):
                        for j in range(ST + 1 if g >= 2 else 1):
                            for hl in range(2):
                                if g < 2:
                                    h = 4 * g + 2 * pair + hl
                                    out = PS[hl * VD:(hl + 1) * VD, 6 + g % 2, pair * P:(pair + 1) * P]
                                    last = pe.matmul(out, vS[:, 5, h, :],
                                                     probT[0][:, g, (2 * pair + hl) * P:(2 * pair + hl + 1) * P],
                                                     start=True, stop=True)
                                else:
                                    last = pe.matmul(PS[hl * VD:(hl + 1) * VD, 6 + g % 2, :],
                                                     vS[:, j, 2 * (g - 2) + hl, :], probT[hl][:, j, :],
                                                     start=(j == 0), stop=(j == ST))
                    last.then_inc(ev("pv_mm"), 1)
            pe.wait_ge(ev("gated"), NT)
            for t in range(NT):
                if t < 2:
                    pe.wait_ge(ev("prob"), NATT)
                if t >= 4:
                    pe.wait_ge(ev("ot_v"), t - 3)
                for j in range(4):
                    last = pe.transpose(quad(t % 4)[:, j, :], oret[:, t, j * P:(j + 1) * P], ident)
                last.then_inc(ev("o_t"), 1)
            pe.wait_ge(ev("o_c"), 6)
            pe.wait_ge(ev("octx_c"), 4)
            pe.wait_ge(ev("ot_v"), NT)
            project_out(0, "ev_out", oT, lambda k: 2 * k if k < 4 else 2 * (k - 4) + 1)

            def moe(l):
                q = 2 * l + 1
                pe.wait_ge(ev("wo_ev"), KD * l + KD)
                norm_sums(q)
                pe.wait_ge(ev("wr_in"), 32 * (l + 1))
                for t in range(NT):
                    for k in range(KD):
                        if t in (0, ST):
                            pe.wait_ge(ev("h_s" if t < ST else "h_c"), KD * q + k + 1)
                        last = pe.matmul(PS[:, 0, t * ROUTE:(t + 1) * ROUTE], hT[:, k, t * P:t * P + P],
                                         wr[:, k, :], start=(k == 0), stop=(k == KD - 1))
                last.then_inc(ev("route_mm"), 1)
                for i in range(2 * NT):
                    t, half = i // 2, i % 2
                    if i >= 4:
                        pe.wait_ge(ev("htok_a"), 2 * NT * l + i - 3)
                    for j in range(4):
                        last = pe.transpose(quad((1, 2, 3, 7)[i % 4])[:, j, :],
                                            hT[:, 4 * half + j, t * P:t * P + P], ident)
                    last.then_inc(ev("htok_t"), 1)
                pe.wait_ge(ev("chosen"), l + 1)
                for t in range(NT):
                    for j in range(t + 1):
                        pe.matmul(PS[:, 5, t * EXPERTS:(t + 1) * EXPERTS], ones if j < t else tri, both[:, j, :],
                                  start=(j == 0), stop=(j == t))
                for j in range(NT):
                    last = pe.matmul(PS[:, 6, 0:EXPERTS], ones, both[:, j, :], start=(j == 0), stop=(j == NT - 1))
                last.then_inc(ev("rank_mm"), 1)
                pe.wait_ge(ev("htok_a"), 2 * NT * l + 2 * NT)
                for i in range(2 * RT):
                    j, half = i // 2, i % 2
                    if half == 0 and j % 2 == 0:
                        pe.wait_ge(ev(f"rows_back{j // 2}"), 16 * (l + 1))
                    if i >= 4:
                        pe.wait_ge(ev(("xs_v", "xs_a")[i % 2]), RT * l + (i - 4) // 2 + 1)
                    for m in range(4):
                        last = pe.transpose(quad(i % 4)[:, m, :], xback[:, j, (4 * half + m) * P:(4 * half + m + 1) * P],
                                            ident)
                    last.then_inc(ev("xs_t"), 1)
                pe.wait_ge(ev("xs_v"), RT * l + RT)
                pe.wait_ge(ev("xs_a"), RT * l + RT)
                pe.wait_ge(ev("pad"), l + 1)
                pe.wait_ge(ev("tab"), 4 * l + 4)
                n0 = at[(f"expert{l}", 0)]

                def expert(e, p, laps):
                    blocks = pe.value_load(tab[0:1, bass.ds(e + EXPERTS, 1)], min_val=1, max_val=MAXBLK)
                    before = pe.value_load(tab[0:1, bass.ds(e + 2 * EXPERTS, 1)], min_val=0, max_val=2 * ALLBLK)
                    s = [(n0 + PER_EXPERT * p + j) % SLOTS for j in range(PER_EXPERT)]
                    up = [ring[:, s[j], :].rearrange("p (k a n) -> p k a n", k=4, a=2) for j in range(2)]
                    down = ring[:, s[2], :].rearrange("p (k n) -> p k n", k=2)
                    with pe.Fori(0, blocks) as b:
                        pe.wait_ge(ev("xblk_c"), before + b + 1)
                        pe.wait_ge(ev("act"), before + b + 1)
                        for k in range(KD):
                            if k % 4 == 0:
                                pe.wait_ge(ring_full[s[k // 4]], laps(PER_EXPERT * p + k // 4))
                            for i in range(2):
                                last = pe.matmul(
                                    PS[i * BLK:(i + 1) * BLK, 0, 0:2 * P].rearrange("p (a n) -> p a n", a=2),
                                    xblk[:, k, :], up[k // 4][:, k % 4, :, i * P:(i + 1) * P],
                                    start=(k == 0), stop=(k == KD - 1))
                        last.then_inc(ev("up_mm"), 1)
                        pe.wait_ge(ev("act"), before + b + 2)
                        pe.transpose(PS[:, 1, 0:P], gact[:, :], ident).then_inc(ev("h_t"), 1)
                        pe.wait_ge(ring_full[s[2]], laps(PER_EXPERT * p + 2))
                        pe.wait_ge(ev("hblk_c"), before + b + 1)
                        pe.wait_ge(ev("yblk_c"), before + b + 1)
                        for i in range(2):
                            for c in range(2):
                                last = pe.matmul(PS[c * BLK:(c + 1) * BLK, 2, :], hblk[:, i, :],
                                                 down[:, i, c * 512:(c + 1) * 512], start=(i == 0), stop=(i == 1))
                        last.then_inc(ev("down_mm"), 1)

                rounds = EXPERTS // RING_EXPERTS
                with pe.Fori(0, rounds) as g:
                    for p in range(RING_EXPERTS):
                        expert(g * RING_EXPERTS + p, p, lambda c: g * 16 + full_count[n0 + c])
                for e in range(rounds * RING_EXPERTS, EXPERTS):
                    expert(e, e % RING_EXPERTS, lambda c: 16 * rounds + full_count[n0 + c])
                for i in range(2 * NT):
                    t, half = i // 2, i % 2
                    if half == 0:
                        pe.wait_ge(ev("comb_v"), NT * l + t + 1)
                    if i >= 4:
                        pe.wait_ge(ev("comb"), 2 * NT * l + i - 3)
                    for m in range(4):
                        c = (4 * half + m) * P
                        last = pe.transpose(quad(4 + i % 4)[:, m, :], ygat[:, t, c:c + P], ident)
                    last.then_inc(ev("comb_mm"), 1)

            moe(0)
            pe.wait_ge(ev("comb"), 2 * NT)
            norm_sums(2)

            def gated_in(j):
                arrived(("od_in", j))
                w = w_view(("od_in", j)).rearrange("p (k a n) -> p k a n", k=KD, a=2)
                if j >= 1:
                    pe.wait_ge(ev("sig"), 2 * j)
                    pe.wait_ge(ev("u_w"), 3 * j)
                for a in (1, 0):
                    for k in range(KD):
                        if j == 0 and a == 1:
                            pe.wait_ge(ev("h_s"), 2 * KD + k + 1)
                            pe.wait_ge(ev("h_c"), 2 * KD + k + 1)
                        for n in range(2):
                            last = pe.matmul(PS[:, 2 * a + n, 0:SEG], w[:, k, a, :], hT[:, k, n * SEG:(n + 1) * SEG],
                                             start=(k == 0), stop=(k == KD - 1))
                    if a == 1:
                        last.then_inc(ev("gate_mm"), 1)
                last.then_inc(ev("gate_mm"), 1)

            def taps(j):
                pe.wait_ge(ev("tap_d"), PE_TAPS * (j + 1))
                pe.wait_ge(ev("u_w"), 3 * (j + 1))
                if j == 0:
                    pe.wait_ge(ev("u_zero"), 1)
                else:
                    pe.wait_ge(ev("conv_v"), CONV_OPS * j)
                for w in range(PE_TAPS):
                    for n, (c0, c1) in enumerate(((0, HALF), (HALF, SPAN))):
                        last = pe.matmul(PS[:, 4 + n, 0:c1 - c0], tapd[:, j % 2, w, :], upad[:, j, w + c0:w + c1],
                                         start=(w == 0), stop=(w == PE_TAPS - 1))
                last.then_inc(ev("tap_mm"), 1)

            def ln_sums(src, k, b, name, count):
                pe.wait_ge(ev(name), count)
                for n, (c0, c1) in enumerate(((0, HALF), (HALF, SPAN))):
                    last = pe.matmul(PS[:, b + n, 0:c1 - c0], ones, src[:, k, c0:c1],
                                     start=(k == 0), stop=(k == KD - 1))
                last.then_inc(ev("ln_mm"), 1)

            gated_in(0)
            for j in range(KD):
                if j + 1 < KD:
                    gated_in(j + 1)
                taps(j)
                if j >= 1:
                    ln_sums(cv, j - 1, 6, "conv_v", CONV_OPS * j)
            ln_sums(cv, KD - 1, 6, "conv_v", CONV_OPS * KD)
            pe.wait_ge(ev("sig"), 2 * KD)
            pe.wait_ge(ev("u_w"), 3 * KD)
            for k in range(KD):
                ln_sums(cv2, k, 0, "ln_sq", k + 1)
            project_out(1, "od_out", cvn, lambda k: k)
            moe(1)
            pe.wait_ge(ev("comb"), 4 * NT)
            for i in range(2 * NT):
                t, half = i // 2, i % 2
                if i >= 4:
                    pe.wait_ge(ev(("xt_v", "xt_a")[i % 2]), NT + (i - 4) // 2 + 1)
                for j in range(4):
                    last = pe.transpose(quad(4 + i % 4)[:, j, :], xT[:, 4 * half + j, t * P:t * P + P], ident)
                last.then_inc(ev("x_t"), 1)

        @block.scalar
        def _(act):
            step = [0]

            def link(ins):
                step[0] += 1
                ins.then_inc(ev("act_step"), 1)
                act.wait_ge(ev("act_step"), step[0])

            n_param = [0]

            def param(dst, src):
                n_param[0] += 1
                act.dma_start(dst, src).then_inc(ev("params_in"), 16)

            param(cst[:, :], f["consts"])
            v = vrow
            for l in range(2):
                param(v[48 * l:48 * l + 48, 0, :], f["ada_b"][l].rearrange("(r n) -> r n", n=P))
            param(v[96:104, 0, :], f["c"][0].rearrange("(r n) -> r n", n=P))
            param(v[104:112, 0, :], f["c_ctx"].rearrange("(r n) -> r n", n=P))
            param(v[112:128, 0, :], f["norm_mix"].rearrange("l (r n) -> (l r) n", n=P))
            param(v[0:16, 1, :], f["norm_ffn"].rearrange("l (r n) -> (l r) n", n=P))
            param(v[16:24, 1, :], f["od_dw_b"][0].rearrange("(r n) -> r n", n=P))
            param(v[24:32, 1, :], f["od_ln_g"][0].rearrange("(r n) -> r n", n=P))
            param(v[32:40, 1, :], f["od_ln_b"][0].rearrange("(r n) -> r n", n=P))
            param(v[40:44, 1, :], f["ev_ret_gn"][0].rearrange("(r n) -> r n", n=P))
            param(v[44:46, 1, :], f["ev_q_a_norm"][0].rearrange("(r n) -> r n", n=P))
            dw = f["od_dw"][0].rearrange("w (r n) -> (w r) n", n=P)
            param(v[:, 2, :], dw[0:P, :])
            param(v[0:V_ROWS[3], 3, :], dw[P:, :])
            act.dma_start(xtok[:, 0:ST, :], f["x_sample"][0].rearrange("(t p) n -> p t n", p=P)).then_inc(ev("x_in"), 16)
            act.dma_start(xtok[:, ST, :], f["x_prompt"][0]).then_inc(ev("x_in"), 16)

            def late(dst, src):
                act.dma_start(dst, src).then_inc(ev("late_in"), 16)
            late(dist, f["distances"])
            late(dec[:, :], f["ev_ret_decay"][0].rearrange("d h -> (d h)").partition_broadcast(P))
            late(kvg[:, :], f["ev_kv_a_norm"][0].partition_broadcast(P))
            late(qkg[:, 0, :], f["ev_q_norm"][0].partition_broadcast(P))
            late(qkg[:, 1, :], f["ev_k_norm"][0].partition_broadcast(P))
            late(cache_in[:, 0:KVRANK], f["cache_mla_ckv"][0, 0])
            late(cache_in[:, KVRANK:], f["cache_mla_krope"][0, 0])
            for l in range(2):
                late(rb[:, l, 0:GROUPS], f["moe_b_group"][l].partition_broadcast(P))
                late(rb[:, l, GROUPS:], f["moe_b_expert"][l].partition_broadcast(P))

            def router_weights(l):
                act.dma_start(wr[:, :, 0:GROUPS], f["moe_w_group"][l].rearrange("(k p) n -> p k n", p=P)) \
                    .then_inc(ev("wr_in"), 16)
                act.dma_start(wr[:, :, GROUPS:], f["moe_w_expert"][l].rearrange("(k p) n -> p k n", p=P)) \
                    .then_inc(ev("wr_in"), 16)
            router_weights(0)

            act.wait_ge(ev("vec_c"), 4)
            act.wait_ge(ev("sc_zero"), 1)
            act.activation(scT[:, :, 0:2].rearrange("p k a -> p a k"),
                           vecT[:, 0, V_COND:V_COND + 16].rearrange("p (a k) -> p a k", a=2),
                           ACT.Silu).then_inc(ev("sc_ready"), 1)
            act.dma_start(rows_out[ROWS:XW, 0:C_ID + P], cst[0:BLK, C_ID:C_ID + P]).then_inc(ev("y_sent"), 16)
            for i in range(1, 2 * NT, 2):
                act.wait_ge(ev("x_t"), i + 1)
                act.activation(xT[:, 4:8, (i // 2) * P:(i // 2 + 1) * P], quad(i % 4), ACT.Copy).then_inc(ev("xt_a"), 1)

            def mod_rows(g):
                act.wait_ge(ev("mod_mm"), KD * (g + 1))
                if g >= 1:
                    act.wait_ge(ev("mod_t"), g)
                act.activation(mrow, PS[:, 7, :], ACT.Copy).then_inc(ev("mrow_c"), 1)

            def norm(q, ready):
                l = q // 2
                for k in range(KD):
                    ready(k)
                    act.activation(squares(q)[:, k, :], xT[:, k, :], ACT.Square).then_inc(ev("squared"), 1)
                act.wait_ge(ev("sumsq"), q + 1)
                act.activation(rs[:, 0:SAMPLE], PS[:, 4, :], ACT.Sqrt, bias=eps, scale=1.0 / D).then_inc(ev("root"), 1)
                act.activation(rs[:, SAMPLE:T], PS[:, 6, 0:CONTEXT], ACT.Sqrt, bias=eps, scale=1.0 / D) \
                    .then_inc(ev("root"), 1)
                if q == 0:
                    mod_rows(0)
                act.wait_ge(ev("coef"), q + 1)
                for k in range(KD):
                    act.wait_ge(ev("hn"), 2 * KD * q + 2 * k + 1)
                    act.activation(hT[:, k, 0:SAMPLE], hT[:, k, 0:SAMPLE], ACT.Identity,
                                   bias=modT[:, l, 24 * (q % 2) + k, 0:1], scale=modA[:, q, k, 0:1]) \
                        .then_inc(ev("h_s"), 1)

            def x_ready(k):
                if k == 0:
                    act.wait_ge(ev("xt_v"), NT)
                    act.wait_ge(ev("xt_a"), NT)
            norm(0, x_ready)
            for i in range(1, 8 * NT, 2):
                c, t = i // NT, i % NT
                if i == 5 * NT:
                    mod_rows(1)
                n = min(256, EVEN_IN - 256 * c)
                act.wait_ge(ev("z_mm"), i + 1)
                act.activation(z[:, t, 256 * c:256 * c + n], PS[:, i % 4, 0:n], ACT.Copy).then_inc(ev("z_a"), 1)
            mod_rows(2)
            act.dma_start(states[0:RK, 0, :, :], f["state_retention"][0, 0, 0].rearrange("h k v -> k h v")) \
                .then_inc(ev("state_in"), 16)
            act.dma_start(states[RK:P, ST - 1, :, :], f["state_retention"][0, 0, 1].rearrange("h k v -> k h v")) \
                .then_inc(ev("state_in"), 16)
            act.wait_ge(ev("late_in"), 16 * 11)
            link(act.activation(decw[:, 0, :], dec[:, :], ACT.Abs))
            link(act.activation(decw[:, 1, :], decw[:, 0, :], ACT.Exp, scale=-1.0))
            act.activation(decw[:, 2, :], decw[:, 1, :], ACT.Ln, bias=1.0).then_inc(ev("ln_dec"), 1)
            act.wait_ge(ev("edge_arg"), 6)
            act.activation(edge[:, :, :], edge[:, :, :], ACT.Exp).then_inc(ev("edge_e"), 1)
            for h in range(RH):
                for d in range(2):
                    a = D_A1 if d == 0 else D_A2
                    act.activation(mtmp[:, 2 * h + d, :], dist[:, a:a + P], ACT.Exp,
                                   scale=dec[:, d * RH + h:d * RH + h + 1]).then_inc(ev("mask_e"), 1)
            act.wait_ge(ev("z_v"), 4 * NT)
            act.wait_ge(ev("z_a"), 4 * NT)
            act.wait_ge(ev("mask_v"), RH)
            for t in range(NT):
                act.activation(oret[:, t, :], oret[:, t, :], ACT.Silu).then_inc(ev("silu_g"), 1)
            for t in range(NT):
                link(act.activation(qksq[:, 0, 0:QRANK], z[:, t, 0:QRANK], ACT.Square, accum_out=ss[:, 0, t:t + 1]))
                link(act.activation(qksq[:, 0, 0:KVRANK], z[:, t, QRANK:Z_KR], ACT.Square,
                                    accum_out=ss[:, 0, 8 + t:9 + t]))
            act.activation(ss[:, 1, 0:NT], ss[:, 0, 0:NT], ACT.Sqrt, bias=eps, scale=1.0 / QRANK) \
                .then_inc(ev("lat_root"), 1)
            act.activation(ss[:, 1, 8:8 + NT], ss[:, 0, 8:8 + NT], ACT.Sqrt, bias=eps, scale=1.0 / KVRANK) \
                .then_inc(ev("lat_root"), 1)
            mod_rows(3)
            for t in range(NT):
                if t == 3:
                    mod_rows(4)
                act.wait_ge(ev("rq_t"), t + 1)
                if t >= 1:
                    act.wait_ge(ev("rs_mm"), t)
                act.activation(rqT, quad(0)[0:RK], ACT.Copy).then_inc(ev("rq_c"), 1)
                if t < ST:
                    act.wait_ge(ev("qfb_t"), t + 1)
                    if t >= 1:
                        act.wait_ge(ev("ro_mm"), t)
                    act.activation(qfbT, quad(2), ACT.Copy).then_inc(ev("qfb_c"), 1)
                act.wait_ge(ev("gn_v"), t + 1)
                act.activation(rmv[:, :], mv[:, :, 1], ACT.Sqrt, bias=eps).then_inc(ev("gn_root"), 1)
            for u, (kind, t) in enumerate(UNITS):
                raw = qkraw[:, u % 2, :].rearrange("p (h n) -> p h n", h=HEADS)
                act.wait_ge(ev("qk_mm"), u + 1)
                if u >= 2:
                    act.wait_ge(ev("hd_t"), u - 1)
                b = 2 * (u % 2)
                for half in range(2):
                    if kind == "q":
                        ins = act.activation(raw[:, 4 * half:4 * half + 4, :],
                                             PS[:, b + half, 0:384].rearrange("p (h n) -> p h n", h=4), ACT.Copy)
                    else:
                        ins = act.activation(raw[:, 4 * half:4 * half + 4, 0:NOPE],
                                             quad(b + half)[:, :, 0:NOPE], ACT.Copy)
                    if half == 0:
                        link(ins)
                ins.then_inc(ev("raw_a"), 1)
                act.wait_ge(ev("raw_a"), u + 1)
                if kind == "k":
                    act.wait_ge(ev("kr_p"), t + 1)
                if u >= 1:
                    act.wait_ge(ev("hsum"), u)
                act.activation(qksq[:, 0, :], qkraw[:, u % 2, :], ACT.Square).then_inc(ev("qk_sq"), 1)
                act.wait_ge(ev("hsum"), u + 1)
                act.activation(ss[:, 1, 0:HEADS], ss[:, 0, 0:HEADS], ACT.Sqrt, bias=eps, scale=1.0 / QK) \
                    .then_inc(ev("hroot"), 1)
                if u >= 1:
                    k2, t2 = UNITS[u - 1]
                    col = t2 * P if k2 == "q" else KCOL[t2]
                    dst = qT if k2 == "q" else kT
                    act.wait_ge(ev("hd_t"), u)
                    if u == 2:
                        act.wait_ge(ev("side_out"), 64)
                    act.activation(dst[:, 0:4, col:col + P], quad(4)[0:QK], ACT.Copy).then_inc(ev("hd_a"), 1)
            act.wait_ge(ev("hd_t"), len(UNITS))
            act.activation(kT[:, 0:4, KCOL[NT]:KCOL[NT] + P], quad(4)[0:QK], ACT.Copy).then_inc(ev("hd_a"), 1)
            mod_rows(5)
            for i in range(NATT + 3):
                if i < NATT:
                    act.wait_ge(ev("nmax"), i + 1)
                    if i >= 2:
                        act.wait_ge(ev("p_t"), i - 1)
                    if ATT[i][0] == "lat":
                        act.activation(prob[i % 2],
                                       PS[:, 2 * (i % 2):2 * (i % 2) + 2, 0:SEG],
                                       ACT.Exp, bias=nmx[:, i % 2:i % 2 + 1], accum_out=den[:, i % 2:i % 2 + 1]) \
                            .then_inc(ev("prob"), 1)
                    else:
                        act.activation(prob[i % 2][:, 0:4, :], prob[i % 2][:, 0:4, :], ACT.Exp) \
                            .then_inc(ev("prob"), 1)
                if 2 <= i <= NATT + 1:
                    kind, h, t = ATT[i - 2]
                    act.wait_ge(ev("p_t"), i - 1)
                    if kind == "lat":
                        act.wait_ge(ev("pv_mm"), groups_before(i - 2))
                        act.activation(probT[h % 2][:, 0:4, t * P:t * P + P], quad(4), ACT.Copy) \
                            .then_inc(ev("pt_a"), 1)
                    else:
                        act.activation(probT[0][:, h, :], PS[:, 4, :], ACT.Copy).then_inc(ev("pt_a"), 1)
                if i - 3 in GROUP_END:
                    g = GROUP_END[i - 3]
                    act.wait_ge(ev("pv_mm"), g + 1)
                    if g < 2:
                        act.activation(octx[:, 2 * g:2 * g + 2, :],
                                       PS[:, 6 + g % 2, 0:2 * P].rearrange("p (k t) -> p k t", k=2), ACT.Copy) \
                            .then_inc(ev("o_c"), 1)
                    else:
                        act.activation(oT[:, 2 * (g - 2), 0:SAMPLE], PS[:, 6 + g % 2, :], ACT.Copy) \
                            .then_inc(ev("o_c"), 1)

            def moe(l):
                q = 2 * l + 1
                norm(q, lambda k: act.wait_ge(ev("wo_ev"), KD * l + k + 1))
                act.wait_ge(ev("gdiff"), l + 1)
                act.activation(rt[:, 0, :, 0:GROUPS], rt[:, 0, :, 0:GROUPS], ACT.Exp).then_inc(ev("gexp"), 1)
                for i in range(2 * NT):
                    t, half = i // 2, i % 2
                    act.wait_ge(ev("htok_t"), 2 * NT * l + i + 1)
                    act.activation(htok[:, t, 512 * half:512 * half + 512], PS[:, (1, 2, 3, 7)[i % 4], :], ACT.Copy) \
                        .then_inc(ev("htok_a"), 1)
                    if i == 3:
                        act.wait_ge(ev("ediff"), l + 1)
                        act.activation(r1[:, 4, :], r1[:, 4, :], ACT.Exp).then_inc(ev("eexp"), 1)
                act.wait_ge(ev("rows_sent"), 16 * 2 * NT * (l + 1))
                for j in range(RT // 2):
                    act.dma_start(xback[:, 2 * j:2 * j + 2, :],
                                  rows_in[2 * j * P:(2 * j + 2) * P, :].rearrange("(j p) n -> p j n", p=P)) \
                        .then_inc(ev(f"rows_back{j}"), 16)
                for i in range(1, 2 * RT, 2):
                    j = i // 2
                    act.wait_ge(ev("xs_t"), 2 * RT * l + i + 1)
                    act.activation(xsT[:, 4:8, j * P:(j + 1) * P], quad(i % 4), ACT.Copy).then_inc(ev("xs_a"), 1)
                act.wait_ge(ev("tab"), 4 * l + 4)

                with act.Fori(0, EXPERTS) as e:
                    off = act.value_load(tab[0:1, bass.ds(e, 1)], min_val=0, max_val=ROWS)
                    blocks = act.value_load(tab[0:1, bass.ds(e + EXPERTS, 1)], min_val=1, max_val=MAXBLK)
                    before = act.value_load(tab[0:1, bass.ds(e + 2 * EXPERTS, 1)], min_val=0, max_val=2 * ALLBLK)
                    with act.Fori(0, blocks) as b:
                        act.wait_ge(ev("up_mm"), before + b + 2)
                        act.wait_ge(ev("act"), before + b + 1)
                        act.activation(gsil[:, :], PS[:, 0, 0:P], ACT.Silu).then_inc(ev("silu"), 1)
                        act.wait_ge(ev("down_mm"), before + b + 2)
                        act.wait_ge(ev("y_sent"), (before + b) * 32 + 16)
                        act.activation(yblk[:, :], PS[:, 2, :], ACT.Copy).then_inc(ev("yblk_c"), 1)
                        row = act.snap(nc.s_assert_within(
                            off + b * BLK, 0, ROWS,
                            skip_runtime_bounds_check_because="a further block starts inside the expert's rows"))
                        act.wait_ge(ev("yblk_c"), before + b + 2)
                        for c in range(2):
                            act.dma_start(rows_out[bass.ds(row, BLK), c * 512:(c + 1) * 512],
                                          yblk[c * BLK:(c + 1) * BLK, :]).then_inc(ev("y_sent"), 16)
                    act.activation(tick[:, 0:1], eps, ACT.Copy).then_inc(ev("expert_done"), 1)
                total = act.value_load(tab[0:1, 3 * EXPERTS:3 * EXPERTS + 1], min_val=EXPERTS, max_val=2 * ALLBLK)
                act.wait_ge(ev("y_sent"), total * 32 + 16)
                act.activation(tick[:, 2:3], eps, ACT.Copy).then_inc(ev("results_sent"), 1)
                for t in range(NT):
                    act.wait_ge(ev(f"picked{t}"), 32 * (l + 1))
                    act.activation(ygat[:, t, :], ygat[:, t, :], ACT.Copy, scale=wtok[:, 0, t:t + 1]) \
                        .then_inc(ev("y0_w"), 1)
                if l == 0:
                    act.wait_ge(ev("route_mm"), 1)
                    router_weights(1)

            moe(0)
            norm(2, lambda k: act.wait_ge(ev("comb"), 2 * NT))
            for j in range(KD):
                act.wait_ge(ev("gate_mm"), 2 * j + 1)
                if j >= 1:
                    act.wait_ge(ev("u_w"), 3 * j)
                for n in range(2):
                    act.activation(rs[:, n * SEG:(n + 1) * SEG], PS[:, 2 + n, 0:SEG], ACT.Sigmoid) \
                        .then_inc(ev("sig"), 1)
            for k in range(KD):
                act.wait_ge(ev("ln_d"), 2 * (k + 1))
                act.activation(cv2[:, k, :], cv[:, k, :], ACT.Square).then_inc(ev("ln_sq"), 1)
            act.wait_ge(ev("ln_mm"), 2 * KD)
            for n, (c0, c1) in enumerate(((0, HALF), (HALF, SPAN))):
                act.activation(scratch[:, c0:c1], PS[:, n, 0:c1 - c0], ACT.Sqrt, bias=eps, scale=1.0 / CONV) \
                    .then_inc(ev("ln_root"), 1)
            for k in range(KD):
                act.wait_ge(ev("ln_n"), 2 * (k + 1))
                act.activation(cvn[:, k, :], cvn[:, k, :], ACT.Silu,
                               bias=vecT[:, 1, V_LNB + k:V_LNB + k + 1],
                               scale=vecT[:, 1, V_LNG + k:V_LNG + k + 1]).then_inc(ev("act1"), 1)
            moe(1)
            for i in range(1, 2 * NT, 2):
                t = i // 2
                act.wait_ge(ev("x_t"), 2 * NT + i + 1)
                act.activation(xtok[:, t, 512:D], PS[:, 4 + i % 4, :], ACT.Copy).then_inc(ev("xt_a"), 1)

        @block.vector
        def _(dve):
            step = [0]

            def link(ins):
                step[0] += 1
                ins.then_inc(ev("dve_step"), 1)
                dve.wait_ge(ev("dve_step"), step[0])

            def tt(out, a, b, op):
                return dve.tensor_tensor(out, a, b, op)

            dve.wait_ge(ev("vec_t"), 1)
            for g, r in enumerate(V_ROWS):
                dve.tensor_copy(vecT[:, g, 0:r], PS[:, 5, g * P:g * P + r]).then_inc(ev("vec_c"), 1)
            for i in range(0, 2 * NT, 2):
                dve.wait_ge(ev("x_t"), i + 1)
                dve.tensor_copy(xT[:, 0:4, (i // 2) * P:(i // 2 + 1) * P], quad(i % 4)).then_inc(ev("xt_v"), 1)

            def mod_bias(g):
                dve.wait_ge(ev("mod_t"), g + 1)
                bias = vecT[:, 0, 16 * g:16 * g + 16].rearrange("p (c q) -> p c q", c=4).unsqueeze(3)
                out = modT[:, g // 3, 16 * (g % 3):16 * (g % 3) + 16, :].rearrange("p (c q) a -> p c q a", c=4)
                src = quad(5 if g == 0 else 6).rearrange("p q (c a) -> p c q a", c=4)[:, :, :, 0:2]
                tt(out, src, bc(bias, [P, 4, 4, 2]), ALU.add).then_inc(ev("mod_c"), 1)

            def coef(q):
                l = q // 2
                base = (V_NMIX if q % 2 == 0 else V_NFFN) + 8 * l
                g = vecT[:, q % 2, base:base + KD].unsqueeze(2)
                s = 24 * (q % 2) + 8
                dve.scalar_tensor_tensor(out=modA[:, q, :, :], in0=modT[:, l, s:s + KD, :], scalar=1.0,
                                         in1=bc(g, [P, KD, 2]), op0=ALU.add, op1=ALU.mult).then_inc(ev("coef"), 1)

            def normed(q):
                dve.wait_ge(ev("root"), 2 * q + 2)
                link(dve.reciprocal(PS[:, 4, :], rs[:, 0:SAMPLE]))
                link(dve.reciprocal(PS[:, 6, 0:CONTEXT], rs[:, SAMPLE:T]))
                for k in range(KD):
                    tt(hT[:, k, 0:SAMPLE], xT[:, k, 0:SAMPLE], PS[:, 4, :], ALU.mult).then_inc(ev("hn"), 1)
                    tt(hT[:, k, SAMPLE:T], xT[:, k, SAMPLE:T], PS[:, 6, 0:CONTEXT], ALU.mult).then_inc(ev("hn"), 1)

            dve.wait_ge(ev("xt_a"), NT)
            dve.wait_ge(ev("xt_v"), NT)
            normed(0)
            mod_bias(0)
            dve.wait_ge(ev("mod_c"), 1)
            coef(0)
            for i in range(0, 8 * NT, 2):
                c, t = i // NT, i % NT
                if i == 5 * NT + 1:
                    mod_bias(1)
                n = min(256, EVEN_IN - 256 * c)
                dve.wait_ge(ev("z_mm"), i + 1)
                dve.tensor_copy(z[:, t, 256 * c:256 * c + n], PS[:, i % 4, 0:n]).then_inc(ev("z_v"), 1)
            dve.wait_ge(ev("ln_dec"), 1)
            link(dve.scalar_tensor_tensor(out=dec[:, :], in0=dec[:, :], scalar=0.0, in1=decw[:, 2, :],
                                          op0=ALU.min, op1=ALU.subtract))
            for n, d in enumerate((0, 0, 1, 1)):
                dve.tensor_scalar(edge[:, n, :], dec[:, d * RH:(d + 1) * RH], cst[:, C_POS + n:C_POS + n + 1], None,
                                  ALU.mult).then_inc(ev("edge_arg"), 1)
            for d in range(2):
                dve.tensor_scalar(edge[:, 4 + d, :], dec[:, d * RH:(d + 1) * RH], float(P), None, ALU.mult) \
                    .then_inc(ev("edge_arg"), 1)
            dve.wait_ge(ev("edge_e"), 1)
            link(dve.tensor_scalar(edge[:, 0, :], edge[:, 0, :], RK ** -0.5, None, ALU.mult))
            link(dve.tensor_scalar(edge[:, 2, :], edge[:, 2, :], RK ** -0.5, None, ALU.mult))
            for h in range(RH):
                dve.wait_ge(ev("mask_e"), 2 * h + 2)
                link(tt(mtmp[:, 2 * h, :], mtmp[:, 2 * h, :], dist[:, D_U:D_U + P], ALU.mult))
                link(tt(mtmp[:, 2 * h + 1, :], mtmp[:, 2 * h + 1, :], dist[:, D_L:D_L + P], ALU.mult))
                link(tt(mtmp[:, 2 * h, :], mtmp[:, 2 * h, :], mtmp[:, 2 * h + 1, :], ALU.add))
                dve.tensor_scalar(mask[:, h, :], mtmp[:, 2 * h, :], RK ** -0.5, None, ALU.mult).then_inc(ev("mask_v"), 1)
            dve.wait_ge(ev("z_a"), 4 * NT)
            dve.wait_ge(ev("z_v"), 4 * NT)

            def by_edge(out, t, off, n):
                src = z[:, t, off:off + RH * RK].rearrange("p (h n) -> p h n", h=RH)
                return tt(out, src, bc(edge[:, n, :].unsqueeze(2), [P, RH, RK]), ALU.mult)

            def state_row(t):
                if t == 0:
                    dve.wait_ge(ev("state_in"), 32)
            for t in range(NT):
                if t >= 1:
                    dve.wait_ge(ev("upd_mm"), t)
                link(by_edge(kfb[:, :, 0:RK], t, Z_RK, 0))
                by_edge(kfb[:, :, RK:P], t, Z_RK, 2).then_inc(ev("kfb"), 1)
                dve.wait_ge(ev("upd_mm"), t + 1)
                dve.tensor_copy(upd[:, t, :, :], quad(t % 2)).then_inc(ev("upd_c"), 1)
                if t in (0, NT - 1):
                    mod_bias(2 if t == 0 else 3)
            dve.wait_ge(ev("state_in"), 32)
            dve.wait_ge(ev("upd_c"), NT)
            for j in range(ST - 1):
                for h in range(RH):
                    ins = dve.scalar_tensor_tensor(
                        out=states[0:RK, j + 1, h, :], in0=states[0:RK, j, h, :], scalar=edge[0:RK, 4, h:h + 1],
                        in1=upd[0:RK, j, h, :], op0=ALU.mult, op1=ALU.add)
                r = ST - 1 - j
                for h in range(RH):
                    ins = dve.scalar_tensor_tensor(
                        out=states[RK:P, r - 1, h, :], in0=states[RK:P, r, h, :], scalar=edge[RK:P, 5, h:h + 1],
                        in1=upd[RK:P, r, h, :], op0=ALU.mult, op1=ALU.add)
                ins.then_inc(ev("states"), 1)
                dve.wait_ge(ev("states"), j + 1)
            dve.wait_ge(ev("mask_v"), RH)
            for t in range(NT):
                if t < ST:
                    if t >= 1:
                        dve.wait_ge(ev("qfb_t"), t)
                    link(by_edge(qfb[:, :, 0:RK], t, Z_RQ, 1))
                    by_edge(qfb[:, :, RK:P], t, Z_RQ, 3).then_inc(ev("qfb"), 1)
                dve.wait_ge(ev("rk_t"), t + 1)
                if t >= 1:
                    dve.wait_ge(ev("rs_mm"), t)
                dve.tensor_copy(rkT, quad(1)[0:RK]).then_inc(ev("rk_c"), 1)
                if t == 3:
                    mod_bias(4)
                dve.wait_ge(ev("rs_mm"), t + 1)
                if t >= 1:
                    dve.wait_ge(ev("ro_mm"), t)
                tt(rsc, quad(3), mask[:, :, :], ALU.mult).then_inc(ev("rsc"), 1)
                dve.wait_ge(ev("ro_mm"), t + 1)
                for h in range(RH):
                    link(dve.bn_stats(stat[:, h, :], quad(4)[:, h, :]))
                for h in range(RH):
                    ins = dve.bn_aggr(mv[:, h, :], stat[:, h, :])
                ins.then_inc(ev("gn_v"), 1)
                dve.wait_ge(ev("gn_root"), t + 1)
                link(dve.reciprocal(mv[:, :, 1], rmv[:, :]))
                for h in range(RH):
                    ins = dve.tensor_scalar(onrm[:, h, :], quad(4)[:, h, :], mv[:, h, 0:1], mv[:, h, 1:2],
                                            ALU.subtract, ALU.mult)
                ins.then_inc(ev("onrm"), 1)
                dve.wait_ge(ev("onrm"), t + 1)
                dve.wait_ge(ev("silu_g"), t + 1)
                tt(oret[:, t, :], oret[:, t, :], arena[:, A_V + 1536:A_V + 2048], ALU.mult).then_inc(ev("gated"), 1)
                dve.wait_ge(ev("gated"), t + 1)
            dve.wait_ge(ev("lat_root"), 2)
            link(dve.reciprocal(ss[:, 1, 0:NT], ss[:, 1, 0:NT]))
            link(dve.reciprocal(ss[:, 1, 8:8 + NT], ss[:, 1, 8:8 + NT]))
            for t in range(NT):
                dve.tensor_scalar(z[:, t, 0:QRANK], z[:, t, 0:QRANK], ss[:, 1, t:t + 1], None, ALU.mult)
                dve.scalar_tensor_tensor(out=z[:, t, QRANK:Z_KR], in0=z[:, t, QRANK:Z_KR],
                                         scalar=ss[:, 1, 8 + t:9 + t], in1=kvg[:, :],
                                         op0=ALU.mult, op1=ALU.mult).then_inc(ev("lat_n"), 1)
            link(dve.tensor_scalar(qkg[:, 0, :], qkg[:, 0, :], QK ** -0.5, None, ALU.mult))
            tt(tick[:, 0:1], cst[:, 0:1], cst[:, 0:1], ALU.mult).then_inc(ev("qkg_s"), 1)
            for t in range(NT + 1):
                dve.wait_ge(ev("lat_t"), t + 1)
                b = 5 + t % 2
                if t < NT:
                    for j in range(2):
                        dve.tensor_scalar(cT[:, t, j, :], quad(b)[:, j, :], vecT[:, 1, V_QA + j:V_QA + j + 1], None,
                                          ALU.mult)
                    dve.tensor_copy(cT[:, t, 2, :], quad(b)[:, 2, :]).then_inc(ev("lat_c"), 1)
                else:
                    dve.tensor_copy(cache_cT[:, :], quad(b)[:, 0, :]).then_inc(ev("lat_c"), 1)
            for u, (kind, t) in enumerate(UNITS):
                raw = qkraw[:, u % 2, :].rearrange("p (h n) -> p h n", h=HEADS)
                b = 2 * (u % 2)
                if kind == "k":
                    dve.wait_ge(ev("raw_a"), u + 1)
                    for half in range(2):
                        ins = dve.tensor_copy(vS[:, VROW[t], 4 * half:4 * half + 4, :],
                                              quad(b + half)[:, :, NOPE:NOPE + VD])
                    ins.then_inc(ev("v_c"), 1)
                dve.wait_ge(ev("qk_sq"), u + 1)
                dve.tensor_reduce(ss[:, 0, 0:HEADS], qksq[:, 0, :].rearrange("p (h n) -> p h n", h=HEADS), AX.X,
                                  ALU.add).then_inc(ev("hsum"), 1)
                dve.wait_ge(ev("hroot"), u + 1)
                link(dve.reciprocal(ss[:, 0, 8:16], ss[:, 1, 0:HEADS]))
                tt(raw, raw, bc(ss[:, 0, 8:16].unsqueeze(2), [P, HEADS, QK]), ALU.mult).then_inc(ev("qk_r"), 1)
                if u >= 1:
                    k2, t2 = UNITS[u - 1]
                    col = t2 * P if k2 == "q" else KCOL[t2]
                    dst = qT if k2 == "q" else kT
                    dve.wait_ge(ev("hd_t"), u)
                    if u == 2:
                        dve.wait_ge(ev("side_out"), 64)
                    dve.tensor_copy(dst[:, 4:8, col:col + P], quad(5)[0:QK]).then_inc(ev("hd_v"), 1)
            dve.wait_ge(ev("hd_t"), len(UNITS))
            dve.tensor_copy(kT[:, 4:8, KCOL[NT]:KCOL[NT] + P], quad(5)[0:QK]).then_inc(ev("hd_v"), 1)
            mod_bias(5)
            dve.wait_ge(ev("mod_c"), 6)
            coef(1)
            coef(2)
            coef(3)
            for i in range(NATT + 3):
                if i >= 3 and ATT[i - 3][0] == "lat":
                    kind, h, t = ATT[i - 3]
                    dve.wait_ge(ev("p_t"), i - 2)
                    dve.wait_ge(ev("pv_mm"), groups_before(i - 3))
                    dve.tensor_copy(probT[h % 2][:, 4, t * P:t * P + P], quad(5)[:, 0, :]).then_inc(ev("pt_v"), 1)
                if i < NATT:
                    dve.wait_ge(ev("s_mm"), i + 1)
                    if i >= 2:
                        dve.wait_ge(ev("prob"), i - 1)
                    if ATT[i][0] == "lat":
                        dve.tensor_reduce(nmx[:, i % 2:i % 2 + 1], PS[:, 2 * (i % 2):2 * (i % 2) + 2, 0:SEG], AX.XY,
                                          ALU.max, negate=True).then_inc(ev("nmax"), 1)
                    else:
                        link(dve.tensor_reduce(cmx[:, i, :], quad(2 * i), AX.X, ALU.max, negate=True))
                        tt(prob[i][:, 0:4, :], quad(2 * i), bc(cmx[:, i, :].unsqueeze(2), [P, 4, P]), ALU.add) \
                            .then_inc(ev("nmax"), 1)
                if 1 <= i <= NATT:
                    b = (i - 1) % 2
                    dve.wait_ge(ev("prob"), i)
                    if ATT[i - 1][0] == "lat":
                        link(dve.reciprocal(rden[:, b:b + 1], den[:, b:b + 1]))
                        dve.tensor_scalar(prob[b], prob[b], rden[:, b:b + 1], None, ALU.mult) \
                            .then_inc(ev("prob_n"), 1)
                    else:
                        p4 = prob[b][:, 0:4, :]
                        link(dve.tensor_reduce(cmx[:, b, :], p4, AX.X, ALU.add))
                        link(dve.reciprocal(cmx[:, b, :], cmx[:, b, :]))
                        tt(p4, p4, bc(cmx[:, b, :].unsqueeze(2), [P, 4, P]), ALU.mult).then_inc(ev("prob_n"), 1)
            for t in range(NT):
                dve.wait_ge(ev("o_t"), t + 1)
                for j in range(4):
                    ins = dve.tensor_scalar(oT[:, 2 * j + 1, t * P:t * P + P], quad(t % 4)[:, j, :],
                                            vecT[:, 1, V_GN + j:V_GN + j + 1], None, ALU.mult)
                ins.then_inc(ev("ot_v"), 1)

            def add_out(l):
                for m in range(KD):
                    dve.wait_ge(ev("wo_mm"), KD * l + m + 1)
                    b = 4 + 2 * (m % 2)
                    for n, c0, c1, who in ((0, 0, SEG, 0), (1, SEG, SAMPLE, 0), (1, SAMPLE, T, 1)):
                        last = dve.scalar_tensor_tensor(
                            out=xT[:, m, c0:c1], in0=PS[:, b + n, c0 - n * SEG:c1 - n * SEG],
                            scalar=modT[:, l, 16 + m, who:who + 1], in1=xT[:, m, c0:c1], op0=ALU.mult, op1=ALU.add)
                    last.then_inc(ev("wo_ev"), 1)
            add_out(0)

            def moe(l):
                q = 2 * l + 1
                dve.wait_ge(ev("wo_ev"), KD * l + KD)
                normed(q)
                dve.wait_ge(ev("route_mm"), l + 1)
                link(tt(lgt[:, :, :], PS[:, 0, 0:NT * ROUTE].rearrange("p (t n) -> p t n", t=NT),
                        bc(rb[:, l, :].unsqueeze(1), [P, NT, ROUTE]), ALU.add))
                lg = lgt[:, :, 0:GROUPS]
                le = lgt[:, :, GROUPS:ROUTE]
                g4 = [P, NT, GROUPS]
                g8 = [P, NT, PER]
                g48 = [P, NT, GROUPS, PER]

                def w4(i):
                    return rt[:, i, :, 0:GROUPS]

                def w8(i):
                    return rt[:, i, :, :]

                def col(i, n):
                    return bc(r1[:, i, :].unsqueeze(2), [P, NT, n])

                link(dve.tensor_reduce(r1[:, 0, :], lg, AX.X, ALU.max))
                tt(w4(0), lg, col(0, GROUPS), ALU.subtract).then_inc(ev("gdiff"), 1)
                link(tt(w4(1), lg, col(0, GROUPS), ALU.is_equal))
                link(tt(w4(1), w4(1), bc(cst[:, C_PRI4:C_PRI4 + GROUPS].unsqueeze(1), g4), ALU.mult))
                link(dve.tensor_reduce(r1[:, 1, :], w4(1), AX.X, ALU.max))
                link(tt(w4(2), w4(1), col(1, GROUPS), ALU.is_equal))
                b48 = both[:, :, :].rearrange("p t (g e) -> p t g e", g=GROUPS)
                for t in range(NT):
                    ins = tt(b48[:, t], le[:, t].rearrange("p (g e) -> p g e", g=GROUPS),
                             bc(w4(2)[:, t].unsqueeze(2), [P, GROUPS, PER]), ALU.mult)
                link(ins)
                link(dve.tensor_reduce(w8(3), b48.rearrange("p t g e -> p t e g"), AX.X, ALU.add))
                for src, mx, eq, hot in ((3, 2, 4, 5), (6, 3, 7, 8)):
                    link(dve.tensor_reduce(r1[:, mx, :], w8(src), AX.X, ALU.max))
                    link(tt(w8(eq), w8(src), col(mx, PER), ALU.is_equal))
                    link(tt(w8(eq), w8(eq), bc(cst[:, C_PRI8:C_PRI8 + PER].unsqueeze(1), g8), ALU.mult))
                    link(dve.tensor_reduce(r1[:, 5, :], w8(eq), AX.X, ALU.max))
                    link(tt(w8(hot), w8(eq), col(5, PER), ALU.is_equal))
                    if src == 3:
                        link(dve.scalar_tensor_tensor(out=w8(6), in0=w8(5), scalar=-3.0e38, in1=w8(3),
                                                      op0=ALU.mult, op1=ALU.add))
                tt(r1[:, 4, :], r1[:, 3, :], r1[:, 2, :], ALU.subtract).then_inc(ev("ediff"), 1)
                for c in range(2):
                    o48 = one32[:, c, :, :].rearrange("p t (g e) -> p t g e", g=GROUPS)
                    for t in range(NT):
                        ins = tt(o48[:, t], bc(w4(2)[:, t].unsqueeze(2), [P, GROUPS, PER]),
                                 bc(w8(5 + 3 * c)[:, t].unsqueeze(1), [P, GROUPS, PER]), ALU.mult)
                    link(ins)
                tt(both[:, :, :], one32[:, 0, :, :], one32[:, 1, :, :], ALU.add).then_inc(ev("chosen"), 1)
                dve.wait_ge(ev("gexp"), l + 1)
                link(dve.tensor_reduce(r1[:, 6, :], w4(0), AX.X, ALU.add))
                link(dve.reciprocal(r1[:, 7, :], r1[:, 6, :]))
                dve.wait_ge(ev("eexp"), l + 1)
                link(dve.tensor_scalar(r1[:, 8, :], r1[:, 4, :], 1.0, None, ALU.add))
                link(dve.reciprocal(r1[:, 9, :], r1[:, 8, :]))
                link(tt(wtok[:, 0, :], r1[:, 9, :], r1[:, 7, :], ALU.mult))
                tt(wtok[:, 1, :], wtok[:, 0, :], r1[:, 4, :], ALU.mult)
                dve.wait_ge(ev("rank_mm"), l + 1)
                one = cst[:, C_ONE:C_ONE + EXPERTS]
                link(dve.tensor_copy(cnt[:, 0, :], PS[:, 6, 0:EXPERTS]))
                link(dve.tensor_tensor_scan(cnt[:, 1, :], one, cnt[:, 0, :], 0.0, ALU.mult, ALU.add))
                link(tt(cnt[:, 1, :], cnt[:, 1, :], cnt[:, 0, :], ALU.subtract))
                link(tt(slotpos[:, :, :], PS[:, 5, 0:NT * EXPERTS].rearrange("p (t n) -> p t n", t=NT),
                        bc(cnt[:, 1, :].unsqueeze(1), [P, NT, EXPERTS]), ALU.add))
                for c in range(2):
                    link(tt(one32[:, c, :, :], one32[:, c, :, :], slotpos[:, :, :], ALU.mult))
                    link(dve.tensor_reduce(posf[:, c, :], one32[:, c, :, :], AX.X, ALU.add))
                dve.tensor_copy(posu[:, :], posf[:, :, :].rearrange("p c t -> p (c t)")).then_inc(ev("pos"), 1)
                link(tt(cmpt[:, :, :], bc(cnt[:, 0, :].unsqueeze(2), [P, EXPERTS, MAXBLK - 1]),
                        bc(cst[:, C_THR:C_THR + MAXBLK - 1].unsqueeze(1), [P, EXPERTS, MAXBLK - 1]), ALU.is_gt))
                link(dve.tensor_reduce(cnt[:, 2, :], cmpt[:, :, :], AX.X, ALU.add))
                link(dve.tensor_scalar(cnt[:, 2, :], cnt[:, 2, :], 1.0, None, ALU.add))
                link(dve.tensor_tensor_scan(cnt[:, 3, :], one, cnt[:, 2, :], 0.0, ALU.mult, ALU.add))
                link(tt(cnt[:, 3, :], cnt[:, 3, :], cnt[:, 2, :], ALU.subtract))
                if l == 0:
                    link(tt(blocks0[:, :], cnt[:, 3, EXPERTS - 1:EXPERTS], cnt[:, 2, EXPERTS - 1:EXPERTS], ALU.add))
                else:
                    link(dve.tensor_scalar(cnt[:, 3, :], cnt[:, 3, :], blocks0[:, 0:1], None, ALU.add))
                tt(tab[0:1, 3 * EXPERTS:], cnt[0:1, 3, EXPERTS - 1:EXPERTS], cnt[0:1, 2, EXPERTS - 1:EXPERTS],
                   ALU.add).then_inc(ev("tab"), 1)
                for n in range(3):
                    dve.tensor_copy(tab[0:1, n * EXPERTS:(n + 1) * EXPERTS], cnt[0:1, n + 1, :]).then_inc(ev("tab"), 1)
                for i in range(0, 2 * RT, 2):
                    j = i // 2
                    dve.wait_ge(ev("xs_t"), 2 * RT * l + i + 1)
                    dve.tensor_copy(xsT[:, 0:4, j * P:(j + 1) * P], quad(i % 4)).then_inc(ev("xs_v"), 1)
                dve.wait_ge(ev("tab"), 4 * l + 4)
                if l == 0:
                    for name in ("act", "up_mm", "h_t", "down_mm", "yblk_c"):
                        dve.memset(tick[:, 1:2], 0.0).then_inc(ev(name), 1)
                        dve.wait_ge(ev(name), 1)
                with dve.Fori(0, EXPERTS) as e:
                    blocks = dve.value_load(tab[0:1, bass.ds(e + EXPERTS, 1)], min_val=1, max_val=MAXBLK)
                    before = dve.value_load(tab[0:1, bass.ds(e + 2 * EXPERTS, 1)], min_val=0, max_val=2 * ALLBLK)
                    with dve.Fori(0, blocks) as b:
                        dve.wait_ge(ev("silu"), before + b + 1)
                        dve.wait_ge(ev("h_t"), before + b + 1)
                        tt(gact[:, :], gsil[:, :], PS[:, 0, P:2 * P], ALU.mult).then_inc(ev("act"), 1)
                        dve.wait_ge(ev("h_t"), before + b + 2)
                        dve.wait_ge(ev("down_mm"), before + b + 1)
                        dve.tensor_copy(hblk[:, :, :], PS[:, 1, 0:P].rearrange("p (i n) -> p i n", i=2)) \
                            .then_inc(ev("hblk_c"), 1)
                for t in range(NT):
                    dve.wait_ge(ev("y0_w"), NT * l + t + 1)
                    dve.scalar_tensor_tensor(out=ygat[:, t, :], in0=ygat[:, NT + t, :], scalar=wtok[:, 1, t:t + 1],
                                             in1=ygat[:, t, :], op0=ALU.mult, op1=ALU.add).then_inc(ev("comb_v"), 1)
                for i in range(2 * NT):
                    t, half = i // 2, i % 2
                    dve.wait_ge(ev("comb_mm"), 2 * NT * l + i + 1)
                    for m in range(4):
                        k = 4 * half + m
                        c = 0 if t < ST else 1
                        ins = dve.scalar_tensor_tensor(
                            out=xT[:, k, t * P:t * P + P], in0=quad(4 + i % 4)[:, m, :], scalar=modT[:, l, 40 + k, c:c + 1],
                            in1=xT[:, k, t * P:t * P + P], op0=ALU.mult, op1=ALU.add)
                    ins.then_inc(ev("comb"), 1)

            moe(0)
            dve.wait_ge(ev("comb"), 2 * NT)
            normed(2)

            def gated_u(j):
                dve.wait_ge(ev("gate_mm"), 2 * j + 2)
                dve.wait_ge(ev("sig"), 2 * j + 2)
                for n, c0, c1 in ((0, 0, SEG), (1, SEG, SAMPLE), (1, SAMPLE, T)):
                    to = HALO + c0 + (HALO if c0 == SAMPLE else 0)
                    tt(upad[:, j, to:to + c1 - c0], rs[:, c0:c1], PS[:, n, c0 - n * SEG:c1 - n * SEG],
                       ALU.mult).then_inc(ev("u_w"), 1)

            gated_u(0)
            dve.wait_ge(ev("u_zero"), 1)
            for j in range(KD):
                dve.wait_ge(ev("u_w"), 3 * (j + 1))
                for n in range(DTAPS):
                    w = PE_TAPS + n
                    r = w * KD + j
                    wc = vecT[:, 2 + r // P, r % P:r % P + 1]
                    acc = cv[:, j, :] if n % 2 == 0 else cvb
                    src = upad[:, j, w:w + SPAN]
                    if n == 0:
                        dve.tensor_scalar(acc, src, wc, vecT[:, 1, V_DWB + j:V_DWB + j + 1],
                                          ALU.mult, ALU.add).then_inc(ev("conv_v"), 1)
                    elif n == 1:
                        dve.tensor_scalar(acc, src, wc, None, ALU.mult).then_inc(ev("conv_v"), 1)
                    else:
                        dve.wait_ge(ev("conv_v"), CONV_OPS * j + n - 1)
                        dve.scalar_tensor_tensor(out=acc, in0=src, scalar=wc, in1=acc,
                                                 op0=ALU.mult, op1=ALU.add).then_inc(ev("conv_v"), 1)
                    if n == DTAPS - LATE_TAPS and j + 1 < KD:
                        gated_u(j + 1)
                dve.wait_ge(ev("conv_v"), CONV_OPS * j + DTAPS)
                tt(cv[:, j, :], cv[:, j, :], cvb, ALU.add).then_inc(ev("conv_v"), 1)
                dve.wait_ge(ev("conv_v"), CONV_OPS * j + DTAPS + 1)
                dve.wait_ge(ev("tap_mm"), j + 1)
                for n, (c0, c1) in enumerate(((0, HALF), (HALF, SPAN))):
                    tt(cv[:, j, c0:c1], cv[:, j, c0:c1], PS[:, 4 + n, 0:c1 - c0], ALU.add).then_inc(ev("conv_v"), 1)
                dve.wait_ge(ev("conv_v"), CONV_OPS * (j + 1))
            dve.wait_ge(ev("ln_mm"), KD)
            for k in range(KD):
                for n, (c0, c1) in enumerate(((0, HALF), (HALF, SPAN))):
                    dve.scalar_tensor_tensor(out=cv[:, k, c0:c1], in0=PS[:, 6 + n, 0:c1 - c0], scalar=-1.0 / CONV,
                                             in1=cv[:, k, c0:c1], op0=ALU.mult, op1=ALU.add).then_inc(ev("ln_d"), 1)
            dve.wait_ge(ev("ln_root"), 2)
            dve.wait_ge(ev("ln_d"), 2 * KD)
            link(dve.reciprocal(scratch[:, 0:SAMPLE], scratch[:, 0:SAMPLE]))
            link(dve.reciprocal(scratch[:, CTX0:SPAN], scratch[:, CTX0:SPAN]))
            for k in range(KD):
                tt(cvn[:, k, 0:SAMPLE], cv[:, k, 0:SAMPLE], scratch[:, 0:SAMPLE], ALU.mult).then_inc(ev("ln_n"), 1)
                tt(cvn[:, k, SAMPLE:T], cv[:, k, CTX0:SPAN], scratch[:, CTX0:SPAN], ALU.mult).then_inc(ev("ln_n"), 1)
            add_out(1)
            moe(1)
            for i in range(0, 2 * NT, 2):
                t = i // 2
                dve.wait_ge(ev("x_t"), 2 * NT + i + 1)
                dve.tensor_copy(xtok[:, t, 0:512], PS[:, 4 + i % 4, :]).then_inc(ev("xt_v"), 1)

        @block.gpsimd
        def _(pool):
            step = [0]

            def link(ins):
                step[0] += 1
                ins.then_inc(ev("pool_step"), 1)
                pool.wait_ge(ev("pool_step"), step[0])

            def ctx_mod(q):
                l = q // 2
                pool.wait_ge(ev("coef"), q + 1)
                for k in range(KD):
                    pool.wait_ge(ev("hn"), 2 * KD * q + 2 * k + 2)
                    pool.tensor_scalar(hT[:, k, SAMPLE:T], hT[:, k, SAMPLE:T], modA[:, q, k, 1:2],
                                       modT[:, l, 24 * (q % 2) + k, 1:2], ALU.mult, ALU.add).then_inc(ev("h_c"), 1)

            pool.memset(scT[:, :, :], 0.0).then_inc(ev("sc_zero"), 1)

            ctx_mod(0)
            n_out = 0
            pool.wait_ge(ev("z_v"), 4 * NT)
            pool.wait_ge(ev("z_a"), 4 * NT)
            pool.dma_start(f["new_krope"][0, 0], z[:, ST, Z_KR:Z_RQ]).then_inc(ev("side_out"), 16)
            pool.wait_ge(ev("upd_c"), NT)
            for d in range(2):
                pool.dma_start(f["new_state"][0, 0, d].rearrange("h k v -> k h v"),
                               upd[d * RK:(d + 1) * RK, ST, :, :]).then_inc(ev("side_out"), 16)
            pool.wait_ge(ev("lat_n"), NT)
            pool.dma_start(f["new_ckv"][0, 0], z[:, ST, QRANK:Z_KR]).then_inc(ev("side_out"), 16)
            pool.wait_ge(ev("qkg_s"), 1)
            for u, (kind, t) in enumerate(UNITS):
                raw = qkraw[:, u % 2, :].rearrange("p (h n) -> p h n", h=HEADS)
                if kind == "k":
                    kr = z[:, t, Z_KR:Z_RQ] if t < NT else cache_in[:, KVRANK:]
                    if u >= 2:
                        pool.wait_ge(ev("hd_t"), u - 1)
                    pool.tensor_copy(raw[:, :, NOPE:QK], bc(kr.unsqueeze(1), [P, HEADS, ROPE])).then_inc(ev("kr_p"), 1)
                pool.wait_ge(ev("qk_r"), u + 1)
                gain = bc(qkg[:, 0 if kind == "q" else 1, :].unsqueeze(1), [P, HEADS, QK])
                ins = pool.tensor_tensor(raw, raw, gain, ALU.mult)
                if t < ST:
                    link(ins)
                    x1, x2 = raw[:, :, NOPE:NOPE + 16], raw[:, :, NOPE + 16:QK]
                    cs = bc(cst[:, C_COS + 16 * t:C_COS + 16 * t + 16].unsqueeze(1), [P, HEADS, 16])
                    sn = bc(cst[:, C_SIN + 16 * t:C_SIN + 16 * t + 16].unsqueeze(1), [P, HEADS, 16])
                    r = [ropet[:, n, :].rearrange("p (h n) -> p h n", h=HEADS) for n in range(4)]
                    pool.tensor_tensor(r[0], x1, cs, ALU.mult)
                    pool.tensor_tensor(r[1], x2, sn, ALU.mult)
                    pool.tensor_tensor(r[2], x1, sn, ALU.mult)
                    link(pool.tensor_tensor(r[3], x2, cs, ALU.mult))
                    link(pool.tensor_tensor(x1, r[0], r[1], ALU.subtract))
                    ins = pool.tensor_tensor(x2, r[2], r[3], ALU.add)
                ins.then_inc(ev("qk_n"), 1)
                pool.wait_ge(ev("qk_n"), u + 1)
            pool.wait_ge(ev("hd_t"), len(UNITS))
            for hp in range(4):
                pool.wait_ge(ev("o_c"), 3 + hp)
                pool.tensor_copy(oT[:, 2 * hp, SAMPLE:T], octx[:, hp, :]).then_inc(ev("octx_c"), 1)

            def moe(l):
                q = 2 * l + 1
                ctx_mod(q)
                if l == 0:
                    pool.wait_ge(ev("side_out"), 64)
                pool.wait_ge(ev("pos"), l + 1)
                for t in range(NT):
                    pool.wait_ge(ev("htok_a"), 2 * NT * l + 2 * (t + 1))
                    for c in range(2):
                        pool.indirect_dma_start(
                            rows_in[:, :], bass.IndirectOffsetOnAxis(ap=posu[:, c * NT + t:c * NT + t + 1], axis=0),
                            htok[:, t, :], None).then_inc(ev("rows_sent"), 16)
                pool.wait_ge(ev("rows_sent"), 16 * 2 * NT * (l + 1))
                pool.memset(xsT[:, :, ROWS:XW], 0.0).then_inc(ev("pad"), 1)
                pool.wait_ge(ev("xs_v"), RT * l + RT)
                pool.wait_ge(ev("xs_a"), RT * l + RT)
                pool.wait_ge(ev("pad"), l + 1)
                pool.wait_ge(ev("tab"), 4 * l + 4)
                if l == 0:
                    pool.wait_ge(ev("up_mm"), 1)
                with pool.Fori(0, EXPERTS) as e:
                    off = pool.value_load(tab[0:1, bass.ds(e, 1)], min_val=0, max_val=ROWS)
                    blocks = pool.value_load(tab[0:1, bass.ds(e + EXPERTS, 1)], min_val=1, max_val=MAXBLK)
                    before = pool.value_load(tab[0:1, bass.ds(e + 2 * EXPERTS, 1)], min_val=0, max_val=2 * ALLBLK)
                    with pool.Fori(0, blocks) as b:
                        pool.wait_ge(ev("up_mm"), before + b + 1)
                        row = pool.snap(nc.s_assert_within(
                            off + b * BLK, 0, ROWS,
                            skip_runtime_bounds_check_because="a further block starts inside the expert's rows"))
                        pool.tensor_copy(xblk[:, :, :], xsT[:, :, bass.ds(row, BLK)]).then_inc(ev("xblk_c"), 1)
                pool.wait_ge(ev("results_sent"), l + 1)
                for t in range(NT):
                    for c in range(2):
                        pool.indirect_dma_start(
                            ygat[:, c * NT + t, :], None, rows_out[0:ROWS, :],
                            bass.IndirectOffsetOnAxis(ap=posu[:, c * NT + t:c * NT + t + 1], axis=0)) \
                            .then_inc(ev(f"picked{t}"), 16)

            moe(0)
            pool.wait_ge(ev("comb"), 2 * NT)
            for t in range(NT):
                pool.wait_ge(ev(f"picked{t}"), 32)
            ctx_mod(2)
            pool.memset(upad[:, :, 0:HALO], 0.0)
            pool.memset(upad[:, :, HALO + SAMPLE:HALO + CTX0], 0.0)
            pool.memset(upad[:, :, PADW - HALO:PADW], 0.0).then_inc(ev("u_zero"), 1)
            for j in range(KD):
                if j >= 2:
                    pool.wait_ge(ev("tap_mm"), j - 1)
                for w in range(PE_TAPS):
                    r = w * KD + j
                    pool.tensor_scalar(tapd[:, j % 2, w, :], ident, vecT[:, 2 + r // P, r % P:r % P + 1], None,
                                       ALU.mult).then_inc(ev("tap_d"), 1)
            moe(1)


_INS = ['x_prompt', 'x_sample', 'cache_mla_ckv', 'cache_mla_krope', 'state_retention', 'c', 'c_ctx', 'ada_w', 'ada_b',
        'norm_mix', 'norm_ffn', 'ev_w_in', 'ev_q_a_norm', 'ev_w_q_up', 'ev_kv_a_norm', 'ev_w_kv_up', 'ev_q_norm',
        'ev_k_norm', 'ev_ret_decay', 'ev_ret_gn', 'ev_w_out', 'od_w_in', 'od_dw', 'od_dw_b', 'od_ln_g', 'od_ln_b',
        'od_w_out', 'moe_w_group', 'moe_b_group', 'moe_w_expert', 'moe_b_expert', 'moe_w_up', 'moe_w_down']
_OUTS = [("y_prompt", (1, CONTEXT, D)), ("y_sample", (1, SAMPLE, D)), ("new_ckv", (1, 1, CONTEXT, KVRANK)),
         ("new_krope", (1, 1, CONTEXT, ROPE)), ("new_state", (1, 1, 2, RH, RK, RV))]


def shape_constants():
    import numpy as np
    c = np.zeros((P, C_W), np.float32)
    i = np.arange(P)
    c[:, C_ID:C_ID + P] = np.eye(P)
    c[:, C_ONE:C_ONE + P] = 1.0
    c[:, C_TRI:C_TRI + P] = i[:, None] < i[None, :]
    d = i[None, :] - i[:, None]
    dist = np.concatenate([np.maximum(d, 0), d >= 0, np.maximum(-d, 0), d <= 0], axis=1).astype(np.float32)
    freqs = np.float32(10000.0) ** (-np.arange(8, dtype=np.float32) / np.float32(8))
    tok = np.arange(SAMPLE)
    ang = np.concatenate([(tok // GRID_W)[:, None] * freqs, (tok % GRID_W)[:, None] * freqs], axis=1)
    for off, v in ((C_COS, np.cos(ang)), (C_SIN, np.sin(ang))):
        c[:, off:off + ST * 16] = v.reshape(ST, P, 16).transpose(1, 0, 2).reshape(P, ST * 16)
    c[:, C_POS:C_POS + 4] = np.stack([P - 1 - i, i + 1, i, P - i], axis=1)
    c[:, C_PRI4:C_PRI4 + 4] = np.arange(4, 0, -1)
    c[:, C_PRI8:C_PRI8 + 8] = np.arange(8, 0, -1)
    c[:, C_THR:C_THR + MAXBLK - 1] = BLK * np.arange(1, MAXBLK)
    c[:, C_EPS] = EPS
    return c, dist


def kernel(**inputs):
    import numpy as _np
    import concourse.bacc as _bacc
    from concourse import mybir as _mybir
    from concourse.bass_utils import run_bass_kernel_spmd as _run

    nc = _bacc.Bacc("TRN2", target_bir_lowering=False, num_devices=1)
    arrays, io = {}, {}
    named = {name: _np.ascontiguousarray(inputs[name]) for name in _INS}
    named["consts"], named["distances"] = shape_constants()
    for name, a in named.items():
        arrays[f"in_{name}"] = a
        io[name] = nc.dram_tensor(f"in_{name}", a.shape, _mybir.dt.from_np(a.dtype), kind="ExternalInput").ap()
    for name, shape in _OUTS:
        io[name] = nc.dram_tensor(f"out_{name}", shape, F32, kind="ExternalOutput").ap()
    build(nc, io)
    r = _run(nc, [arrays], core_ids=[0])
    return tuple(r.results[0][f"out_{name}"] for name, _ in _OUTS)
```

```python
from contextlib import ExitStack

import concourse.bass as bass
from concourse import mybir

F32 = mybir.dt.float32
I32 = mybir.dt.int32
U32 = mybir.dt.uint32
ALU = mybir.AluOpType
ACT = mybir.ActivationFunctionType
AX = mybir.AxisListType

P = 128
D = 1024
KD = D // P
SAMPLE, CONTEXT = 512, 128
T = SAMPLE + CONTEXT
NT = T // P
ST = SAMPLE // P
PAST = 128
GRID_W = 64
EPS = 1e-6
HEADS, NOPE, ROPE, VD = 8, 64, 32, 64
QK = NOPE + ROPE
QRANK, KVRANK = 256, 128
RH, RK, RV = 4, 64, 128
EVEN_IN = QRANK + KVRANK + ROPE + 2 * RH * RK + 2 * RH * RV
Z_KR = QRANK + KVRANK
Z_RQ = Z_KR + ROPE
Z_RK = Z_RQ + RH * RK
Z_RV = Z_RK + RH * RK
Z_RG = Z_RV + RH * RV
CONV = 1024
TAPS = 31
HALO = TAPS // 2
PADW = HALO + SAMPLE + HALO + CONTEXT + HALO
SPAN = SAMPLE + HALO + CONTEXT
CTX0 = SAMPLE + HALO
GROUPS, PER, EXPERTS, TOPK, FF = 4, 8, 32, 2, 256
ROUTE = GROUPS + EXPERTS
ROWS = T * TOPK
RT = ROWS // P
BLK = 64
XW = ROWS + BLK
MAXBLK = (T + BLK - 1) // BLK
ALLBLK = ROWS // BLK + EXPERTS

SLOT = 2048
SLOTS = 9
PER_EXPERT = 3
RING_EXPERTS = SLOTS // PER_EXPERT

C_ID, C_ONE, C_TRI = 0, P, 2 * P
D_A1, D_U, D_A2, D_L = 0, P, 2 * P, 3 * P
C_COS = 3 * P
C_SIN = C_COS + ST * 16
C_POS = C_SIN + ST * 16
C_PRI4 = C_POS + 4
C_PRI8 = C_PRI4 + 4
C_THR = C_PRI8 + 8
C_EPS = C_THR + MAXBLK - 1
C_W = C_EPS + 1

V_ADAB, V_COND, V_NMIX = 0, 96, 112
V_NFFN, V_DWB, V_LNG, V_LNB, V_GN, V_QA = 0, 16, 24, 32, 40, 44
V_ROWS = (128, 46, 128, TAPS * 8 - 128)

A_H = 0
A_QT = 0
A_Z = 5120
A_KT = A_Z + NT * EVEN_IN
A_V = A_KT + 6144
ARENA = A_V + 3072
A_XS = 0
A_HTOK = 5120
A_YG = KD * XW
A_BLK = A_YG + 2 * NT * D
A_U = 5120
A_CV = A_U + KD * PADW
A_DG = A_CV + KD * SPAN
PE_TAPS = 5
LAST_TAPS = 16
A_CB = A_DG + 2 * PE_TAPS * P
A_DL = A_CB + SPAN
SEG = T // 2
HALF = (SPAN + 1) // 2
LATE_TAPS = 5
assert A_BLK + 1408 <= ARENA and A_DL + LAST_TAPS * P <= ARENA


def ada(n):
    return "ada%d" % (n // 24), n % 24


def weight_plan():
    plan = [("ada0", j) for j in range(8)]
    for c in range(8):
        plan += [("ev_in", c)] + [ada(8 + 3 * c + j) for j in range(3)]
    plan += [ada(n) for n in range(32, 48)]
    plan += [("q_up", 0), ("kv_up", 0)]
    plan += [("ev_out", j) for j in range(4)]
    plan += [("expert0", i) for i in range(PER_EXPERT * EXPERTS)]
    plan += [("od_in", j) for j in range(8)]
    plan += [("od_out", j) for j in range(4)]
    plan += [("expert1", i) for i in range(PER_EXPERT * EXPERTS)]
    return plan


def build(nc, io):
    f = io
    ctx = ExitStack()
    with ctx:
        def sb(name, shape, dt=F32):
            return ctx.enter_context(nc.sbuf_tensor(name, shape, dt))

        def sem(name):
            return ctx.enter_context(nc.semaphore(name))

        xT = sb("xT", [P, KD, T])
        arena = sb("arena", [P, ARENA])
        ring = sb("ring", [P, SLOTS, SLOT])
        cst = sb("cst", [P, C_W])
        vrow = arena[:, A_V:A_V + 4 * P].rearrange("p (g n) -> p g n", g=4)
        vecT = sb("vecT", [P, 4, P])
        scT = sb("scT", [P, KD, 32])
        modT = sb("modT", [P, 2, 48, 2])
        modA = sb("modA", [P, 4, KD, 2])
        wr = sb("wr", [P, KD, ROUTE])
        rb = sb("rb", [P, 2, ROUTE])
        kvg = sb("kvg", [P, KVRANK])
        qkg = sb("qkg", [P, 2, QK])
        gcol = sb("gcol", [P, 2])
        dec = sb("dec", [P, 2 * RH])
        decw = sb("decw", [P, 3, 2 * RH])
        edge = sb("edge", [P, 6, RH])
        cache_cT = sb("cache_cT", [P, P])
        ss = sb("ss", [P, 2, 16])
        stat = sb("stat", [P, RH, 6])
        mv = sb("mv", [P, RH, 2])
        rmv = sb("rmv", [P, RH])
        nmx = sb("nmx", [P, 2])
        cmx = sb("cmx", [P, 2, 4])
        den = sb("den", [P, 2])
        rden = sb("rden", [P, 2])
        r1 = sb("r1", [P, 12, NT])
        cnt = sb("cnt", [P, 6, EXPERTS])
        posf = sb("posf", [P, 2, NT])
        posu = sb("posu", [P, 2 * NT], U32)
        wtok = sb("wtok", [P, 2, NT])
        tab = sb("tab", [1, 3 * EXPERTS + 1], I32)
        blocks0 = sb("blocks0", [P, 1])
        tick = sb("tick", [P, 4])
        PS = ctx.enter_context(nc.psum_tensor("PS", [P, 8, 512], F32))

        rows_in = nc.dram_tensor("rows_in", (ROWS, D), F32).ap()
        rows_out = nc.dram_tensor("rows_out", (XW, D), F32).ap()

        ident = cst[:, C_ID:C_ID + P]
        ones = cst[:, C_ONE:C_ONE + P]
        tri = cst[:, C_TRI:C_TRI + P]
        eps = cst[:, C_EPS:C_EPS + 1]

        hT = arena[:, A_H:A_H + KD * T].rearrange("p (k t) -> p k t", k=KD)
        z = arena[:, A_Z:A_Z + NT * EVEN_IN].rearrange("p (t n) -> p t n", t=NT)
        xtok = arena[:, A_Z:A_Z + NT * D].rearrange("p (t n) -> p t n", t=NT)
        A_K = A_KT
        states = arena[:, A_K:A_K + ST * 512].rearrange("p (t h n) -> p t h n", t=ST, h=RH)
        upd = arena[:, A_K + 2048:A_K + 2048 + NT * 512].rearrange("p (t h n) -> p t h n", t=NT, h=RH)

        def four(off):
            return arena[:, off:off + 4 * P].rearrange("p (h n) -> p h n", h=4)
        rqkT = [four(A_K + 4608), four(A_K + 5120)]
        qfbT = [four(A_K + 5632), four(A_V)]
        kfb = arena[:, A_V:A_V + 512].rearrange("p (h n) -> p h n", h=RH)
        qfb = arena[:, A_V + 512:A_V + 1024].rearrange("p (h n) -> p h n", h=RH)
        rsc = [four(A_V + 1024), four(A_V + 2048)]
        onrm = arena[:, A_V + 1536:A_V + 2048].rearrange("p (h n) -> p h n", h=RH)
        mtmp = arena[:, A_V + 1024:A_V + 2048].rearrange("p (a n) -> p a n", a=8)
        dist = arena[:, A_V + 2048:A_V + 2560]
        mask = arena[:, A_V + 2560:A_V + 3072].rearrange("p (h n) -> p h n", h=RH)
        qT = arena[0:QK, A_QT:A_QT + HEADS * T].rearrange("p (h t) -> p h t", h=HEADS)
        kT = arena[0:QK, A_KT:A_KT + HEADS * 768].rearrange("p (h t) -> p h t", h=HEADS)
        vS = arena[:, A_V:A_V + 3072].rearrange("p (j h n) -> p j h n", j=6, h=HEADS)

        cT = z[:, :, Z_RV:Z_RV + 3 * P].rearrange("p t (j n) -> p t j n", j=3)
        prob = [z[:, :, 0:P], z[:, :, P:2 * P]]
        probT = [z[:, :, Z_RQ:Z_RQ + 512], z[:, :, Z_RQ + 512:Z_RQ + 1024]]
        oret = z[:, :, Z_RG:Z_RG + 512]
        oT = arena[:, A_QT:A_QT + KD * T].rearrange("p (k t) -> p k t", k=KD)
        htok = arena[:, A_HTOK:A_HTOK + NT * D].rearrange("p (t n) -> p t n", t=NT)
        xsT = arena[:, A_XS:A_XS + KD * XW].rearrange("p (k r) -> p k r", k=KD)
        xback = arena[:, A_YG:A_YG + RT * D].rearrange("p (j n) -> p j n", j=RT)
        ygat = xback
        xblk = arena[:, A_BLK:A_BLK + 512].rearrange("p (k n) -> p k n", k=KD)
        gsil = arena[:, A_BLK + 512:A_BLK + 640]
        gact = arena[:, A_BLK + 640:A_BLK + 768]
        hblk = arena[:, A_BLK + 768:A_BLK + 896].rearrange("p (i n) -> p i n", i=2)
        yblk = arena[:, A_BLK + 896:A_BLK + 1408]
        upad = arena[:, A_U:A_U + KD * PADW].rearrange("p (k t) -> p k t", k=KD)
        cv = arena[:, A_CV:A_CV + KD * SPAN].rearrange("p (k t) -> p k t", k=KD)
        cv2 = arena[:, 0:KD * SPAN].rearrange("p (k t) -> p k t", k=KD)
        tapd = arena[:, A_DG:A_DG + 2 * PE_TAPS * P].rearrange("p (b w n) -> p b w n", b=2, w=PE_TAPS)
        cache_in = sb("cache_in", [P, KVRANK + ROPE])
        sq1 = arena[:, A_Z:A_Z + KD * T].rearrange("p (k t) -> p k t", k=KD)
        cvn = arena[:, KD * SPAN:KD * (SPAN + T)].rearrange("p (k t) -> p k t", k=KD)
        cvb = arena[:, A_CB:A_CB + SPAN]
        tapl = arena[:, A_DL:A_DL + LAST_TAPS * P].rearrange("p (w n) -> p w n", w=LAST_TAPS)
        scratch = sb("scratch", [P, 3 * HEADS * QK])
        qkraw = scratch[:, 0:2 * HEADS * QK].rearrange("p (b n) -> p b n", b=2)
        qksq = scratch[:, 2 * HEADS * QK:].unsqueeze(1)
        ropet = z[:, 0:4, Z_RV + 3 * P:Z_RV + 4 * P]
        octx = scratch[:, 0:4 * P].rearrange("p (k t) -> p k t", k=4)
        mrow = scratch[:, 0:512]
        cell = [0]

        def cells(*shape):
            n = 1
            for x in shape:
                n *= x
            cell[0] += n
            assert cell[0] <= 3 * HEADS * QK
            names = " ".join("abc"[:len(shape)])
            return scratch[:, cell[0] - n:cell[0]].rearrange(
                f"p ({names}) -> p {names}", **dict(zip("abc", shape))) if len(shape) > 1 \
                else scratch[:, cell[0] - n:cell[0]]
        lgt = cells(NT, ROUTE)
        rt = cells(9, NT, PER)
        one32 = cells(2, NT, EXPERTS)
        both = cells(NT, EXPERTS)
        slotpos = cells(NT, EXPERTS)
        cmpt = cells(EXPERTS, MAXBLK - 1)
        rs = cells(T)

        plan = weight_plan()
        at = {}
        for n, key in enumerate(plan):
            at[key] = n
        ring_full = [sem(f"ring_full{s}") for s in range(SLOTS)]
        S = {}

        def ev(name):
            if name not in S:
                S[name] = sem(name)
            return S[name]

        def released(key):
            kind, j = key
            if kind == "ada0":
                return ev("mod_mm"), j + 1
            if kind == "ada1":
                return ev("mod_mm"), 24 + j + 1
            if kind == "ev_in":
                return ev("z_mm"), NT * (j + 1)
            if kind in ("q_up", "kv_up"):
                return ev("qk_mm"), NT + NT + 1
            if kind == "ev_out":
                return ev("wo_mm"), 2 * (j + 1)
            if kind == "od_in":
                return ev("gate_mm"), 2 * (j + 1)
            return ev("wo_mm"), KD + 2 * (j + 1)

        NPARAM = 14

        def pe_taps(j):
            return LAST_TAPS if j == KD - 1 else PE_TAPS

        def taps_until(j):
            return sum(pe_taps(i) for i in range(j))

        def conv_ops(j):
            return (TAPS + 3) * j - taps_until(j)

        def tap_diag(j, w):
            return tapl[:, w, :] if j == KD - 1 else tapd[:, j % 2, w, :]
        full_count, filled = [], [0] * SLOTS
        for n, key in enumerate(plan):
            filled[n % SLOTS] += 32 if key[0] == "od_in" else 16
            full_count.append(filled[n % SLOTS])
        ATT = [("ctx", g, 0) for g in range(2)] + [("lat", h, t) for h in range(HEADS) for t in range(ST)]
        NATT = len(ATT)
        GROUP_END = {0: 0, 1: 1}
        for hp in range(4):
            GROUP_END[2 + (hp + 1) * 2 * ST - 1] = 2 + hp

        def groups_before(i):
            return i if i < 2 else 2 + (i - 2) // (2 * ST)
        UNITS = [(kind, t) for t in range(NT) for kind in "qk"] + [("k", NT)]
        KCOL = [0, P, 2 * P, 3 * P, 5 * P, 4 * P]
        VROW = [0, 1, 2, 3, 5, 4]
        PSf = PS[:, :, :].rearrange("p b n -> p (b n)")

        def w_view(key):
            return ring[:, at[key] % SLOTS, :]

        def quad(b):
            return PS[:, b, :].rearrange("p (j n) -> p j n", j=4)

        def squares(q):
            return sq1 if q == 1 else hT

        def bc(ap, shape):
            return ap.to_broadcast(shape)

        block = ctx.enter_context(nc.Block())

        @block.sync
        def _(sp):
            def source(key):
                kind, j = key
                v8 = w_view(key).rearrange("p (k n) -> p k n", k=KD)
                if kind in ("ada0", "ada1"):
                    r, k = j // KD, j % KD
                    return f["ada_w"][int(kind[3]), k * P:(k + 1) * P, SLOT * r:SLOT * (r + 1)], w_view(key)
                if kind == "ev_in":
                    n = min(256, EVEN_IN - 256 * j)
                    return f["ev_w_in"][0, :, 256 * j:256 * j + n].rearrange("(k p) n -> p k n", p=P), v8[:, :, 0:n]
                if kind == "q_up":
                    return (f["ev_w_q_up"][0].rearrange("(k p) n -> p k n", p=P),
                            w_view(key)[:, 0:1536].rearrange("p (k n) -> p k n", k=2))
                if kind == "kv_up":
                    return f["ev_w_kv_up"][0], w_view(key)[:, 0:1024]
                if kind in ("ev_out", "od_out"):
                    w = f["ev_w_out" if kind == "ev_out" else "od_w_out"]
                    return w[0, :, 256 * j:256 * j + 256].rearrange("(k p) n -> p k n", p=P), v8

            def load(n):
                key = plan[n]
                if n >= SLOTS and not plan[n - SLOTS][0].startswith("expert"):
                    sp.wait_ge(*released(plan[n - SLOTS]))
                full = ring_full[n % SLOTS]
                if key[0] == "od_in":
                    v = f["od_w_in"][0].rearrange("(k p) (a n) -> p k a n", p=P, a=2)
                    d = w_view(key).rearrange("p (k a n) -> p k a n", k=KD, a=2)
                    for a in range(2):
                        sp.dma_start(d[:, :, a, :], v[:, :, a, P * key[1]:P * key[1] + P]).then_inc(full, 16)
                elif key[0].startswith("expert"):
                    load_part(int(key[0][6]), key[1] // PER_EXPERT, key[1] % PER_EXPERT, n % SLOTS)
                else:
                    src, dst = source(key)
                    sp.dma_start(dst, src).then_inc(full, 16)

            def load_part(l, e, j, s):
                if j < 2:
                    src = f["moe_w_up"][l, bass.ds(e, 1), 512 * j:512 * j + 512, :] \
                        .rearrange("e (k p) n -> p (e k) n", p=P)
                    sp.dma_start(ring[:, s, :].rearrange("p (k n) -> p k n", k=4), src).then_inc(ring_full[s], 16)
                else:
                    src = f["moe_w_down"][l, bass.ds(e, 1), :, :].rearrange("e (k p) n -> p (e k) n", p=P)
                    sp.dma_start(ring[:, s, :].rearrange("p (k n) -> p k n", k=2), src).then_inc(ring_full[s], 16)

            def store_rows(e):
                off = sp.value_load(tab[0:1, bass.ds(e, 1)], min_val=0, max_val=ROWS)
                blocks = sp.value_load(tab[0:1, bass.ds(e + EXPERTS, 1)], min_val=1, max_val=MAXBLK)
                before = sp.value_load(tab[0:1, bass.ds(e + 2 * EXPERTS, 1)], min_val=0, max_val=2 * ALLBLK)
                with sp.Fori(0, blocks) as b:
                    row = sp.snap(nc.s_assert_within(
                        off + b * BLK, 0, ROWS,
                        skip_runtime_bounds_check_because="a further block starts inside the expert's rows"))
                    sp.wait_ge(ev("yblk_c"), before + b + 2)
                    for c in range(2):
                        sp.dma_start(rows_out[bass.ds(row, BLK), c * 512:(c + 1) * 512],
                                     yblk[c * BLK:(c + 1) * BLK, :]).then_inc(ev("y_sent"), 16)

            def load_experts(l):
                n0 = at[(f"expert{l}", 0)]
                rounds = EXPERTS // RING_EXPERTS
                for i in range(SLOTS):
                    load(n0 + i)
                sp.wait_ge(ev("tab"), 4 * l + 4)
                with sp.Fori(1, rounds) as g:
                    for p in range(RING_EXPERTS):
                        store_rows(g * RING_EXPERTS + (p - RING_EXPERTS))
                        for j in range(PER_EXPERT):
                            load_part(l, g * RING_EXPERTS + p, j, (n0 + PER_EXPERT * p + j) % SLOTS)
                for e in range(RING_EXPERTS * (rounds - 1), EXPERTS):
                    store_rows(e)
                    if e + RING_EXPERTS < EXPERTS:
                        for j in range(PER_EXPERT):
                            load(n0 + PER_EXPERT * (e + RING_EXPERTS) + j)

            sp.wait_ge(ev("params_in"), 16 * NPARAM)
            n = 0
            while n < len(plan):
                if plan[n][0].startswith("expert"):
                    load_experts(int(plan[n][0][6]))
                    n += PER_EXPERT * EXPERTS
                else:
                    load(n)
                    n += 1
            for t in range(NT):
                sp.wait_ge(ev("xt_v"), NT + t + 1)
                sp.wait_ge(ev("xt_a"), NT + t + 1)
                dst = f["y_sample"][0, t * P:t * P + P, :] if t < ST else f["y_prompt"][0, :, :]
                sp.dma_start(dst, xtok[:, t, :]).then_inc(ev("y_out"), 16)
            sp.wait_ge(ev("y_out"), 16 * NT)

        @block.tensor
        def _(pe):
            def arrived(key):
                n = at[key]
                pe.wait_ge(ring_full[n % SLOTS], full_count[n])

            def mod_columns(g):
                pe.wait_ge(ev("mrow_c"), g + 1)
                for q in range(4):
                    last = pe.transpose(quad(5 if g == 0 else 6)[:, q, :], mrow[:, q * P:(q + 1) * P], ident)
                last.then_inc(ev("mod_t"), 1)

            def modulation(n):
                l, j = n // 24, n % 24
                if n % KD == 0 and n > KD:
                    mod_columns(n // KD - 1)
                arrived((f"ada{l}", j))
                w = w_view((f"ada{l}", j))
                for c in range(4):
                    last = pe.matmul(PS[32 * c:32 * c + 32, 7, :], scT[:, j % KD, :], w[:, 512 * c:512 * c + 512],
                                     start=(j % KD == 0), stop=(j % KD == KD - 1))
                last.then_inc(ev("mod_mm"), 1)

            def norm_sums(q):
                for k in range(KD):
                    pe.wait_ge(ev("squared"), KD * q + k + 1)
                    pe.matmul(PS[:, 4, :], ones, squares(q)[:, k, 0:SAMPLE], start=(k == 0), stop=(k == KD - 1))
                    last = pe.matmul(PS[:, 6, 0:CONTEXT], ones, squares(q)[:, k, SAMPLE:T],
                                     start=(k == 0), stop=(k == KD - 1))
                last.then_inc(ev("sumsq"), 1)

            def project_out(l, kind, src, tile):
                for m in range(KD):
                    if m % 2 == 0:
                        arrived((kind, m // 2))
                        w = w_view((kind, m // 2)).rearrange("p (k n) -> p k n", k=KD)
                    if m >= 2:
                        pe.wait_ge(ev("wo_ev"), KD * l + m - 1)
                    b = 4 + 2 * (m % 2)
                    c = (m % 2) * P
                    for k in range(KD):
                        if l == 1 and m == 0:
                            pe.wait_ge(ev("act1"), k + 1)
                        for n in range(2):
                            last = pe.matmul(PS[:, b + n, 0:SEG], w[:, k, c:c + P], src[:, tile(k), n * SEG:(n + 1) * SEG],
                                             start=(k == 0), stop=(k == KD - 1))
                    last.then_inc(ev("wo_mm"), 1)

            pe.wait_ge(ev("params_in"), 16 * NPARAM)
            for g, r in enumerate(V_ROWS):
                last = pe.transpose(PS[:, 5, g * P:g * P + r], vrow[0:r, g, :], cst[0:r, C_ID:C_ID + r])
            last.then_inc(ev("vec_t"), 1)
            for i in range(2 * NT):
                t, half = i // 2, i % 2
                if half == 0:
                    pe.wait_ge(ev("x_in"), 32)
                if i >= 4:
                    pe.wait_ge(ev(("xt_v", "xt_a")[i % 2]), (i - 4) // 2 + 1)
                for j in range(4):
                    last = pe.transpose(quad(i % 4)[:, j, :],
                                        xtok[:, t, (4 * half + j) * P:(4 * half + j + 1) * P], ident)
                last.then_inc(ev("x_t"), 1)
            norm_sums(0)
            pe.wait_ge(ev("sc_ready"), 1)
            for j in range(8):
                modulation(j)
            mod_columns(0)
            pe.wait_ge(ev("xt_v"), NT)
            pe.wait_ge(ev("xt_a"), NT)
            pe.wait_ge(ev("vec_c"), 4)
            for c in range(8):
                n = min(256, EVEN_IN - 256 * c)
                arrived(("ev_in", c))
                w = w_view(("ev_in", c)).rearrange("p (k n) -> p k n", k=KD)
                for t in range(NT):
                    i = NT * c + t
                    if i >= 4:
                        pe.wait_ge(ev(("z_v", "z_a")[i % 2]), (i - 4) // 2 + 1)
                    for k in range(KD):
                        if i < NT:
                            pe.wait_ge(ev("h_s" if t < ST else "h_c"), k + 1)
                        last = pe.matmul(PS[:, i % 4, 0:n], hT[:, k, t * P:t * P + P], w[:, k, 0:n],
                                         start=(k == 0), stop=(k == KD - 1))
                    last.then_inc(ev("z_mm"), 1)
                for j in range(3):
                    modulation(8 + 3 * c + j)
            pe.wait_ge(ev("z_v"), 20)
            pe.wait_ge(ev("z_a"), 20)
            for t in range(NT):
                pe.wait_ge(ev("kfb"), t + 1)
                if t >= 2:
                    pe.wait_ge(ev("upd_c"), t - 1)
                for h in range(RH):
                    last = pe.matmul(quad(t % 2)[:, h, :], kfb[:, h, :], z[:, t, Z_RV + h * RV:Z_RV + (h + 1) * RV],
                                     start=True, stop=True)
                last.then_inc(ev("upd_mm"), 1)
                modulation(32 + 2 * t)
                modulation(33 + 2 * t)
            pe.wait_ge(ev("upd_c"), NT)
            def turn_qk(t):
                if t >= 2:
                    pe.wait_ge(ev("rqk_c"), t - 1)
                for j in range(4):
                    last = pe.transpose(quad(t % 2)[:, j, :], z[:, t, Z_RQ + j * P:Z_RQ + (j + 1) * P], ident)
                last.then_inc(ev("rqk_t"), 1)

            def scores(t):
                if t < ST:
                    pe.wait_ge(ev("qfb"), t + 1)
                    if t >= 1:
                        pe.wait_ge(ev("qfb_c"), t)
                    for h in range(RH):
                        last = pe.transpose(quad(2)[:, h, :], qfb[:, h, :], ident)
                    last.then_inc(ev("qfb_t"), 1)
                pe.wait_ge(ev("rqk_c"), t + 1)
                if t >= 1:
                    pe.wait_ge(ev("rsc"), t)
                for h in range(RH):
                    r = RK * (h % 2)
                    last = pe.matmul(quad(3 + 3 * (h % 2))[:, h // 2, :], rqkT[t % 2][r:r + RK, 2 + h // 2, :],
                                     rqkT[t % 2][r:r + RK, h // 2, :], start=True, stop=True)
                last.then_inc(ev("rs_mm"), 1)

            turn_qk(0)
            scores(0)
            for t in range(NT):
                if t + 1 < NT:
                    turn_qk(t + 1)
                modulation(42 + t)
                pe.wait_ge(ev("rsc"), t + 1)
                if t < ST:
                    pe.wait_ge(ev("qfb_c"), t + 1)
                    pe.wait_ge(ev("states"), ST - 1)
                if t >= 2:
                    pe.wait_ge(ev("onrm"), t - 1)
                for h in range(RH):
                    last = pe.matmul(quad(4 + t % 2)[:, h, :], rsc[t % 2][:, h, :],
                                     z[:, t, Z_RV + h * RV:Z_RV + (h + 1) * RV], start=True, stop=(t == ST))
                    if t < ST:
                        last = pe.matmul(quad(4 + t % 2)[:, h, :], qfbT[t % 2][:, h, :], states[:, t, h, :],
                                         start=False, stop=True)
                last.then_inc(ev("ro_mm"), 1)
                if t + 1 < NT:
                    scores(t + 1)
            modulation(47)
            pe.wait_ge(ev("mod_c"), 5)
            for t in range(NT + 1):
                if t < NT:
                    pe.wait_ge(ev("lat_n"), t + 1)
                if t >= 2:
                    pe.wait_ge(ev("lat_c"), t - 1)
                b = 5 + t % 2
                if t < NT:
                    for j in range(3):
                        last = pe.transpose(quad(b)[:, j, :], z[:, t, j * P:(j + 1) * P], ident)
                else:
                    last = pe.transpose(quad(b)[:, 0, :], cache_in[:, 0:KVRANK], ident)
                last.then_inc(ev("lat_t"), 1)
            arrived(("q_up", 0))
            arrived(("kv_up", 0))
            wq = w_view(("q_up", 0))[:, 0:1536].rearrange("p (k n) -> p k n", k=2)
            wkv = w_view(("kv_up", 0))
            pe.wait_ge(ev("lat_c"), NT + 1)
            pe.wait_ge(ev("onrm"), NT)
            for u in range(len(UNITS) + 1):
                if u < len(UNITS):
                    kind, t = UNITS[u]
                    b = 2 * (u % 2)
                    if u >= 2:
                        pe.wait_ge(ev("raw_a"), u - 1)
                        if UNITS[u - 2][0] == "k":
                            pe.wait_ge(ev("v_c"), (u - 2) // 2 + 1 if u - 2 < 10 else 6)
                    if u == 10:
                        pe.wait_ge(ev("v_c"), 4)
                    for half in range(2):
                        if kind == "q":
                            for k in range(2):
                                last = pe.matmul(PS[:, b + half, 0:384], cT[:, t, k, :],
                                                 wq[:, k, half * 384:half * 384 + 384],
                                                 start=(k == 0), stop=(k == 1))
                        else:
                            lat = cT[:, t, 2, :] if t < NT else cache_cT[:, :]
                            last = pe.matmul(PS[:, b + half, :], lat, wkv[:, half * 512:half * 512 + 512],
                                             start=True, stop=True)
                    last.then_inc(ev("qk_mm"), 1)
                if u >= 1:
                    pe.wait_ge(ev("qk_n"), u)
                    if u >= 2:
                        pe.wait_ge(ev("hd_a"), u - 1)
                        pe.wait_ge(ev("hd_v"), u - 1)
                    raw = qkraw[:, (u - 1) % 2, :].rearrange("p (h n) -> p h n", h=HEADS)
                    for h in range(HEADS):
                        last = pe.transpose(quad(4 + h // 4)[0:QK, h % 4, :], raw[:, h, :], ident)
                    last.then_inc(ev("hd_t"), 1)
            pe.wait_ge(ev("hd_a"), len(UNITS))
            pe.wait_ge(ev("hd_v"), len(UNITS))
            pe.wait_ge(ev("v_c"), NT + 1)
            mod_columns(5)
            pe.wait_ge(ev("mod_c"), 6)
            for i in range(NATT + 3):
                if i < NATT:
                    kind, h, t = ATT[i]
                    b = 2 * (i % 2)
                    if i >= 2:
                        pe.wait_ge(ev("prob"), i - 1)
                    if kind == "lat":
                        for n in range(2):
                            last = pe.matmul(PS[:, b + n, 0:SEG], qT[:, h, t * P:t * P + P],
                                             kT[:, h, n * SEG:(n + 1) * SEG], start=True, stop=True)
                    else:
                        for n in range(4):
                            last = pe.matmul(quad(b)[:, n, :], qT[:, 4 * h + n, SAMPLE:T],
                                             kT[:, 4 * h + n, 640:768], start=True, stop=True)
                    last.then_inc(ev("s_mm"), 1)
                if 2 <= i <= NATT + 1:
                    kind = ATT[i - 2][0]
                    pe.wait_ge(ev("prob_n"), i - 1)
                    if i >= 3:
                        pe.wait_ge(ev("pt_a"), i - 2)
                    if i >= 5:
                        pe.wait_ge(ev("pt_v"), i - 4)
                    for j in range(ST + 1 if kind == "lat" else 4):
                        last = pe.transpose(quad(4 + j // 4)[:, j % 4, :], prob[i % 2][:, j, :], ident)
                    last.then_inc(ev("p_t"), 1)
                if i - 3 in GROUP_END:
                    g = GROUP_END[i - 3]
                    pe.wait_ge(ev("pt_a"), i - 2)
                    if g >= 2:
                        pe.wait_ge(ev("pt_v"), i - 4)
                        pe.wait_ge(ev("o_c"), g - 1)
                    for pair in (range(2) if g < 2 else (0,)):
                        for j in range(ST + 1 if g >= 2 else 1):
                            for hl in range(2):
                                if g < 2:
                                    h = 4 * g + 2 * pair + hl
                                    out = PS[hl * VD:(hl + 1) * VD, 6 + g % 2, pair * P:(pair + 1) * P]
                                    last = pe.matmul(out, vS[:, 5, h, :],
                                                     probT[0][:, g, (2 * pair + hl) * P:(2 * pair + hl + 1) * P],
                                                     start=True, stop=True)
                                else:
                                    last = pe.matmul(PS[hl * VD:(hl + 1) * VD, 6 + g % 2, :],
                                                     vS[:, j, 2 * (g - 2) + hl, :], probT[hl][:, j, :],
                                                     start=(j == 0), stop=(j == ST))
                    last.then_inc(ev("pv_mm"), 1)
            pe.wait_ge(ev("gated"), NT)
            for t in range(NT):
                if t < 2:
                    pe.wait_ge(ev("prob"), NATT)
                if t >= 4:
                    pe.wait_ge(ev("ot_v"), t - 3)
                for j in range(4):
                    last = pe.transpose(quad(t % 4)[:, j, :], oret[:, t, j * P:(j + 1) * P], ident)
                last.then_inc(ev("o_t"), 1)
            pe.wait_ge(ev("o_c"), 6)
            pe.wait_ge(ev("octx_c"), 4)
            pe.wait_ge(ev("ot_v"), NT)
            project_out(0, "ev_out", oT, lambda k: 2 * k if k < 4 else 2 * (k - 4) + 1)

            def moe(l):
                q = 2 * l + 1
                pe.wait_ge(ev("wo_ev"), KD * l + KD)
                norm_sums(q)
                pe.wait_ge(ev("wr_in"), 32 * (l + 1))
                for k in range(KD):
                    for n in range(2):
                        pe.wait_ge(ev("h_s"), KD * q + k + 1)
                        if n == 1:
                            pe.wait_ge(ev("h_c"), KD * q + k + 1)
                        last = pe.matmul(PS[0:ROUTE, 5 * n, 0:SEG], wr[:, k, :], hT[:, k, n * SEG:(n + 1) * SEG],
                                         start=(k == 0), stop=(k == KD - 1))
                last.then_inc(ev("route_mm"), 1)

                def ranks():
                    pe.wait_ge(ev("chosen"), l + 1)
                    place = PS[:, 5, 0:NT * EXPERTS].rearrange("p (t n) -> p t n", t=NT)
                    pe.matmul(place, tri, both[:, :, :], start=True, stop=False)
                    for j in range(NT - 1):
                        n = NT - 1 - j
                        pe.matmul(place[:, j + 1:, :], ones, bc(both[:, j:j + 1, :], [P, n, EXPERTS]),
                                  start=False, stop=(j == NT - 2))
                    for j in range(NT):
                        last = pe.matmul(PS[:, 6, 0:EXPERTS], ones, both[:, j, :], start=(j == 0), stop=(j == NT - 1))
                    last.then_inc(ev("rank_mm"), 1)

                def turn_logits():
                    pe.wait_ge(ev("route_c"), 2 * (l + 1))
                    for t in range(NT):
                        last = pe.transpose(PS[:, 0, t * ROUTE:(t + 1) * ROUTE], rs[0:ROUTE, t * P:(t + 1) * P],
                                            cst[0:ROUTE, C_ID:C_ID + ROUTE])
                    last.then_inc(ev("route_mm"), 1)

                for i in range(2 * NT):
                    t, half = i // 2, i % 2
                    if i >= 4:
                        pe.wait_ge(ev("htok_a"), 2 * NT * l + i - 3)
                    for j in range(4):
                        last = pe.transpose(quad((1, 2, 3, 7)[i % 4])[:, j, :],
                                            hT[:, 4 * half + j, t * P:t * P + P], ident)
                    last.then_inc(ev("htok_t"), 1)
                    if i == 0:
                        turn_logits()
                    if i == 6:
                        ranks()
                pe.wait_ge(ev("htok_a"), 2 * NT * l + 2 * NT)
                for i in range(2 * RT):
                    j, half = i // 2, i % 2
                    if half == 0 and j % 2 == 0:
                        pe.wait_ge(ev(f"rows_back{j // 2}"), 16 * (l + 1))
                    if i >= 4:
                        pe.wait_ge(ev(("xs_v", "xs_a")[i % 2]), RT * l + (i - 4) // 2 + 1)
                    for m in range(4):
                        last = pe.transpose(quad(i % 4)[:, m, :], xback[:, j, (4 * half + m) * P:(4 * half + m + 1) * P],
                                            ident)
                    last.then_inc(ev("xs_t"), 1)
                pe.wait_ge(ev("xs_v"), RT * l + RT)
                pe.wait_ge(ev("xs_a"), RT * l + RT)
                pe.wait_ge(ev("pad"), l + 1)
                pe.wait_ge(ev("tab"), 4 * l + 4)
                n0 = at[(f"expert{l}", 0)]

                def slots(p):
                    return [(n0 + PER_EXPERT * p + j) % SLOTS for j in range(PER_EXPERT)]

                def up(n, p, laps):
                    s = slots(p)
                    pe.wait_ge(ev("act"), n + 1)
                    for k in range(KD):
                        if k % 4 == 0:
                            pe.wait_ge(ev("xblk_c"), 2 * n + (k // 4 + 1))
                            pe.wait_ge(ring_full[s[k // 4]], laps(PER_EXPERT * p + k // 4))
                        w = ring[:, s[k // 4], :].rearrange("p (k a n) -> p k a n", k=4, a=2)
                        for i in range(2):
                            last = pe.matmul(
                                PS[i * BLK:(i + 1) * BLK, 0, 0:2 * P].rearrange("p (a n) -> p a n", a=2),
                                xblk[:, k, :], w[:, k % 4, :, i * P:(i + 1) * P],
                                start=(k == 0), stop=(k == KD - 1))
                        if k % 4 == 3:
                            last.then_inc(ev("up_mm"), 1)

                def turn(n):
                    pe.wait_ge(ev("act"), n + 2)
                    pe.transpose(PS[:, 1, 0:P], gact[:, :], ident).then_inc(ev("h_t"), 1)

                def down(n, p, laps):
                    s = slots(p)
                    w = ring[:, s[2], :].rearrange("p (k n) -> p k n", k=2)
                    pe.wait_ge(ring_full[s[2]], laps(PER_EXPERT * p + 2))
                    pe.wait_ge(ev("hblk_c"), n + 1)
                    pe.wait_ge(ev("yblk_c"), n + 1)
                    for i in range(2):
                        for c in range(2):
                            last = pe.matmul(PS[c * BLK:(c + 1) * BLK, 2, :], hblk[:, i, :],
                                             w[:, i, c * 512:(c + 1) * 512], start=(i == 0), stop=(i == 1))
                    last.then_inc(ev("down_mm"), 1)

                def expert(e, p, laps, next_laps):
                    blocks = pe.value_load(tab[0:1, bass.ds(e + EXPERTS, 1)], min_val=1, max_val=MAXBLK)
                    before = pe.value_load(tab[0:1, bass.ds(e + 2 * EXPERTS, 1)], min_val=0, max_val=2 * ALLBLK)
                    with pe.If(blocks > 1):
                        with pe.Fori(1, blocks) as b:
                            turn(before + b - 1)
                            up(before + b, p, laps)
                            down(before + b - 1, p, laps)
                    end = pe.snap(before + blocks)
                    turn(end - 1)
                    if next_laps is not None:
                        up(end, (p + 1) % RING_EXPERTS, next_laps)
                    down(end - 1, p, laps)

                rounds = EXPERTS // RING_EXPERTS

                def laps_at(g):
                    return lambda c: g * 16 + full_count[n0 + c]

                first = pe.value_load(tab[0:1, 2 * EXPERTS:2 * EXPERTS + 1], min_val=0, max_val=ALLBLK)
                up(first, 0, laps_at(0))
                with pe.Fori(0, rounds) as g:
                    for p in range(RING_EXPERTS):
                        wrap = p == RING_EXPERTS - 1
                        expert(g * RING_EXPERTS + p, p, laps_at(g), laps_at(g + 1 if wrap else g))
                for e in range(rounds * RING_EXPERTS, EXPERTS):
                    expert(e, e % RING_EXPERTS, laps_at(rounds), laps_at(rounds) if e + 1 < EXPERTS else None)
                for i in range(2 * NT):
                    t, half = i // 2, i % 2
                    if half == 0:
                        pe.wait_ge(ev("comb_v"), NT * l + t + 1)
                    if i >= 4:
                        pe.wait_ge(ev("comb"), 2 * NT * l + i - 3)
                    for m in range(4):
                        c = (4 * half + m) * P
                        last = pe.transpose(quad(4 + i % 4)[:, m, :], ygat[:, t, c:c + P], ident)
                    last.then_inc(ev("comb_mm"), 1)

            moe(0)
            pe.wait_ge(ev("comb"), 2 * NT)
            norm_sums(2)

            def gated_in(j):
                arrived(("od_in", j))
                w = w_view(("od_in", j)).rearrange("p (k a n) -> p k a n", k=KD, a=2)
                if j >= 1:
                    pe.wait_ge(ev("sig"), 2 * j)
                    pe.wait_ge(ev("u_w"), 3 * j)
                for a in (1, 0):
                    for k in range(KD):
                        if j == 0 and a == 1:
                            pe.wait_ge(ev("h_s"), 2 * KD + k + 1)
                            pe.wait_ge(ev("h_c"), 2 * KD + k + 1)
                        for n in range(2):
                            last = pe.matmul(PS[:, 2 * a + n, 0:SEG], w[:, k, a, :], hT[:, k, n * SEG:(n + 1) * SEG],
                                             start=(k == 0), stop=(k == KD - 1))
                    if a == 1:
                        last.then_inc(ev("gate_mm"), 1)
                last.then_inc(ev("gate_mm"), 1)

            def taps(j):
                pe.wait_ge(ev("tap_d"), taps_until(j + 1))
                pe.wait_ge(ev("u_w"), 3 * (j + 1))
                if j == 0:
                    pe.wait_ge(ev("u_zero"), 1)
                else:
                    pe.wait_ge(ev("conv_v"), conv_ops(j))
                for w in range(pe_taps(j)):
                    for n, (c0, c1) in enumerate(((0, HALF), (HALF, SPAN))):
                        last = pe.matmul(PS[:, 4 + n, 0:c1 - c0], tap_diag(j, w), upad[:, j, w + c0:w + c1],
                                         start=(w == 0), stop=(w == pe_taps(j) - 1))
                last.then_inc(ev("tap_mm"), 1)

            def ln_sums(src, k, b, name, count):
                pe.wait_ge(ev(name), count)
                for n, (c0, c1) in enumerate(((0, HALF), (HALF, SPAN))):
                    last = pe.matmul(PS[:, b + n, 0:c1 - c0], ones, src[:, k, c0:c1],
                                     start=(k == 0), stop=(k == KD - 1))
                last.then_inc(ev("ln_mm"), 1)

            gated_in(0)
            for j in range(KD):
                if j + 1 < KD:
                    gated_in(j + 1)
                taps(j)
                if j >= 1:
                    ln_sums(cv, j - 1, 6, "conv_v", conv_ops(j))
            ln_sums(cv, KD - 1, 6, "conv_v", conv_ops(KD))
            pe.wait_ge(ev("sig"), 2 * KD)
            pe.wait_ge(ev("u_w"), 3 * KD)
            for k in range(KD):
                ln_sums(cv2, k, 0, "ln_sq", k + 1)
            project_out(1, "od_out", cvn, lambda k: k)
            moe(1)
            pe.wait_ge(ev("comb"), 4 * NT)
            for i in range(2 * NT):
                t, half = i // 2, i % 2
                if i >= 4:
                    pe.wait_ge(ev(("xt_v", "xt_a")[i % 2]), NT + (i - 4) // 2 + 1)
                for j in range(4):
                    last = pe.transpose(quad(4 + i % 4)[:, j, :], xT[:, 4 * half + j, t * P:t * P + P], ident)
                last.then_inc(ev("x_t"), 1)

        @block.scalar
        def _(act):
            step = [0]

            def link(ins):
                step[0] += 1
                ins.then_inc(ev("act_step"), 1)
                act.wait_ge(ev("act_step"), step[0])

            n_param = [0]

            def param(dst, src):
                n_param[0] += 1
                act.dma_start(dst, src).then_inc(ev("params_in"), 16)

            param(cst[:, :], f["consts"])
            v = vrow
            for l in range(2):
                param(v[48 * l:48 * l + 48, 0, :], f["ada_b"][l].rearrange("(r n) -> r n", n=P))
            param(v[96:104, 0, :], f["c"][0].rearrange("(r n) -> r n", n=P))
            param(v[104:112, 0, :], f["c_ctx"].rearrange("(r n) -> r n", n=P))
            param(v[112:128, 0, :], f["norm_mix"].rearrange("l (r n) -> (l r) n", n=P))
            param(v[0:16, 1, :], f["norm_ffn"].rearrange("l (r n) -> (l r) n", n=P))
            param(v[16:24, 1, :], f["od_dw_b"][0].rearrange("(r n) -> r n", n=P))
            param(v[24:32, 1, :], f["od_ln_g"][0].rearrange("(r n) -> r n", n=P))
            param(v[32:40, 1, :], f["od_ln_b"][0].rearrange("(r n) -> r n", n=P))
            param(v[40:44, 1, :], f["ev_ret_gn"][0].rearrange("(r n) -> r n", n=P))
            param(v[44:46, 1, :], f["ev_q_a_norm"][0].rearrange("(r n) -> r n", n=P))
            dw = f["od_dw"][0].rearrange("w (r n) -> (w r) n", n=P)
            param(v[:, 2, :], dw[0:P, :])
            param(v[0:V_ROWS[3], 3, :], dw[P:, :])
            act.dma_start(xtok[:, 0:ST, :], f["x_sample"][0].rearrange("(t p) n -> p t n", p=P)).then_inc(ev("x_in"), 16)
            act.dma_start(xtok[:, ST, :], f["x_prompt"][0]).then_inc(ev("x_in"), 16)

            def router_weights(l):
                act.dma_start(wr[:, :, 0:GROUPS], f["moe_w_group"][l].rearrange("(k p) n -> p k n", p=P)) \
                    .then_inc(ev("wr_in"), 16)
                act.dma_start(wr[:, :, GROUPS:], f["moe_w_expert"][l].rearrange("(k p) n -> p k n", p=P)) \
                    .then_inc(ev("wr_in"), 16)
            router_weights(0)

            act.wait_ge(ev("vec_c"), 4)
            act.wait_ge(ev("sc_zero"), 1)
            act.activation(scT[:, :, 0:2].rearrange("p k a -> p a k"),
                           vecT[:, 0, V_COND:V_COND + 16].rearrange("p (a k) -> p a k", a=2),
                           ACT.Silu).then_inc(ev("sc_ready"), 1)
            for c in range(2):
                act.dma_start(rows_out[ROWS:XW, c * P:(c + 1) * P], cst[0:BLK, C_ID:C_ID + P]) \
                    .then_inc(ev("y_sent"), 16)
            for i in range(1, 2 * NT, 2):
                act.wait_ge(ev("x_t"), i + 1)
                act.activation(xT[:, 4:8, (i // 2) * P:(i // 2 + 1) * P], quad(i % 4), ACT.Copy).then_inc(ev("xt_a"), 1)

            def mod_rows(g):
                act.wait_ge(ev("mod_mm"), KD * (g + 1))
                if g >= 1:
                    act.wait_ge(ev("mod_t"), g)
                act.activation(mrow, PS[:, 7, :], ACT.Copy).then_inc(ev("mrow_c"), 1)

            def decays():
                act.dma_start(states[0:RK, 0, :, :], f["state_retention"][0, 0, 0].rearrange("h k v -> k h v")) \
                    .then_inc(ev("state_in"), 16)
                act.dma_start(states[RK:P, ST - 1, :, :], f["state_retention"][0, 0, 1].rearrange("h k v -> k h v")) \
                    .then_inc(ev("state_in"), 16)
                act.wait_ge(ev("late_in"), 16 * 13)
                link(act.activation(decw[:, 0, :], dec[:, :], ACT.Abs))
                link(act.activation(decw[:, 1, :], decw[:, 0, :], ACT.Exp, scale=-1.0))
                act.activation(decw[:, 2, :], decw[:, 1, :], ACT.Ln, bias=1.0).then_inc(ev("ln_dec"), 1)
                act.wait_ge(ev("edge_arg"), 6)
                act.activation(edge[:, :, :], edge[:, :, :], ACT.Exp).then_inc(ev("edge_e"), 1)
                for h in range(RH):
                    for d in range(2):
                        a = D_A1 if d == 0 else D_A2
                        act.activation(mtmp[:, 2 * h + d, :], dist[:, a:a + P], ACT.Exp,
                                       scale=dec[:, d * RH + h:d * RH + h + 1]).then_inc(ev("mask_e"), 1)

            def norm(q, ready):
                l = q // 2
                for k in range(KD):
                    ready(k)
                    act.activation(squares(q)[:, k, :], xT[:, k, :], ACT.Square).then_inc(ev("squared"), 1)
                act.wait_ge(ev("sumsq"), q + 1)
                act.activation(rs[:, 0:SAMPLE], PS[:, 4, :], ACT.Sqrt, bias=eps, scale=1.0 / D).then_inc(ev("root"), 1)
                act.activation(rs[:, SAMPLE:T], PS[:, 6, 0:CONTEXT], ACT.Sqrt, bias=eps, scale=1.0 / D) \
                    .then_inc(ev("root"), 1)
                if q == 0:
                    decays()
                    mod_rows(0)
                act.wait_ge(ev("coef"), q + 1)
                for k in range(KD):
                    act.wait_ge(ev("hn"), 2 * KD * q + 2 * k + 1)
                    act.activation(hT[:, k, 0:SAMPLE], hT[:, k, 0:SAMPLE], ACT.Identity,
                                   bias=modT[:, l, 24 * (q % 2) + k, 0:1], scale=modA[:, q, k, 0:1]) \
                        .then_inc(ev("h_s"), 1)

            def x_ready(k):
                if k == 0:
                    act.wait_ge(ev("xt_v"), NT)
                    act.wait_ge(ev("xt_a"), NT)
            norm(0, x_ready)
            for i in range(1, 8 * NT, 2):
                c, t = i // NT, i % NT
                if i in (3 * NT, 6 * NT + 1):
                    mod_rows(1 if i == 3 * NT else 2)
                n = min(256, EVEN_IN - 256 * c)
                act.wait_ge(ev("z_mm"), i + 1)
                act.activation(z[:, t, 256 * c:256 * c + n], PS[:, i % 4, 0:n], ACT.Copy).then_inc(ev("z_a"), 1)
            mod_rows(3)
            act.wait_ge(ev("z_v"), 4 * NT)
            act.wait_ge(ev("z_a"), 4 * NT)
            act.wait_ge(ev("mask_v"), RH)
            for t in range(NT):
                act.activation(oret[:, t, :], oret[:, t, :], ACT.Silu).then_inc(ev("silu_g"), 1)
            for t in range(NT):
                link(act.activation(qksq[:, 0, 0:QRANK], z[:, t, 0:QRANK], ACT.Square, accum_out=ss[:, 0, t:t + 1]))
                link(act.activation(qksq[:, 0, 0:KVRANK], z[:, t, QRANK:Z_KR], ACT.Square,
                                    accum_out=ss[:, 0, 8 + t:9 + t]))
            act.activation(ss[:, 1, 0:NT], ss[:, 0, 0:NT], ACT.Sqrt, bias=eps, scale=1.0 / QRANK) \
                .then_inc(ev("lat_root"), 1)
            act.activation(ss[:, 1, 8:8 + NT], ss[:, 0, 8:8 + NT], ACT.Sqrt, bias=eps, scale=1.0 / KVRANK) \
                .then_inc(ev("lat_root"), 1)
            mod_rows(4)

            def take_qk(t):
                act.wait_ge(ev("rqk_t"), t + 1)
                if t >= 2:
                    act.wait_ge(ev("rs_mm"), t - 1)
                act.activation(rqkT[t % 2], quad(t % 2), ACT.Copy).then_inc(ev("rqk_c"), 1)

            def take_qfb(t):
                act.wait_ge(ev("qfb_t"), t + 1)
                if t >= 2:
                    act.wait_ge(ev("ro_mm"), t - 1)
                act.activation(qfbT[t % 2], quad(2), ACT.Copy).then_inc(ev("qfb_c"), 1)

            def normalise(t):
                act.wait_ge(ev("gn_v"), t + 1)
                act.activation(rmv[:, :], mv[:, :, 1], ACT.Sqrt, bias=eps).then_inc(ev("gn_root"), 1)
                act.wait_ge(ev("gn_b"), t + 1)
                if t >= 1:
                    act.wait_ge(ev("gated"), t)
                for h in range(RH):
                    ins = act.activation(onrm[:, h, :], quad(4 + t % 2)[:, h, :], ACT.Identity,
                                         bias=rmv[:, h:h + 1], scale=mv[:, h, 1:2])
                ins.then_inc(ev("onrm"), 1)

            take_qk(0)
            take_qfb(0)
            for t in range(NT):
                if t + 1 < NT:
                    take_qk(t + 1)
                    if t + 1 < ST:
                        take_qfb(t + 1)
                if t >= 1:
                    normalise(t - 1)
            normalise(NT - 1)
            for u, (kind, t) in enumerate(UNITS):
                raw = qkraw[:, u % 2, :].rearrange("p (h n) -> p h n", h=HEADS)
                act.wait_ge(ev("qk_mm"), u + 1)
                if u >= 2:
                    act.wait_ge(ev("hd_t"), u - 1)
                b = 2 * (u % 2)
                for half in range(2):
                    if kind == "q":
                        ins = act.activation(raw[:, 4 * half:4 * half + 4, :],
                                             PS[:, b + half, 0:384].rearrange("p (h n) -> p h n", h=4), ACT.Copy)
                    else:
                        ins = act.activation(raw[:, 4 * half:4 * half + 4, 0:NOPE],
                                             quad(b + half)[:, :, 0:NOPE], ACT.Copy)
                    if half == 0:
                        link(ins)
                ins.then_inc(ev("raw_a"), 1)
                act.wait_ge(ev("raw_a"), u + 1)
                if kind == "k":
                    act.wait_ge(ev("kr_p"), t + 1)
                if u >= 1:
                    act.wait_ge(ev("hsum"), u)
                act.activation(qksq[:, 0, :], qkraw[:, u % 2, :], ACT.Square).then_inc(ev("qk_sq"), 1)
                act.wait_ge(ev("hsum"), u + 1)
                act.activation(ss[:, 1, 0:HEADS], ss[:, 0, 0:HEADS], ACT.Sqrt, bias=eps, scale=1.0 / QK) \
                    .then_inc(ev("hroot"), 1)
                if u >= 1:
                    k2, t2 = UNITS[u - 1]
                    col = t2 * P if k2 == "q" else KCOL[t2]
                    dst = qT if k2 == "q" else kT
                    act.wait_ge(ev("hd_t"), u)
                    if u == 2:
                        act.wait_ge(ev("side_out"), 64)
                    gain = gcol[0:QK, 0:1] if k2 == "q" else gcol[0:QK, 1:2]
                    act.activation(dst[:, 0:4, col:col + P], quad(4)[0:QK], ACT.Copy, scale=gain) \
                        .then_inc(ev("hd_a"), 1)
            act.wait_ge(ev("hd_t"), len(UNITS))
            act.activation(kT[:, 0:4, KCOL[NT]:KCOL[NT] + P], quad(4)[0:QK], ACT.Copy, scale=gcol[0:QK, 1:2]) \
                .then_inc(ev("hd_a"), 1)
            mod_rows(5)
            for i in range(NATT + 3):
                if i < NATT:
                    act.wait_ge(ev("nmax"), i + 1)
                    if i >= 2:
                        act.wait_ge(ev("p_t"), i - 1)
                    if ATT[i][0] == "lat":
                        act.activation(prob[i % 2],
                                       PS[:, 2 * (i % 2):2 * (i % 2) + 2, 0:SEG],
                                       ACT.Exp, bias=nmx[:, i % 2:i % 2 + 1], accum_out=den[:, i % 2:i % 2 + 1]) \
                            .then_inc(ev("prob"), 1)
                    else:
                        act.activation(prob[i % 2][:, 0:4, :], prob[i % 2][:, 0:4, :], ACT.Exp) \
                            .then_inc(ev("prob"), 1)
                if 2 <= i <= NATT + 1:
                    kind, h, t = ATT[i - 2]
                    act.wait_ge(ev("p_t"), i - 1)
                    if kind == "lat":
                        act.wait_ge(ev("pv_mm"), groups_before(i - 2))
                        act.activation(probT[h % 2][:, 0:4, t * P:t * P + P], quad(4), ACT.Copy) \
                            .then_inc(ev("pt_a"), 1)
                    else:
                        act.activation(probT[0][:, h, :], PS[:, 4, :], ACT.Copy).then_inc(ev("pt_a"), 1)
                if i - 3 in GROUP_END:
                    g = GROUP_END[i - 3]
                    act.wait_ge(ev("pv_mm"), g + 1)
                    if g < 2:
                        act.activation(octx[:, 2 * g:2 * g + 2, :],
                                       PS[:, 6 + g % 2, 0:2 * P].rearrange("p (k t) -> p k t", k=2), ACT.Copy) \
                            .then_inc(ev("o_c"), 1)
                    else:
                        act.activation(oT[:, 2 * (g - 2), 0:SAMPLE], PS[:, 6 + g % 2, :], ACT.Copy) \
                            .then_inc(ev("o_c"), 1)

            def moe(l):
                q = 2 * l + 1
                norm(q, lambda k: act.wait_ge(ev("wo_ev"), KD * l + k + 1))
                act.wait_ge(ev("gdiff"), l + 1)
                act.activation(rt[:, 0, :, 0:GROUPS], rt[:, 0, :, 0:GROUPS], ACT.Exp).then_inc(ev("gexp"), 1)
                for i in range(2 * NT):
                    t, half = i // 2, i % 2
                    act.wait_ge(ev("htok_t"), 2 * NT * l + i + 1)
                    act.activation(htok[:, t, 512 * half:512 * half + 512], PS[:, (1, 2, 3, 7)[i % 4], :], ACT.Copy) \
                        .then_inc(ev("htok_a"), 1)
                    if i == 3:
                        act.wait_ge(ev("ediff"), l + 1)
                        act.activation(r1[:, 4, :], r1[:, 4, :], ACT.Exp).then_inc(ev("eexp"), 1)
                act.wait_ge(ev("rows_sent"), 16 * 2 * NT * (l + 1))
                for j in range(RT // 2):
                    act.dma_start(xback[:, 2 * j:2 * j + 2, :],
                                  rows_in[2 * j * P:(2 * j + 2) * P, :].rearrange("(j p) n -> p j n", p=P)) \
                        .then_inc(ev(f"rows_back{j}"), 16)
                for i in range(1, 2 * RT, 2):
                    j = i // 2
                    act.wait_ge(ev("xs_t"), 2 * RT * l + i + 1)
                    act.activation(xsT[:, 4:8, j * P:(j + 1) * P], quad(i % 4), ACT.Copy).then_inc(ev("xs_a"), 1)
                act.wait_ge(ev("tab"), 4 * l + 4)

                act.wait_ge(ev("yblk_c"), 1)
                first = act.value_load(tab[0:1, 2 * EXPERTS:2 * EXPERTS + 1], min_val=0, max_val=ALLBLK)
                end = act.value_load(tab[0:1, 3 * EXPERTS:3 * EXPERTS + 1], min_val=EXPERTS, max_val=2 * ALLBLK)
                with act.Fori(first, end) as n:
                    act.wait_ge(ev("act"), n + 1)
                    act.activation(tick[:, 3:4], eps, ACT.Silu)
                    act.wait_ge(ev("up_mm"), 2 * n + 4)
                    act.activation(gsil[:, :], PS[:, 0, 0:P], ACT.Silu).then_inc(ev("silu"), 1)
                act.wait_ge(ev("y_sent"), end * 32 + 32)
                act.activation(tick[:, 2:3], eps, ACT.Copy).then_inc(ev("results_sent"), 1)
                for t in range(NT):
                    act.wait_ge(ev(f"picked{t}"), 32 * (l + 1))
                    act.activation(ygat[:, t, :], ygat[:, t, :], ACT.Copy, scale=wtok[:, 0, t:t + 1]) \
                        .then_inc(ev("y0_w"), 1)
                if l == 0:
                    act.wait_ge(ev("route_mm"), 1)
                    router_weights(1)

            moe(0)
            norm(2, lambda k: act.wait_ge(ev("comb"), 2 * NT))
            for j in range(KD):
                act.wait_ge(ev("gate_mm"), 2 * j + 1)
                if j >= 1:
                    act.wait_ge(ev("u_w"), 3 * j)
                for n in range(2):
                    act.activation(rs[:, n * SEG:(n + 1) * SEG], PS[:, 2 + n, 0:SEG], ACT.Sigmoid) \
                        .then_inc(ev("sig"), 1)
            for k in range(KD):
                act.wait_ge(ev("ln_d"), 2 * (k + 1))
                act.activation(cv2[:, k, :], cv[:, k, :], ACT.Square).then_inc(ev("ln_sq"), 1)
            act.wait_ge(ev("ln_mm"), 2 * KD)
            for n, (c0, c1) in enumerate(((0, HALF), (HALF, SPAN))):
                act.activation(scratch[:, c0:c1], PS[:, n, 0:c1 - c0], ACT.Sqrt, bias=eps, scale=1.0 / CONV) \
                    .then_inc(ev("ln_root"), 1)
            for k in range(KD):
                act.wait_ge(ev("ln_n"), 2 * (k + 1))
                act.activation(cvn[:, k, :], cvn[:, k, :], ACT.Silu,
                               bias=vecT[:, 1, V_LNB + k:V_LNB + k + 1],
                               scale=vecT[:, 1, V_LNG + k:V_LNG + k + 1]).then_inc(ev("act1"), 1)
            moe(1)
            for i in range(1, 2 * NT, 2):
                t = i // 2
                act.wait_ge(ev("x_t"), 2 * NT + i + 1)
                act.activation(xtok[:, t, 512:D], PS[:, 4 + i % 4, :], ACT.Copy).then_inc(ev("xt_a"), 1)

        @block.vector
        def _(dve):
            step = [0]

            def link(ins):
                step[0] += 1
                ins.then_inc(ev("dve_step"), 1)
                dve.wait_ge(ev("dve_step"), step[0])

            def tt(out, a, b, op):
                return dve.tensor_tensor(out, a, b, op)

            dve.wait_ge(ev("vec_t"), 1)
            for g, r in enumerate(V_ROWS):
                dve.tensor_copy(vecT[:, g, 0:r], PS[:, 5, g * P:g * P + r]).then_inc(ev("vec_c"), 1)
            for i in range(0, 2 * NT, 2):
                dve.wait_ge(ev("x_t"), i + 1)
                dve.tensor_copy(xT[:, 0:4, (i // 2) * P:(i // 2 + 1) * P], quad(i % 4)).then_inc(ev("xt_v"), 1)

            def mod_bias(g):
                dve.wait_ge(ev("mod_t"), g + 1)
                bias = vecT[:, 0, 16 * g:16 * g + 16].rearrange("p (c q) -> p c q", c=4).unsqueeze(3)
                out = modT[:, g // 3, 16 * (g % 3):16 * (g % 3) + 16, :].rearrange("p (c q) a -> p c q a", c=4)
                src = quad(5 if g == 0 else 6).rearrange("p q (c a) -> p c q a", c=4)[:, :, :, 0:2]
                tt(out, src, bc(bias, [P, 4, 4, 2]), ALU.add).then_inc(ev("mod_c"), 1)

            def coef(q):
                l = q // 2
                base = (V_NMIX if q % 2 == 0 else V_NFFN) + 8 * l
                g = vecT[:, q % 2, base:base + KD].unsqueeze(2)
                s = 24 * (q % 2) + 8
                dve.scalar_tensor_tensor(out=modA[:, q, :, :], in0=modT[:, l, s:s + KD, :], scalar=1.0,
                                         in1=bc(g, [P, KD, 2]), op0=ALU.add, op1=ALU.mult).then_inc(ev("coef"), 1)

            def normed(q):
                dve.wait_ge(ev("root"), 2 * q + 2)
                link(dve.reciprocal(PS[:, 4, :], rs[:, 0:SAMPLE]))
                link(dve.reciprocal(PS[:, 6, 0:CONTEXT], rs[:, SAMPLE:T]))
                for k in range(KD):
                    tt(hT[:, k, 0:SAMPLE], xT[:, k, 0:SAMPLE], PS[:, 4, :], ALU.mult).then_inc(ev("hn"), 1)
                    tt(hT[:, k, SAMPLE:T], xT[:, k, SAMPLE:T], PS[:, 6, 0:CONTEXT], ALU.mult).then_inc(ev("hn"), 1)

            dve.wait_ge(ev("xt_a"), NT)
            dve.wait_ge(ev("xt_v"), NT)
            normed(0)
            dve.wait_ge(ev("ln_dec"), 1)
            link(dve.scalar_tensor_tensor(out=dec[:, :], in0=dec[:, :], scalar=0.0, in1=decw[:, 2, :],
                                          op0=ALU.min, op1=ALU.subtract))
            for n, d in enumerate((0, 0, 1, 1)):
                dve.tensor_scalar(edge[:, n, :], dec[:, d * RH:(d + 1) * RH], cst[:, C_POS + n:C_POS + n + 1], None,
                                  ALU.mult).then_inc(ev("edge_arg"), 1)
            for d in range(2):
                dve.tensor_scalar(edge[:, 4 + d, :], dec[:, d * RH:(d + 1) * RH], float(P), None, ALU.mult) \
                    .then_inc(ev("edge_arg"), 1)
            dve.wait_ge(ev("edge_e"), 1)
            link(dve.tensor_scalar(edge[:, 0, :], edge[:, 0, :], RK ** -0.5, None, ALU.mult))
            link(dve.tensor_scalar(edge[:, 2, :], edge[:, 2, :], RK ** -0.5, None, ALU.mult))
            for h in range(RH):
                dve.wait_ge(ev("mask_e"), 2 * h + 2)
                link(tt(mtmp[:, 2 * h, :], mtmp[:, 2 * h, :], dist[:, D_U:D_U + P], ALU.mult))
                link(tt(mtmp[:, 2 * h + 1, :], mtmp[:, 2 * h + 1, :], dist[:, D_L:D_L + P], ALU.mult))
                link(tt(mtmp[:, 2 * h, :], mtmp[:, 2 * h, :], mtmp[:, 2 * h + 1, :], ALU.add))
                dve.tensor_scalar(mask[:, h, :], mtmp[:, 2 * h, :], RK ** -0.5, None, ALU.mult).then_inc(ev("mask_v"), 1)
            mod_bias(0)
            dve.wait_ge(ev("mod_c"), 1)
            coef(0)
            for i in range(0, 8 * NT, 2):
                c, t = i // NT, i % NT
                if i in (3 * NT + 1, 6 * NT):
                    mod_bias(1 if i == 3 * NT + 1 else 2)
                n = min(256, EVEN_IN - 256 * c)
                dve.wait_ge(ev("z_mm"), i + 1)
                dve.tensor_copy(z[:, t, 256 * c:256 * c + n], PS[:, i % 4, 0:n]).then_inc(ev("z_v"), 1)
            dve.wait_ge(ev("z_a"), 4 * NT)
            dve.wait_ge(ev("z_v"), 4 * NT)

            def by_edge(out, t, off, n):
                src = z[:, t, off:off + RH * RK].rearrange("p (h n) -> p h n", h=RH)
                return tt(out, src, bc(edge[:, n, :].unsqueeze(2), [P, RH, RK]), ALU.mult)

            for t in range(NT):
                if t >= 1:
                    dve.wait_ge(ev("upd_mm"), t)
                link(by_edge(kfb[:, :, 0:RK], t, Z_RK, 0))
                by_edge(kfb[:, :, RK:P], t, Z_RK, 2).then_inc(ev("kfb"), 1)
                dve.wait_ge(ev("upd_mm"), t + 1)
                dve.tensor_copy(upd[:, t, :, :], quad(t % 2)).then_inc(ev("upd_c"), 1)
                if t in (0, NT - 1):
                    mod_bias(3 if t == 0 else 4)
            dve.wait_ge(ev("state_in"), 32)
            dve.wait_ge(ev("upd_c"), NT)
            for j in range(ST - 1):
                for h in range(RH):
                    ins = dve.scalar_tensor_tensor(
                        out=states[0:RK, j + 1, h, :], in0=states[0:RK, j, h, :], scalar=edge[0:RK, 4, h:h + 1],
                        in1=upd[0:RK, j, h, :], op0=ALU.mult, op1=ALU.add)
                r = ST - 1 - j
                for h in range(RH):
                    ins = dve.scalar_tensor_tensor(
                        out=states[RK:P, r - 1, h, :], in0=states[RK:P, r, h, :], scalar=edge[RK:P, 5, h:h + 1],
                        in1=upd[RK:P, r, h, :], op0=ALU.mult, op1=ALU.add)
                ins.then_inc(ev("states"), 1)
                dve.wait_ge(ev("states"), j + 1)
            dve.wait_ge(ev("mask_v"), RH)
            def decay_q(t):
                if t >= 1:
                    dve.wait_ge(ev("qfb_t"), t)
                link(by_edge(qfb[:, :, 0:RK], t, Z_RQ, 1))
                by_edge(qfb[:, :, RK:P], t, Z_RQ, 3).then_inc(ev("qfb"), 1)

            def group_norm(t):
                dve.wait_ge(ev("ro_mm"), t + 1)
                for h in range(RH):
                    ins = dve.bn_stats(stat[:, h, :], quad(4 + t % 2)[:, h, :])
                link(ins)
                for h in range(RH):
                    ins = dve.bn_aggr(mv[:, h, :], stat[:, h, :])
                ins.then_inc(ev("gn_v"), 1)
                dve.wait_ge(ev("gn_root"), t + 1)
                link(dve.reciprocal(mv[:, :, 1], rmv[:, :]))
                dve.scalar_tensor_tensor(out=rmv[:, :], in0=mv[:, :, 0], scalar=-1.0, in1=mv[:, :, 1],
                                         op0=ALU.mult, op1=ALU.mult).then_inc(ev("gn_b"), 1)

            def gate(t):
                dve.wait_ge(ev("onrm"), t + 1)
                dve.wait_ge(ev("silu_g"), t + 1)
                tt(oret[:, t, :], oret[:, t, :], arena[:, A_V + 1536:A_V + 2048], ALU.mult).then_inc(ev("gated"), 1)

            decay_q(0)
            for t in range(NT):
                dve.wait_ge(ev("rs_mm"), t + 1)
                if t >= 2:
                    dve.wait_ge(ev("ro_mm"), t - 1)
                for hl in range(2):
                    ins = tt(rsc[t % 2][:, hl::2, :], quad(3 + 3 * hl)[:, 0:2, :], mask[:, hl::2, :], ALU.mult)
                ins.then_inc(ev("rsc"), 1)
                if t + 1 < ST:
                    decay_q(t + 1)
                if t >= 2:
                    gate(t - 2)
                if t >= 1:
                    group_norm(t - 1)
            gate(NT - 2)
            group_norm(NT - 1)
            gate(NT - 1)
            dve.wait_ge(ev("gated"), NT)
            dve.wait_ge(ev("lat_root"), 2)
            link(dve.reciprocal(ss[:, 1, 0:NT], ss[:, 1, 0:NT]))
            link(dve.reciprocal(ss[:, 1, 8:8 + NT], ss[:, 1, 8:8 + NT]))
            for t in range(NT):
                dve.tensor_scalar(z[:, t, 0:QRANK], z[:, t, 0:QRANK], ss[:, 1, t:t + 1], None, ALU.mult)
                dve.scalar_tensor_tensor(out=z[:, t, QRANK:Z_KR], in0=z[:, t, QRANK:Z_KR],
                                         scalar=ss[:, 1, 8 + t:9 + t], in1=kvg[:, :],
                                         op0=ALU.mult, op1=ALU.mult).then_inc(ev("lat_n"), 1)
            link(dve.tensor_scalar(qkg[:, 0, :], qkg[:, 0, :], QK ** -0.5, None, ALU.mult))
            link(dve.tensor_scalar(gcol[0:NOPE, 0:1], gcol[0:NOPE, 0:1], QK ** -0.5, None, ALU.mult))
            tt(tick[:, 0:1], cst[:, 0:1], cst[:, 0:1], ALU.mult).then_inc(ev("qkg_s"), 1)
            for t in range(NT + 1):
                dve.wait_ge(ev("lat_t"), t + 1)
                b = 5 + t % 2
                if t < NT:
                    for j in range(2):
                        dve.tensor_scalar(cT[:, t, j, :], quad(b)[:, j, :], vecT[:, 1, V_QA + j:V_QA + j + 1], None,
                                          ALU.mult)
                    dve.tensor_copy(cT[:, t, 2, :], quad(b)[:, 2, :]).then_inc(ev("lat_c"), 1)
                else:
                    dve.tensor_copy(cache_cT[:, :], quad(b)[:, 0, :]).then_inc(ev("lat_c"), 1)
            for u, (kind, t) in enumerate(UNITS):
                raw = qkraw[:, u % 2, :].rearrange("p (h n) -> p h n", h=HEADS)
                b = 2 * (u % 2)
                if kind == "k":
                    dve.wait_ge(ev("raw_a"), u + 1)
                    for half in range(2):
                        ins = dve.tensor_copy(vS[:, VROW[t], 4 * half:4 * half + 4, :],
                                              quad(b + half)[:, :, NOPE:NOPE + VD])
                    ins.then_inc(ev("v_c"), 1)
                dve.wait_ge(ev("qk_sq"), u + 1)
                dve.tensor_reduce(ss[:, 0, 0:HEADS], qksq[:, 0, :].rearrange("p (h n) -> p h n", h=HEADS), AX.X,
                                  ALU.add).then_inc(ev("hsum"), 1)
                dve.wait_ge(ev("hroot"), u + 1)
                link(dve.reciprocal(ss[:, 0, 8:16], ss[:, 1, 0:HEADS]))
                tt(raw, raw, bc(ss[:, 0, 8:16].unsqueeze(2), [P, HEADS, QK]), ALU.mult).then_inc(ev("qk_r"), 1)
                if u >= 1:
                    k2, t2 = UNITS[u - 1]
                    col = t2 * P if k2 == "q" else KCOL[t2]
                    dst = qT if k2 == "q" else kT
                    dve.wait_ge(ev("hd_t"), u)
                    if u == 2:
                        dve.wait_ge(ev("side_out"), 64)
                    gain = gcol[0:QK, 0:1] if k2 == "q" else gcol[0:QK, 1:2]
                    dve.tensor_scalar(dst[:, 4:8, col:col + P], quad(5)[0:QK], gain, None, ALU.mult) \
                        .then_inc(ev("hd_v"), 1)
            dve.wait_ge(ev("hd_t"), len(UNITS))
            dve.tensor_scalar(kT[:, 4:8, KCOL[NT]:KCOL[NT] + P], quad(5)[0:QK], gcol[0:QK, 1:2], None, ALU.mult) \
                .then_inc(ev("hd_v"), 1)
            mod_bias(5)
            dve.wait_ge(ev("mod_c"), 6)
            coef(1)
            coef(2)
            coef(3)
            for i in range(NATT + 3):
                if i >= 3 and ATT[i - 3][0] == "lat":
                    kind, h, t = ATT[i - 3]
                    dve.wait_ge(ev("p_t"), i - 2)
                    dve.wait_ge(ev("pv_mm"), groups_before(i - 3))
                    dve.tensor_copy(probT[h % 2][:, 4, t * P:t * P + P], quad(5)[:, 0, :]).then_inc(ev("pt_v"), 1)
                if i < NATT:
                    dve.wait_ge(ev("s_mm"), i + 1)
                    if i >= 2:
                        dve.wait_ge(ev("prob"), i - 1)
                    if ATT[i][0] == "lat":
                        dve.tensor_reduce(nmx[:, i % 2:i % 2 + 1], PS[:, 2 * (i % 2):2 * (i % 2) + 2, 0:SEG], AX.XY,
                                          ALU.max, negate=True).then_inc(ev("nmax"), 1)
                    else:
                        link(dve.tensor_reduce(cmx[:, i, :], quad(2 * i), AX.X, ALU.max, negate=True))
                        tt(prob[i][:, 0:4, :], quad(2 * i), bc(cmx[:, i, :].unsqueeze(2), [P, 4, P]), ALU.add) \
                            .then_inc(ev("nmax"), 1)
                if 1 <= i <= NATT:
                    b = (i - 1) % 2
                    dve.wait_ge(ev("prob"), i)
                    if ATT[i - 1][0] == "lat":
                        link(dve.reciprocal(rden[:, b:b + 1], den[:, b:b + 1]))
                        dve.tensor_scalar(prob[b], prob[b], rden[:, b:b + 1], None, ALU.mult) \
                            .then_inc(ev("prob_n"), 1)
                    else:
                        p4 = prob[b][:, 0:4, :]
                        link(dve.tensor_reduce(cmx[:, b, :], p4, AX.X, ALU.add))
                        link(dve.reciprocal(cmx[:, b, :], cmx[:, b, :]))
                        tt(p4, p4, bc(cmx[:, b, :].unsqueeze(2), [P, 4, P]), ALU.mult).then_inc(ev("prob_n"), 1)
            for t in range(NT):
                dve.wait_ge(ev("o_t"), t + 1)
                for j in range(4):
                    ins = dve.tensor_scalar(oT[:, 2 * j + 1, t * P:t * P + P], quad(t % 4)[:, j, :],
                                            vecT[:, 1, V_GN + j:V_GN + j + 1], None, ALU.mult)
                ins.then_inc(ev("ot_v"), 1)

            def add_out(l):
                for m in range(KD):
                    dve.wait_ge(ev("wo_mm"), KD * l + m + 1)
                    b = 4 + 2 * (m % 2)
                    for n, c0, c1, who in ((0, 0, SEG, 0), (1, SEG, SAMPLE, 0), (1, SAMPLE, T, 1)):
                        last = dve.scalar_tensor_tensor(
                            out=xT[:, m, c0:c1], in0=PS[:, b + n, c0 - n * SEG:c1 - n * SEG],
                            scalar=modT[:, l, 16 + m, who:who + 1], in1=xT[:, m, c0:c1], op0=ALU.mult, op1=ALU.add)
                    last.then_inc(ev("wo_ev"), 1)
            add_out(0)

            def moe(l):
                q = 2 * l + 1
                dve.wait_ge(ev("wo_ev"), KD * l + KD)
                normed(q)
                dve.wait_ge(ev("route_mm"), 2 * l + 1)
                for n in range(2):
                    dve.tensor_copy(rs[0:ROUTE, n * SEG:(n + 1) * SEG], PS[0:ROUTE, 5 * n, 0:SEG]) \
                        .then_inc(ev("route_c"), 1)
                dve.wait_ge(ev("route_mm"), 2 * l + 2)
                link(tt(lgt[:, :, :], PS[:, 0, 0:NT * ROUTE].rearrange("p (t n) -> p t n", t=NT),
                        bc(rb[:, l, :].unsqueeze(1), [P, NT, ROUTE]), ALU.add))
                lg = lgt[:, :, 0:GROUPS]
                le = lgt[:, :, GROUPS:ROUTE]
                g4 = [P, NT, GROUPS]
                g8 = [P, NT, PER]
                g48 = [P, NT, GROUPS, PER]

                def w4(i):
                    return rt[:, i, :, 0:GROUPS]

                def w8(i):
                    return rt[:, i, :, :]

                def col(i, n):
                    return bc(r1[:, i, :].unsqueeze(2), [P, NT, n])

                link(dve.tensor_reduce(r1[:, 0, :], lg, AX.X, ALU.max))
                tt(w4(0), lg, col(0, GROUPS), ALU.subtract).then_inc(ev("gdiff"), 1)
                link(tt(w4(1), lg, col(0, GROUPS), ALU.is_equal))
                link(tt(w4(1), w4(1), bc(cst[:, C_PRI4:C_PRI4 + GROUPS].unsqueeze(1), g4), ALU.mult))
                link(dve.tensor_reduce(r1[:, 1, :], w4(1), AX.X, ALU.max))
                link(tt(w4(2), w4(1), col(1, GROUPS), ALU.is_equal))
                b48 = both[:, :, :].rearrange("p t (g e) -> p t g e", g=GROUPS)
                for t in range(NT):
                    ins = tt(b48[:, t], le[:, t].rearrange("p (g e) -> p g e", g=GROUPS),
                             bc(w4(2)[:, t].unsqueeze(2), [P, GROUPS, PER]), ALU.mult)
                link(ins)
                link(dve.tensor_reduce(w8(3), b48.rearrange("p t g e -> p t e g"), AX.X, ALU.add))
                for src, mx, eq, hot in ((3, 2, 4, 5), (6, 3, 7, 8)):
                    link(dve.tensor_reduce(r1[:, mx, :], w8(src), AX.X, ALU.max))
                    link(tt(w8(eq), w8(src), col(mx, PER), ALU.is_equal))
                    link(tt(w8(eq), w8(eq), bc(cst[:, C_PRI8:C_PRI8 + PER].unsqueeze(1), g8), ALU.mult))
                    link(dve.tensor_reduce(r1[:, 5, :], w8(eq), AX.X, ALU.max))
                    link(tt(w8(hot), w8(eq), col(5, PER), ALU.is_equal))
                    if src == 3:
                        link(dve.scalar_tensor_tensor(out=w8(6), in0=w8(5), scalar=-3.0e38, in1=w8(3),
                                                      op0=ALU.mult, op1=ALU.add))
                tt(r1[:, 4, :], r1[:, 3, :], r1[:, 2, :], ALU.subtract).then_inc(ev("ediff"), 1)
                for c in range(2):
                    o48 = one32[:, c, :, :].rearrange("p t (g e) -> p t g e", g=GROUPS)
                    for t in range(NT):
                        ins = tt(o48[:, t], bc(w4(2)[:, t].unsqueeze(2), [P, GROUPS, PER]),
                                 bc(w8(5 + 3 * c)[:, t].unsqueeze(1), [P, GROUPS, PER]), ALU.mult)
                    link(ins)
                tt(both[:, :, :], one32[:, 0, :, :], one32[:, 1, :, :], ALU.add).then_inc(ev("chosen"), 1)
                dve.wait_ge(ev("gexp"), l + 1)
                link(dve.tensor_reduce(r1[:, 6, :], w4(0), AX.X, ALU.add))
                link(dve.reciprocal(r1[:, 7, :], r1[:, 6, :]))
                dve.wait_ge(ev("eexp"), l + 1)
                link(dve.tensor_scalar(r1[:, 8, :], r1[:, 4, :], 1.0, None, ALU.add))
                link(dve.reciprocal(r1[:, 9, :], r1[:, 8, :]))
                link(tt(wtok[:, 0, :], r1[:, 9, :], r1[:, 7, :], ALU.mult))
                tt(wtok[:, 1, :], wtok[:, 0, :], r1[:, 4, :], ALU.mult)
                dve.wait_ge(ev("rank_mm"), l + 1)
                one = cst[:, C_ONE:C_ONE + EXPERTS]
                link(dve.tensor_copy(cnt[:, 0, :], PS[:, 6, 0:EXPERTS]))
                link(dve.tensor_tensor_scan(cnt[:, 1, :], one, cnt[:, 0, :], 0.0, ALU.mult, ALU.add))
                link(tt(cnt[:, 1, :], cnt[:, 1, :], cnt[:, 0, :], ALU.subtract))
                link(tt(slotpos[:, :, :], PS[:, 5, 0:NT * EXPERTS].rearrange("p (t n) -> p t n", t=NT),
                        bc(cnt[:, 1, :].unsqueeze(1), [P, NT, EXPERTS]), ALU.add))
                for c in range(2):
                    link(tt(one32[:, c, :, :], one32[:, c, :, :], slotpos[:, :, :], ALU.mult))
                    link(dve.tensor_reduce(posf[:, c, :], one32[:, c, :, :], AX.X, ALU.add))
                dve.tensor_copy(posu[:, :], posf[:, :, :].rearrange("p c t -> p (c t)")).then_inc(ev("pos"), 1)
                link(tt(cmpt[:, :, :], bc(cnt[:, 0, :].unsqueeze(2), [P, EXPERTS, MAXBLK - 1]),
                        bc(cst[:, C_THR:C_THR + MAXBLK - 1].unsqueeze(1), [P, EXPERTS, MAXBLK - 1]), ALU.is_gt))
                link(dve.tensor_reduce(cnt[:, 2, :], cmpt[:, :, :], AX.X, ALU.add))
                link(dve.tensor_scalar(cnt[:, 2, :], cnt[:, 2, :], 1.0, None, ALU.add))
                link(dve.tensor_tensor_scan(cnt[:, 3, :], one, cnt[:, 2, :], 0.0, ALU.mult, ALU.add))
                link(tt(cnt[:, 3, :], cnt[:, 3, :], cnt[:, 2, :], ALU.subtract))
                if l == 0:
                    link(tt(blocks0[:, :], cnt[:, 3, EXPERTS - 1:EXPERTS], cnt[:, 2, EXPERTS - 1:EXPERTS], ALU.add))
                else:
                    link(dve.tensor_scalar(cnt[:, 3, :], cnt[:, 3, :], blocks0[:, 0:1], None, ALU.add))
                tt(tab[0:1, 3 * EXPERTS:], cnt[0:1, 3, EXPERTS - 1:EXPERTS], cnt[0:1, 2, EXPERTS - 1:EXPERTS],
                   ALU.add).then_inc(ev("tab"), 1)
                for n in range(3):
                    dve.tensor_copy(tab[0:1, n * EXPERTS:(n + 1) * EXPERTS], cnt[0:1, n + 1, :]).then_inc(ev("tab"), 1)
                for i in range(0, 2 * RT, 2):
                    j = i // 2
                    dve.wait_ge(ev("xs_t"), 2 * RT * l + i + 1)
                    dve.tensor_copy(xsT[:, 0:4, j * P:(j + 1) * P], quad(i % 4)).then_inc(ev("xs_v"), 1)
                dve.wait_ge(ev("tab"), 4 * l + 4)
                if l == 0:
                    for name, count in (("act", 1), ("up_mm", 2), ("h_t", 1), ("down_mm", 1), ("yblk_c", 1)):
                        dve.memset(tick[:, 1:2], 0.0).then_inc(ev(name), count)
                        dve.wait_ge(ev(name), count)
                first = dve.value_load(tab[0:1, 2 * EXPERTS:2 * EXPERTS + 1], min_val=0, max_val=ALLBLK)
                end = dve.value_load(tab[0:1, 3 * EXPERTS:3 * EXPERTS + 1], min_val=EXPERTS, max_val=2 * ALLBLK)

                def gate_block(n):
                    dve.wait_ge(ev("silu"), n + 1)
                    dve.wait_ge(ev("h_t"), n + 1)
                    tt(gact[:, :], gsil[:, :], PS[:, 0, P:2 * P], ALU.mult).then_inc(ev("act"), 1)
                    dve.wait_ge(ev("h_t"), n + 2)
                    dve.wait_ge(ev("down_mm"), n + 1)
                    dve.tensor_copy(hblk[:, :, :], PS[:, 1, 0:P].rearrange("p (i n) -> p i n", i=2)) \
                        .then_inc(ev("hblk_c"), 1)

                def take_block(n):
                    dve.wait_ge(ev("down_mm"), n + 1)
                    dve.wait_ge(ev("y_sent"), n * 32)
                    dve.tensor_copy(yblk[:, :], PS[:, 2, :]).then_inc(ev("yblk_c"), 1)

                gate_block(first)
                with dve.Fori(first + 1, end) as n:
                    gate_block(n)
                    take_block(n)
                take_block(end)
                for t in range(NT):
                    dve.wait_ge(ev("y0_w"), NT * l + t + 1)
                    dve.scalar_tensor_tensor(out=ygat[:, t, :], in0=ygat[:, NT + t, :], scalar=wtok[:, 1, t:t + 1],
                                             in1=ygat[:, t, :], op0=ALU.mult, op1=ALU.add).then_inc(ev("comb_v"), 1)
                for i in range(2 * NT):
                    t, half = i // 2, i % 2
                    dve.wait_ge(ev("comb_mm"), 2 * NT * l + i + 1)
                    for m in range(4):
                        k = 4 * half + m
                        c = 0 if t < ST else 1
                        ins = dve.scalar_tensor_tensor(
                            out=xT[:, k, t * P:t * P + P], in0=quad(4 + i % 4)[:, m, :], scalar=modT[:, l, 40 + k, c:c + 1],
                            in1=xT[:, k, t * P:t * P + P], op0=ALU.mult, op1=ALU.add)
                    ins.then_inc(ev("comb"), 1)

            moe(0)
            dve.wait_ge(ev("comb"), 2 * NT)
            normed(2)

            def gated_u(j):
                dve.wait_ge(ev("gate_mm"), 2 * j + 2)
                dve.wait_ge(ev("sig"), 2 * j + 2)
                for n, c0, c1 in ((0, 0, SEG), (1, SEG, SAMPLE), (1, SAMPLE, T)):
                    to = HALO + c0 + (HALO if c0 == SAMPLE else 0)
                    tt(upad[:, j, to:to + c1 - c0], rs[:, c0:c1], PS[:, n, c0 - n * SEG:c1 - n * SEG],
                       ALU.mult).then_inc(ev("u_w"), 1)

            gated_u(0)
            dve.wait_ge(ev("u_zero"), 1)
            for j in range(KD):
                dve.wait_ge(ev("u_w"), 3 * (j + 1))
                dtaps = TAPS - pe_taps(j)
                for n in range(dtaps):
                    w = pe_taps(j) + n
                    r = w * KD + j
                    wc = vecT[:, 2 + r // P, r % P:r % P + 1]
                    acc = cv[:, j, :] if n % 2 == 0 else cvb
                    src = upad[:, j, w:w + SPAN]
                    if n == 0:
                        dve.tensor_scalar(acc, src, wc, vecT[:, 1, V_DWB + j:V_DWB + j + 1],
                                          ALU.mult, ALU.add).then_inc(ev("conv_v"), 1)
                    elif n == 1:
                        dve.tensor_scalar(acc, src, wc, None, ALU.mult).then_inc(ev("conv_v"), 1)
                    else:
                        dve.wait_ge(ev("conv_v"), conv_ops(j) + n - 1)
                        dve.scalar_tensor_tensor(out=acc, in0=src, scalar=wc, in1=acc,
                                                 op0=ALU.mult, op1=ALU.add).then_inc(ev("conv_v"), 1)
                    if n == dtaps - LATE_TAPS and j + 1 < KD:
                        gated_u(j + 1)
                dve.wait_ge(ev("conv_v"), conv_ops(j) + dtaps)
                tt(cv[:, j, :], cv[:, j, :], cvb, ALU.add).then_inc(ev("conv_v"), 1)
                dve.wait_ge(ev("conv_v"), conv_ops(j) + dtaps + 1)
                dve.wait_ge(ev("tap_mm"), j + 1)
                for n, (c0, c1) in enumerate(((0, HALF), (HALF, SPAN))):
                    tt(cv[:, j, c0:c1], cv[:, j, c0:c1], PS[:, 4 + n, 0:c1 - c0], ALU.add).then_inc(ev("conv_v"), 1)
                dve.wait_ge(ev("conv_v"), conv_ops(j + 1))
            dve.wait_ge(ev("ln_mm"), KD)
            for k in range(KD):
                for n, (c0, c1) in enumerate(((0, HALF), (HALF, SPAN))):
                    dve.scalar_tensor_tensor(out=cv[:, k, c0:c1], in0=PS[:, 6 + n, 0:c1 - c0], scalar=-1.0 / CONV,
                                             in1=cv[:, k, c0:c1], op0=ALU.mult, op1=ALU.add).then_inc(ev("ln_d"), 1)
            dve.wait_ge(ev("ln_root"), 2)
            dve.wait_ge(ev("ln_d"), 2 * KD)
            link(dve.reciprocal(scratch[:, 0:SAMPLE], scratch[:, 0:SAMPLE]))
            link(dve.reciprocal(scratch[:, CTX0:SPAN], scratch[:, CTX0:SPAN]))
            for k in range(KD):
                tt(cvn[:, k, 0:SAMPLE], cv[:, k, 0:SAMPLE], scratch[:, 0:SAMPLE], ALU.mult).then_inc(ev("ln_n"), 1)
                tt(cvn[:, k, SAMPLE:T], cv[:, k, CTX0:SPAN], scratch[:, CTX0:SPAN], ALU.mult).then_inc(ev("ln_n"), 1)
            add_out(1)
            moe(1)
            for i in range(0, 2 * NT, 2):
                t = i // 2
                dve.wait_ge(ev("x_t"), 2 * NT + i + 1)
                dve.tensor_copy(xtok[:, t, 0:512], PS[:, 4 + i % 4, :]).then_inc(ev("xt_v"), 1)

        @block.gpsimd
        def _(pool):
            step = [0]

            def link(ins):
                step[0] += 1
                ins.then_inc(ev("pool_step"), 1)
                pool.wait_ge(ev("pool_step"), step[0])

            def ctx_mod(q):
                l = q // 2
                pool.wait_ge(ev("coef"), q + 1)
                for k in range(KD):
                    pool.wait_ge(ev("hn"), 2 * KD * q + 2 * k + 2)
                    pool.tensor_scalar(hT[:, k, SAMPLE:T], hT[:, k, SAMPLE:T], modA[:, q, k, 1:2],
                                       modT[:, l, 24 * (q % 2) + k, 1:2], ALU.mult, ALU.add).then_inc(ev("h_c"), 1)

            pool.memset(scT[:, :, :], 0.0).then_inc(ev("sc_zero"), 1)

            def late(dst, src):
                pool.dma_start(dst, src).then_inc(ev("late_in"), 16)
            late(dist, f["distances"])
            late(dec[:, :], f["ev_ret_decay"][0].rearrange("d h -> (d h)").partition_broadcast(P))
            late(kvg[:, :], f["ev_kv_a_norm"][0].partition_broadcast(P))
            late(qkg[:, 0, :], f["ev_q_norm"][0].partition_broadcast(P))
            late(qkg[:, 1, :], f["ev_k_norm"][0].partition_broadcast(P))
            link(pool.memset(gcol[:, :], 1.0))
            late(gcol[0:NOPE, 0:1], f["ev_q_norm"][0, 0:NOPE].rearrange("(n a) -> n a", a=1))
            late(gcol[0:NOPE, 1:2], f["ev_k_norm"][0, 0:NOPE].rearrange("(n a) -> n a", a=1))
            late(cache_in[:, 0:KVRANK], f["cache_mla_ckv"][0, 0])
            late(cache_in[:, KVRANK:], f["cache_mla_krope"][0, 0])
            for l in range(2):
                late(rb[:, l, 0:GROUPS], f["moe_b_group"][l].partition_broadcast(P))
                late(rb[:, l, GROUPS:], f["moe_b_expert"][l].partition_broadcast(P))


            ctx_mod(0)
            pool.wait_ge(ev("z_v"), 4 * NT)
            pool.wait_ge(ev("z_a"), 4 * NT)
            pool.dma_start(f["new_krope"][0, 0], z[:, ST, Z_KR:Z_RQ]).then_inc(ev("side_out"), 16)
            pool.wait_ge(ev("upd_c"), NT)
            for d in range(2):
                pool.dma_start(f["new_state"][0, 0, d].rearrange("h k v -> k h v"),
                               upd[d * RK:(d + 1) * RK, ST, :, :]).then_inc(ev("side_out"), 16)
            pool.wait_ge(ev("lat_n"), NT)
            pool.dma_start(f["new_ckv"][0, 0], z[:, ST, QRANK:Z_KR]).then_inc(ev("side_out"), 16)
            pool.wait_ge(ev("qkg_s"), 1)
            for u, (kind, t) in enumerate(UNITS):
                raw = qkraw[:, u % 2, :].rearrange("p (h n) -> p h n", h=HEADS)
                if kind == "k":
                    kr = z[:, t, Z_KR:Z_RQ] if t < NT else cache_in[:, KVRANK:]
                    if u >= 2:
                        pool.wait_ge(ev("hd_t"), u - 1)
                    pool.tensor_copy(raw[:, :, NOPE:QK], bc(kr.unsqueeze(1), [P, HEADS, ROPE])).then_inc(ev("kr_p"), 1)
                pool.wait_ge(ev("qk_r"), u + 1)
                gain = bc(qkg[:, 0 if kind == "q" else 1, NOPE:QK].unsqueeze(1), [P, HEADS, ROPE])
                ins = pool.tensor_tensor(raw[:, :, NOPE:QK], raw[:, :, NOPE:QK], gain, ALU.mult)
                if t < ST:
                    link(ins)
                    x1, x2 = raw[:, :, NOPE:NOPE + 16], raw[:, :, NOPE + 16:QK]
                    cs = bc(cst[:, C_COS + 16 * t:C_COS + 16 * t + 16].unsqueeze(1), [P, HEADS, 16])
                    sn = bc(cst[:, C_SIN + 16 * t:C_SIN + 16 * t + 16].unsqueeze(1), [P, HEADS, 16])
                    r = [ropet[:, n, :].rearrange("p (h n) -> p h n", h=HEADS) for n in range(4)]
                    pool.tensor_tensor(r[0], x1, cs, ALU.mult)
                    pool.tensor_tensor(r[1], x2, sn, ALU.mult)
                    pool.tensor_tensor(r[2], x1, sn, ALU.mult)
                    link(pool.tensor_tensor(r[3], x2, cs, ALU.mult))
                    link(pool.tensor_tensor(x1, r[0], r[1], ALU.subtract))
                    ins = pool.tensor_tensor(x2, r[2], r[3], ALU.add)
                ins.then_inc(ev("qk_n"), 1)
                pool.wait_ge(ev("qk_n"), u + 1)
            pool.wait_ge(ev("hd_t"), len(UNITS))
            for hp in range(4):
                pool.wait_ge(ev("o_c"), 3 + hp)
                pool.tensor_copy(oT[:, 2 * hp, SAMPLE:T], octx[:, hp, :]).then_inc(ev("octx_c"), 1)

            def moe(l):
                q = 2 * l + 1
                ctx_mod(q)
                if l == 0:
                    pool.wait_ge(ev("side_out"), 64)
                pool.wait_ge(ev("pos"), l + 1)
                for t in range(NT):
                    pool.wait_ge(ev("htok_a"), 2 * NT * l + 2 * (t + 1))
                    for c in range(2):
                        pool.indirect_dma_start(
                            rows_in[:, :], bass.IndirectOffsetOnAxis(ap=posu[:, c * NT + t:c * NT + t + 1], axis=0),
                            htok[:, t, :], None).then_inc(ev("rows_sent"), 16)
                pool.wait_ge(ev("rows_sent"), 16 * 2 * NT * (l + 1))
                pool.memset(xsT[:, :, ROWS:XW], 0.0).then_inc(ev("pad"), 1)
                pool.wait_ge(ev("xs_v"), RT * l + RT)
                pool.wait_ge(ev("xs_a"), RT * l + RT)
                pool.wait_ge(ev("pad"), l + 1)
                pool.wait_ge(ev("yblk_c"), 1)
                with pool.Fori(0, EXPERTS) as e:
                    off = pool.value_load(tab[0:1, bass.ds(e, 1)], min_val=0, max_val=ROWS)
                    blocks = pool.value_load(tab[0:1, bass.ds(e + EXPERTS, 1)], min_val=1, max_val=MAXBLK)
                    before = pool.value_load(tab[0:1, bass.ds(e + 2 * EXPERTS, 1)], min_val=0, max_val=2 * ALLBLK)
                    with pool.Fori(0, blocks) as b:
                        row = pool.snap(nc.s_assert_within(
                            off + b * BLK, 0, ROWS,
                            skip_runtime_bounds_check_because="a further block starts inside the expert's rows"))
                        twice = pool.snap((before + b) * 2)
                        for half in range(2):
                            pool.wait_ge(ev("up_mm"), twice + (half + 1))
                            pool.tensor_copy(xblk[:, 4 * half:4 * half + 4, :],
                                             xsT[:, 4 * half:4 * half + 4, bass.ds(row, BLK)]) \
                                .then_inc(ev("xblk_c"), 1)
                pool.wait_ge(ev("results_sent"), l + 1)
                for t in range(NT):
                    for c in range(2):
                        pool.indirect_dma_start(
                            ygat[:, c * NT + t, :], None, rows_out[0:ROWS, :],
                            bass.IndirectOffsetOnAxis(ap=posu[:, c * NT + t:c * NT + t + 1], axis=0)) \
                            .then_inc(ev(f"picked{t}"), 16)

            moe(0)
            pool.wait_ge(ev("comb"), 2 * NT)
            for t in range(NT):
                pool.wait_ge(ev(f"picked{t}"), 32)
            ctx_mod(2)
            pool.memset(upad[:, :, 0:HALO], 0.0)
            pool.memset(upad[:, :, HALO + SAMPLE:HALO + CTX0], 0.0)
            pool.memset(upad[:, :, PADW - HALO:PADW], 0.0).then_inc(ev("u_zero"), 1)
            for j in range(KD):
                if 2 <= j < KD - 1:
                    pool.wait_ge(ev("tap_mm"), j - 1)
                for w in range(pe_taps(j)):
                    r = w * KD + j
                    pool.tensor_scalar(tap_diag(j, w), ident, vecT[:, 2 + r // P, r % P:r % P + 1], None,
                                       ALU.mult).then_inc(ev("tap_d"), 1)
            moe(1)


_INS = ['x_prompt', 'x_sample', 'cache_mla_ckv', 'cache_mla_krope', 'state_retention', 'c', 'c_ctx', 'ada_w', 'ada_b',
        'norm_mix', 'norm_ffn', 'ev_w_in', 'ev_q_a_norm', 'ev_w_q_up', 'ev_kv_a_norm', 'ev_w_kv_up', 'ev_q_norm',
        'ev_k_norm', 'ev_ret_decay', 'ev_ret_gn', 'ev_w_out', 'od_w_in', 'od_dw', 'od_dw_b', 'od_ln_g', 'od_ln_b',
        'od_w_out', 'moe_w_group', 'moe_b_group', 'moe_w_expert', 'moe_b_expert', 'moe_w_up', 'moe_w_down']
_OUTS = [("y_prompt", (1, CONTEXT, D)), ("y_sample", (1, SAMPLE, D)), ("new_ckv", (1, 1, CONTEXT, KVRANK)),
         ("new_krope", (1, 1, CONTEXT, ROPE)), ("new_state", (1, 1, 2, RH, RK, RV))]


def shape_constants():
    import numpy as np
    c = np.zeros((P, C_W), np.float32)
    i = np.arange(P)
    c[:, C_ID:C_ID + P] = np.eye(P)
    c[:, C_ONE:C_ONE + P] = 1.0
    c[:, C_TRI:C_TRI + P] = i[:, None] < i[None, :]
    d = i[None, :] - i[:, None]
    dist = np.concatenate([np.maximum(d, 0), d >= 0, np.maximum(-d, 0), d <= 0], axis=1).astype(np.float32)
    freqs = np.float32(10000.0) ** (-np.arange(8, dtype=np.float32) / np.float32(8))
    tok = np.arange(SAMPLE)
    ang = np.concatenate([(tok // GRID_W)[:, None] * freqs, (tok % GRID_W)[:, None] * freqs], axis=1)
    for off, v in ((C_COS, np.cos(ang)), (C_SIN, np.sin(ang))):
        c[:, off:off + ST * 16] = v.reshape(ST, P, 16).transpose(1, 0, 2).reshape(P, ST * 16)
    c[:, C_POS:C_POS + 4] = np.stack([P - 1 - i, i + 1, i, P - i], axis=1)
    c[:, C_PRI4:C_PRI4 + 4] = np.arange(4, 0, -1)
    c[:, C_PRI8:C_PRI8 + 8] = np.arange(8, 0, -1)
    c[:, C_THR:C_THR + MAXBLK - 1] = BLK * np.arange(1, MAXBLK)
    c[:, C_EPS] = EPS
    return c, dist


def kernel(**inputs):
    import numpy as _np
    import concourse.bacc as _bacc
    from concourse import mybir as _mybir
    from concourse.bass_utils import run_bass_kernel_spmd as _run

    nc = _bacc.Bacc("TRN2", target_bir_lowering=False, num_devices=1)
    arrays, io = {}, {}
    named = {name: _np.ascontiguousarray(inputs[name]) for name in _INS}
    named["consts"], named["distances"] = shape_constants()
    for name, a in named.items():
        arrays[f"in_{name}"] = a
        io[name] = nc.dram_tensor(f"in_{name}", a.shape, _mybir.dt.from_np(a.dtype), kind="ExternalInput").ap()
    for name, shape in _OUTS:
        io[name] = nc.dram_tensor(f"out_{name}", shape, F32, kind="ExternalOutput").ap()
    build(nc, io)
    r = _run(nc, [arrays], core_ids=[0])
    return tuple(r.results[0][f"out_{name}"] for name, _ in _OUTS)
```
